# Optimizing a Trainium2 kernel written in Bass

```python
import jax, jax.numpy as jnp
from jax import lax
import numpy as np
import math

D_MODEL = 1024
BATCH = 1
SEQ = 512
DEPTH = 1

HG_WIDTH = D_MODEL // 2
HG_HEAD_DIM = 128
HG_HEADS = HG_WIDTH // HG_HEAD_DIM
ML_WIDTH = D_MODEL - HG_WIDTH
ML_V_DIM = 128
ML_HEADS = ML_WIDTH // ML_V_DIM
ML_QK_DIM = ML_V_DIM // 2
D_MIX = HG_WIDTH + ML_WIDTH
CONV_WIDTH = 4
D_FF = 2816
CHUNK = 64
EPS = 1e-6
SPLIT_SIZES = (HG_WIDTH, HG_WIDTH, HG_WIDTH, HG_WIDTH,
               ML_HEADS * ML_QK_DIM, ML_HEADS * ML_QK_DIM,
               ML_WIDTH, ML_WIDTH,
               ML_HEADS, ML_HEADS)
D_IN = 4 * HG_WIDTH + 2 * ML_HEADS * ML_QK_DIM + 2 * ML_WIDTH + 2 * ML_HEADS


def rms_norm(x, g):
    xf = x.astype(jnp.float32)
    y = xf * lax.rsqrt(jnp.mean(xf * xf, axis=-1, keepdims=True) + EPS)
    return (y * g.astype(jnp.float32)).astype(x.dtype)

def swiglu_ffn(x, w_in, w_out):
    gate, up = jnp.split(x @ w_in, 2, axis=-1)
    return (jax.nn.silu(gate) * up) @ w_out

def split_cols(x, sizes):
    outs, start = [], 0
    for s in sizes:
        outs.append(x[..., start:start + s])
        start += s
    return outs

def causal_depthwise_conv(x, w, b):
    y = lax.conv_general_dilated(
        x, w[:, None, :].astype(x.dtype), window_strides=(1,),
        padding=[(CONV_WIDTH - 1, 0)], dimension_numbers=("NWC", "WIO", "NWC"),
        feature_group_count=x.shape[-1])
    return y + b.astype(x.dtype)

def to_chunks(x):
    B, T, H, d = x.shape
    return x.reshape(B, T // CHUNK, CHUNK, H, d).transpose(1, 0, 3, 2, 4)

def scalar_to_chunks(x):
    B, T, H = x.shape
    return x.reshape(B, T // CHUNK, CHUNK, H).transpose(1, 0, 3, 2)

def from_chunks(y):
    NC, B, H, L, d = y.shape
    return y.transpose(1, 0, 3, 2, 4).reshape(B, NC * L, H, d)

def hgrn2_chunkwise(q, k, v, log_f):
    B, T, H, dk = q.shape
    dv = v.shape[-1]
    causal = jnp.tril(jnp.ones((CHUNK, CHUNK), dtype=bool))[:, :, None]

    def step(S, inp):
        qc, kc, vc, gc = inp
        G = jnp.cumsum(gc, axis=2)
        o_inter = jnp.einsum("bhtk,bhkv->bhtv", qc * jnp.exp(G), S)
        rel = G[:, :, :, None, :] - G[:, :, None, :, :]
        decay = jnp.exp(jnp.where(causal, rel, -jnp.inf))
        scores = jnp.sum(qc[:, :, :, None, :] * kc[:, :, None, :, :] * decay, axis=-1)
        o = o_inter + jnp.einsum("bhts,bhsv->bhtv", scores, vc)
        G_end = G[:, :, -1:, :]
        S_new = jnp.exp(G_end[:, :, 0, :])[..., None] * S + jnp.einsum(
            "bhsk,bhsv->bhkv", kc * jnp.exp(G_end - G), vc)
        return S_new, o

    S0 = jnp.zeros((B, H, dk, dv), jnp.float32)
    _, o = lax.scan(step, S0, (to_chunks(q), to_chunks(k), to_chunks(v), to_chunks(log_f)))
    return from_chunks(o)

def mlstm_chunkwise(q, k, v, log_i, log_f):
    B, T, H, dqk = q.shape
    dv = v.shape[-1]
    causal = jnp.tril(jnp.ones((CHUNK, CHUNK), dtype=bool))

    def step(carry, inp):
        C, n, m = carry
        qc, kc, vc, ic, fc = inp
        b = jnp.cumsum(fc, axis=-1)
        a = b + m[..., None]
        D = jnp.where(causal, b[..., :, None] - b[..., None, :] + ic[..., None, :], -jnp.inf)
        m_t = jnp.maximum(a, jnp.max(D, axis=-1))
        inter = jnp.exp(a - m_t)
        P = jnp.einsum("bhtd,bhsd->bhts", qc, kc) * jnp.exp(D - m_t[..., None])
        num = inter[..., None] * jnp.einsum("bhtd,bhdv->bhtv", qc, C) + jnp.einsum("bhts,bhsv->bhtv", P, vc)
        den = inter * jnp.einsum("bhtd,bhd->bht", qc, n) + jnp.sum(P, axis=-1)
        h = num / jnp.maximum(jnp.abs(den), jnp.exp(-m_t))[..., None]
        m_new = m_t[..., -1]
        w = jnp.exp(b[..., -1:] - b + ic - m_new[..., None])
        keep = inter[..., -1]
        C_new = keep[..., None, None] * C + jnp.einsum("bhs,bhsd,bhsv->bhdv", w, kc, vc)
        n_new = keep[..., None] * n + jnp.einsum("bhs,bhsd->bhd", w, kc)
        return (C_new, n_new, m_new), h

    init = (jnp.zeros((B, H, dqk, dv), jnp.float32), jnp.zeros((B, H, dqk), jnp.float32),
            jnp.zeros((B, H), jnp.float32))
    _, h = lax.scan(step, init, (to_chunks(q), to_chunks(k), to_chunks(v),
                                 scalar_to_chunks(log_i), scalar_to_chunks(log_f)))
    return from_chunks(h)

def token_mixer(h, w_in, conv_w, conv_b, gate_bias, lb, hg_norm, ml_norm, w_out):
    B, T, _ = h.shape
    f32 = jnp.float32
    hq, hf, hi, hgate, mq, mk, mv, mo, mig, mfg = split_cols(h @ w_in, SPLIT_SIZES)
    hs = (B, T, HG_HEADS, HG_HEAD_DIM)
    lbh = lb.reshape(HG_HEADS, HG_HEAD_DIM)
    forget = lbh + (1.0 - lbh) * jax.nn.sigmoid(hf.astype(f32).reshape(hs))
    hg_o = hgrn2_chunkwise(jax.nn.silu(hq.astype(f32)).reshape(hs), 1.0 - forget,
                           hi.astype(f32).reshape(hs), jnp.log(forget))
    hg_o = rms_norm(hg_o, hg_norm.reshape(HG_HEADS, HG_HEAD_DIM)).reshape(B, T, HG_WIDTH)
    hg_o = hg_o * jax.nn.silu(hgate.astype(f32))
    qk = jax.nn.silu(causal_depthwise_conv(jnp.concatenate([mq, mk], axis=-1), conv_w, conv_b))
    mq, mk = jnp.split(qk.astype(f32), 2, axis=-1)
    qs = (B, T, ML_HEADS, ML_QK_DIM)
    gates = (jnp.concatenate([mig, mfg], axis=-1) + gate_bias).astype(f32)
    log_i = gates[..., :ML_HEADS]
    log_f = jax.nn.log_sigmoid(gates[..., ML_HEADS:])
    ml_o = mlstm_chunkwise(mq.reshape(qs) * (ML_QK_DIM ** -0.5), mk.reshape(qs),
                           mv.astype(f32).reshape(B, T, ML_HEADS, ML_V_DIM), log_i, log_f)
    ml_o = rms_norm(ml_o, ml_norm.reshape(ML_HEADS, ML_V_DIM)).reshape(B, T, ML_WIDTH)
    ml_o = ml_o * jax.nn.sigmoid(mo.astype(f32))
    mix = jnp.concatenate([hg_o, ml_o], axis=-1).astype(h.dtype)
    return mix @ w_out

def first_inputs(seed: int = 0) -> dict:
    key = jax.random.key(seed)
    ks = jax.random.split(key, 16)
    nrm = jax.random.normal
    gate_bias = jnp.concatenate([
        0.1 * nrm(ks[8], (DEPTH, ML_HEADS)),
        jnp.linspace(3.0, 6.0, ML_HEADS)[None, :] + 0.1 * nrm(ks[9], (DEPTH, ML_HEADS))], axis=-1)
    return {
        "x": nrm(ks[0], (BATCH, SEQ, D_MODEL), jnp.float32),
        "norm_pre": 1.0 + 0.05 * nrm(ks[1], (DEPTH, 3, D_MODEL)),
        "norm_post": 1.0 + 0.05 * nrm(ks[2], (DEPTH, 3, D_MODEL)),
        "ffn1_w_in": nrm(ks[3], (DEPTH, D_MODEL, 2 * D_FF)) * D_MODEL ** -0.5,
        "ffn1_w_out": nrm(ks[4], (DEPTH, D_FF, D_MODEL)) * D_FF ** -0.5,
        "w_mix_in": nrm(ks[5], (DEPTH, D_MODEL, D_IN)) * D_MODEL ** -0.5,
        "conv_w": nrm(ks[6], (DEPTH, CONV_WIDTH, 2 * ML_HEADS * ML_QK_DIM)) * CONV_WIDTH ** -0.5,
        "conv_b": 0.02 * nrm(ks[7], (DEPTH, 2 * ML_HEADS * ML_QK_DIM)),
        "mlstm_gate_bias": gate_bias,
        "hgrn_lb_logits": 0.5 * nrm(ks[10], (DEPTH + 1, HG_WIDTH)),
        "hgrn_norm": 1.0 + 0.05 * nrm(ks[11], (DEPTH, HG_WIDTH)),
        "mlstm_norm": 1.0 + 0.05 * nrm(ks[12], (DEPTH, ML_WIDTH)),
        "w_mix_out": nrm(ks[13], (DEPTH, D_MIX, D_MODEL)) * D_MIX ** -0.5,
        "ffn2_w_in": nrm(ks[14], (DEPTH, D_MODEL, 2 * D_FF)) * D_MODEL ** -0.5,
        "ffn2_w_out": nrm(ks[15], (DEPTH, D_FF, D_MODEL)) * D_FF ** -0.5,
    }

def first_block(x, norm_pre, norm_post, ffn1_w_in, ffn1_w_out, w_mix_in, conv_w, conv_b,
              mlstm_gate_bias, hgrn_lb_logits, hgrn_norm, mlstm_norm, w_mix_out,
              ffn2_w_in, ffn2_w_out):
    lower_bounds = jnp.cumsum(jax.nn.softmax(hgrn_lb_logits.astype(jnp.float32), axis=0), axis=0)
    for l in range(DEPTH):
        x = x + 0.5 * rms_norm(swiglu_ffn(rms_norm(x, norm_pre[l, 0]), ffn1_w_in[l], ffn1_w_out[l]),
                               norm_post[l, 0])
        mixed = token_mixer(rms_norm(x, norm_pre[l, 1]), w_mix_in[l], conv_w[l], conv_b[l],
                            mlstm_gate_bias[l], lower_bounds[l], hgrn_norm[l], mlstm_norm[l],
                            w_mix_out[l])
        x = x + rms_norm(mixed, norm_post[l, 1])
        x = x + 0.5 * rms_norm(swiglu_ffn(rms_norm(x, norm_pre[l, 2]), ffn2_w_in[l], ffn2_w_out[l]),
                               norm_post[l, 2])
    return x


PLE_DIM = 256
FFN_RES_WEIGHT = 0.5
NORM_EPS = 1e-6
Q_BLOCK = 128

MLA_HEADS = 8
MLA_NOPE = 64
MLA_ROPE = 32
MLA_QK = MLA_NOPE + MLA_ROPE
MLA_V = 64
Q_LORA = 384
KV_LORA = 256
ROPE_BASE = 10000.0

SB_HEADS = 8
SB_HEAD_DIM = 64
SB_WIDTH = SB_HEADS * SB_HEAD_DIM
MLA_WIDTH = MLA_HEADS * MLA_V

COL_CQ = Q_LORA
COL_CKV = KV_LORA
COL_KROPE = MLA_ROPE
COL_SB = 3 * SB_WIDTH
COL_GATES = 2 * D_MODEL
IN_COLS = COL_CQ + COL_CKV + COL_KROPE + COL_SB + COL_GATES
SPLITS = list(np.cumsum([COL_CQ, COL_CKV, COL_KROPE, COL_SB])[:])


def rms_norm_2(x, g):
    xf = x.astype(jnp.float32)
    r = lax.rsqrt(jnp.mean(xf * xf, axis=-1, keepdims=True) + NORM_EPS)
    return (xf * r).astype(x.dtype) * g

def apply_rope(x, positions):
    r = x.shape[-1]
    inv_freq = ROPE_BASE ** (-jnp.arange(0, r, 2, dtype=jnp.float32) / r)
    ang = positions.astype(jnp.float32)[..., None] * inv_freq
    cos = jnp.cos(ang)[:, :, None, :].astype(x.dtype)
    sin = jnp.sin(ang)[:, :, None, :].astype(x.dtype)
    x1, x2 = x[..., : r // 2], x[..., r // 2:]
    return jnp.concatenate([x1 * cos - x2 * sin, x2 * cos + x1 * sin], axis=-1)

def swiglu(u, w_in, w_out):
    a, b = jnp.split(u @ w_in, 2, axis=-1)
    return (jax.nn.silu(a) * b) @ w_out

def causal_softmax_attention(q, k, v):
    s_len = q.shape[2]
    scale = 1.0 / math.sqrt(q.shape[-1])
    outs = []
    for i in range(s_len // Q_BLOCK):
        k_len = (i + 1) * Q_BLOCK
        qb = q[:, :, i * Q_BLOCK:(i + 1) * Q_BLOCK]
        kb, vb = k[:, :, :k_len], v[:, :, :k_len]
        sc = jnp.einsum('bhqd,bhkd->bhqk', qb, kb).astype(jnp.float32) * scale
        q_pos = i * Q_BLOCK + jnp.arange(Q_BLOCK)
        mask = jnp.arange(k_len)[None, :] <= q_pos[:, None]
        w = jax.nn.softmax(jnp.where(mask, sc, -jnp.inf), axis=-1)
        outs.append(jnp.einsum('bhqk,bhkd->bhqd', w.astype(vb.dtype), vb))
    return jnp.concatenate(outs, axis=2)

def stick_breaking_attention(q, k, v):
    s_len = q.shape[2]
    scale = 1.0 / math.sqrt(q.shape[-1])
    outs = []
    for i in range(s_len // Q_BLOCK):
        k_len = (i + 1) * Q_BLOCK
        qb = q[:, :, i * Q_BLOCK:(i + 1) * Q_BLOCK]
        kb, vb = k[:, :, :k_len], v[:, :, :k_len]
        z = jnp.einsum('bhqd,bhkd->bhqk', qb, kb).astype(jnp.float32) * scale
        q_pos = i * Q_BLOCK + jnp.arange(Q_BLOCK)
        mask = jnp.arange(k_len)[None, :] < q_pos[:, None]
        log_1m = jnp.where(mask, jax.nn.log_sigmoid(-z), 0.0)
        suffix = lax.cumsum(log_1m, axis=3, reverse=True) - log_1m
        a = jnp.where(mask, jnp.exp(jax.nn.log_sigmoid(z) + suffix), 0.0)
        outs.append(jnp.einsum('bhqk,bhkd->bhqd', a.astype(vb.dtype), vb))
    return jnp.concatenate(outs, axis=2)

def second_inputs(seed: int = 0) -> dict:
    key = jax.random.key(seed)
    ks = iter(jax.random.split(key, 32))
    f32 = jnp.float32

    def w(shape, fan_in):
        return jax.random.normal(next(ks), (DEPTH,) + shape, f32) * fan_in ** -0.5

    def gain(n):
        return 1.0 + 0.02 * jax.random.normal(next(ks), (DEPTH, n), f32)

    x = jax.random.normal(next(ks), (BATCH, SEQ, D_MODEL), f32)
    p = jax.random.normal(next(ks), (DEPTH, BATCH, SEQ, PLE_DIM), f32)
    offset = jax.random.randint(next(ks), (BATCH, 1), 0, 1024, dtype=jnp.int32)
    positions = offset + jnp.arange(SEQ, dtype=jnp.int32)[None, :]
    return {
        "x": x,
        "p": p,
        "positions": positions,
        "ffn1_norm": gain(D_MODEL),
        "ffn1_w_in": w((D_MODEL, 2 * D_FF), D_MODEL),
        "ffn1_w_out": w((D_FF, D_MODEL), D_FF),
        "mix_norm": gain(D_MODEL),
        "w_in": w((D_MODEL, IN_COLS), D_MODEL),
        "q_latent_norm": gain(Q_LORA),
        "w_q_up": w((Q_LORA, MLA_HEADS * MLA_QK), Q_LORA),
        "kv_latent_norm": gain(KV_LORA),
        "w_kv_up": w((KV_LORA, MLA_HEADS * (MLA_NOPE + MLA_V)), KV_LORA),
        "q_head_norm": gain(MLA_QK),
        "k_head_norm": gain(MLA_QK),
        "w_branch_mla": w((MLA_WIDTH, D_MODEL), MLA_WIDTH),
        "w_branch_sb": w((SB_WIDTH, D_MODEL), SB_WIDTH),
        "w_out": w((D_MODEL, D_MODEL), D_MODEL),
        "ffn2_norm": gain(D_MODEL),
        "ffn2_w_in": w((D_MODEL, 2 * D_FF), D_MODEL),
        "ffn2_w_out": w((D_FF, D_MODEL), D_FF),
        "ple_norm": gain(D_MODEL),
        "w_ple_gate": w((D_MODEL, D_MODEL), D_MODEL),
        "w_ple_proj": w((PLE_DIM, D_MODEL), PLE_DIM),
    }

def second_block(x, p, positions, ffn1_norm, ffn1_w_in, ffn1_w_out, mix_norm, w_in,
              q_latent_norm, w_q_up, kv_latent_norm, w_kv_up, q_head_norm, k_head_norm,
              w_branch_mla, w_branch_sb, w_out, ffn2_norm, ffn2_w_in, ffn2_w_out,
              ple_norm, w_ple_gate, w_ple_proj):
    b, s, _ = x.shape
    h = x
    for i in range(DEPTH):
        h = h + FFN_RES_WEIGHT * swiglu(rms_norm_2(h, ffn1_norm[i]), ffn1_w_in[i], ffn1_w_out[i])

        u = rms_norm_2(h, mix_norm[i])
        proj = u @ w_in[i]
        c_q, c_kv, k_rope, sb_qkv, gates = jnp.split(proj, SPLITS, axis=-1)

        q = (rms_norm_2(c_q, q_latent_norm[i]) @ w_q_up[i]).reshape(b, s, MLA_HEADS, MLA_QK)
        kv = (rms_norm_2(c_kv, kv_latent_norm[i]) @ w_kv_up[i]).reshape(b, s, MLA_HEADS, MLA_NOPE + MLA_V)
        k_nope, v_mla = kv[..., :MLA_NOPE], kv[..., MLA_NOPE:]
        k_r = jnp.broadcast_to(k_rope[:, :, None, :], (b, s, MLA_HEADS, MLA_ROPE))
        k = jnp.concatenate([k_nope, k_r], axis=-1)
        q = rms_norm_2(q, q_head_norm[i])
        k = rms_norm_2(k, k_head_norm[i])
        q = jnp.concatenate([q[..., :MLA_NOPE], apply_rope(q[..., MLA_NOPE:], positions)], axis=-1)
        k = jnp.concatenate([k[..., :MLA_NOPE], apply_rope(k[..., MLA_NOPE:], positions)], axis=-1)
        o_mla = causal_softmax_attention(q.transpose(0, 2, 1, 3), k.transpose(0, 2, 1, 3),
                                         v_mla.transpose(0, 2, 1, 3))
        o_mla = o_mla.transpose(0, 2, 1, 3).reshape(b, s, MLA_WIDTH)

        sq, sk, sv = [t.reshape(b, s, SB_HEADS, SB_HEAD_DIM).transpose(0, 2, 1, 3)
                      for t in jnp.split(sb_qkv, 3, axis=-1)]
        o_sb = stick_breaking_attention(sq, sk, sv)
        o_sb = o_sb.transpose(0, 2, 1, 3).reshape(b, s, SB_WIDTH)

        g_mla, g_sb = jnp.split(jax.nn.sigmoid(gates), 2, axis=-1)
        merged = g_mla * (o_mla @ w_branch_mla[i]) + g_sb * (o_sb @ w_branch_sb[i])
        h = h + merged @ w_out[i]

        h = h + FFN_RES_WEIGHT * swiglu(rms_norm_2(h, ffn2_norm[i]), ffn2_w_in[i], ffn2_w_out[i])

        ple_gate = jax.nn.sigmoid(rms_norm_2(h, ple_norm[i]) @ w_ple_gate[i])
        h = h + ple_gate * (p[i] @ w_ple_proj[i])
    return h


def setup_inputs(seed=0):
    out = dict(first_inputs(seed))
    for name, value in second_inputs(seed + 1).items():
        if name != "x":
            out[name + "_2"] = value
    return out


def reference(
    x, norm_pre, norm_post, ffn1_w_in, ffn1_w_out, w_mix_in, conv_w, conv_b, mlstm_gate_bias,
    hgrn_lb_logits, hgrn_norm, mlstm_norm, w_mix_out, ffn2_w_in, ffn2_w_out, p_2, positions_2,
    ffn1_norm_2, ffn1_w_in_2, ffn1_w_out_2, mix_norm_2, w_in_2, q_latent_norm_2, w_q_up_2,
    kv_latent_norm_2, w_kv_up_2, q_head_norm_2, k_head_norm_2, w_branch_mla_2, w_branch_sb_2,
    w_out_2, ffn2_norm_2, ffn2_w_in_2, ffn2_w_out_2, ple_norm_2, w_ple_gate_2, w_ple_proj_2,
):
    x = first_block(
        x, norm_pre, norm_post, ffn1_w_in, ffn1_w_out, w_mix_in, conv_w, conv_b,
        mlstm_gate_bias, hgrn_lb_logits, hgrn_norm, mlstm_norm, w_mix_out, ffn2_w_in,
        ffn2_w_out,
    )
    return second_block(
        x, p_2, positions_2, ffn1_norm_2, ffn1_w_in_2, ffn1_w_out_2, mix_norm_2, w_in_2,
        q_latent_norm_2, w_q_up_2, kv_latent_norm_2, w_kv_up_2, q_head_norm_2, k_head_norm_2,
        w_branch_mla_2, w_branch_sb_2, w_out_2, ffn2_norm_2, ffn2_w_in_2, ffn2_w_out_2,
        ple_norm_2, w_ple_gate_2, w_ple_proj_2,
    )


_drawn_inputs = setup_inputs


def setup_inputs(seed=0):
    import zlib

    import numpy as np

    out = dict(_drawn_inputs(seed))
    spreads = {}
    factors = {'conv_b': 4.801,
     'ffn1_norm_2': 8.0,
     'mix_norm_2': 8.0,
     'q_latent_norm_2': 8.0,
     'kv_latent_norm_2': 8.0,
     'q_head_norm_2': 8.0,
     'k_head_norm_2': 8.0,
     'ffn2_norm_2': 23.198,
     'ple_norm_2': 64.0,
     'p_2': 2.772,
     'w_ple_gate_2': 4.148,
     'w_ple_proj_2': 2.77}
    for name, (base, spread) in spreads.items():
        noise = np.random.default_rng([zlib.crc32(name.encode()), seed]).standard_normal(out[name].shape)
        drawn = base * np.exp(spread * noise) if base else spread * noise
        out[name] = __import__('jax').numpy.asarray(drawn.astype(out[name].dtype))
    for name, factor in factors.items():
        out[name] = (out[name] * factor).astype(out[name].dtype)
    return out
```

```python
from contextlib import ExitStack

import numpy as np
import concourse.bass as bass
from concourse import mybir
from concourse.alu_op_type import AluOpType as ALU

F32 = mybir.dt.float32
F32R = mybir.dt.float32r
I32 = mybir.dt.int32
U32 = mybir.dt.uint32
ACT = mybir.ActivationFunctionType
AX = mybir.AxisListType

P = 128
T = 512
NT = T // P
D = 1024
KD = D // P
DFF = 2816
KF = DFF // P
EPS = 1e-6

HEADS = 4
DK = 128
CH = 64
NC = T // CH
ML_QK = 64
CONV = 4

AH = 8
NOPE, ROPE, QK, HV = 64, 32, 96, 64
KCQ, KCKV = 3, 2

HALF = KF // 2
SLOT = HALF * P
RAW, PAIR = 4, 2
NEVER = -1e30

C_ID, C_ONE, C_LE, C_LT, C_NSUF, C_NONE, C_NGT, C_NGE, C_LEVEL = (i * P for i in range(9))
LEVELS = (1, 2, 4, 8, 16, 32)
C_RESET = C_LEVEL + len(LEVELS) * P
C_SEL = C_RESET + T
C_ROT = C_SEL + HEADS * P
C_FREQ = C_ROT + ROPE
N_CONST = C_FREQ + 1

PARAMS = {}
_n = 0
for _name, _w in (("norm_pre", 3 * KD), ("norm_post", 3 * KD), ("conv_w", CONV * HEADS), ("conv_b", HEADS),
                  ("lb", 2 * HEADS), ("hgrn_norm", HEADS), ("mlstm_norm", HEADS), ("ffn1_norm", KD),
                  ("mix_norm", KD), ("q_latent", KCQ), ("kv_latent", KCKV), ("ffn2_norm", KD), ("ple_norm", KD)):
    PARAMS[_name] = _n
    _n += _w
N_PARAM = _n


CAUSAL = [(i, i * P, P, i * P) for i in range(NT)] + [(0, P, 3 * P, T), (2, 3 * P, P, T + 3 * P), (1, 2 * P, 2 * P, 2 * T)]
N_CAUSAL = 2 * T + 2 * P


def causal_column(i, j):
    if i == j:
        return i * P
    return next(c + j * P - t0 for (n, t0, w, c) in CAUSAL[NT:] if n == i)


ROWS = [(3, 0), (2, T), (0, T + 3 * P), (1, 2 * T)]
GATE_AT = 18
LO_AT = 12


class Done:

    def __init__(self, line, count, looped):
        self.line, self.count, self.looped = line, count, looped


class Line:

    def __init__(self, nc, name, credit=0):
        self.sem = nc.alloc_semaphore(name)
        self.count = credit
        self.per = None
        self.turn = None

    def mark(self, ins):
        ins.then_inc(self.sem, 1)
        self.count += 1
        return Done(self, self.count, self.per is not None)

    def ahead(self, k):
        return Done(self, self.start + k, True)


class Program:

    def __init__(self, nc):
        self.nc = nc
        self.pe, self.act, self.dve, self.pool = nc.tensor, nc.scalar, nc.vector, nc.gpsimd
        credit = 64
        self.PE, self.ACT, self.DVE = (Line(nc, n, credit) for n in ("pe_done", "act_done", "dve_done"))
        for e, line in ((self.pe, self.PE), (self.act, self.ACT), (self.dve, self.DVE)):
            e.sem_inc(line.sem, credit)
        self.lines = [self.PE, self.ACT, self.DVE]
        self.known = {}

    def wait(self, eng, *dones, back=0):
        most = {}
        queue = list(dones)
        while queue:
            d = queue.pop()
            if isinstance(d, (list, tuple)):
                queue += d
            elif d is not None:
                most[(d.line, d.looped)] = max(most.get((d.line, d.looped), 0), d.count)
        for (line, looped), count in most.items():
            if looped and line.per is not None:
                assert count - back * line.per >= 0
                eng.wait_ge(line.sem, line.turn * line.per + (count - back * line.per))
            else:
                key = (id(eng), line)
                if self.known.get(key, -1) >= count:
                    continue
                eng.wait_ge(line.sem, count)
                if line.per is None:
                    self.known[key] = count

    def loop(self, times, **per):
        return Loop(self, times, per)


class Loop:

    def __init__(self, prog, times, per):
        self.prog, self.times = prog, times
        self.per = {named_line(prog, k): v for k, v in per.items()}

    def __enter__(self):
        self.fori = self.prog.nc.Fori(0, self.times)
        i = self.fori.__enter__()
        for line in self.prog.lines:
            line.start, line.per, line.turn = line.count, self.per.get(line, 0), i
        return i

    def __exit__(self, *exc):
        self.fori.__exit__(*exc)
        for line in self.prog.lines:
            assert exc[0] or line.count - line.start == line.per, (line.count - line.start, line.per)
            line.count = line.start + self.times * line.per
            line.per = line.turn = None


def named_line(prog, name):
    return {"pe": prog.PE, "act": prog.ACT, "dve": prog.DVE, "split": prog.W.split, "used": prog.W.used}[name]


class Weights:

    def __init__(self, prog, at):
        nc = self.nc = prog.nc
        self.p = prog
        self.raw, self.hi, self.lo = [], [], []
        for s in range(RAW):
            self.raw.append(nc.alloc_sbuf_tensor_at(f"w_raw{s}", [P, SLOT], F32, offset=at))
            at += SLOT * 4
        for s in range(PAIR):
            self.hi.append(nc.alloc_sbuf_tensor_at(f"w_hi{s}", [P, SLOT], F32R, offset=at))
            self.lo.append(nc.alloc_sbuf_tensor_at(f"w_lo{s}", [P, SLOT], F32R, offset=at + SLOT * 4))
            at += SLOT * 8
        self.end = at
        self.passed = nc.alloc_semaphore("w_passed")
        self.landed = [nc.alloc_semaphore(f"w_landed{s}") for s in range(RAW)]
        self.n = RAW
        self.split = Line(nc, "w_split", 2 * RAW)
        self.used = Line(nc, "w_used", RAW)
        nc.gpsimd.sem_inc(self.split.sem, 2 * RAW)
        nc.tensor.sem_inc(self.used.sem, RAW)
        prog.lines += [self.split, self.used]
        prog.W = self

    def chunk(self, src, rows=P):
        p, nc, cols = self.p, self.nc, src.shape[-1]
        n = self.n
        r, s = n % RAW, n % PAIR
        looped = self.split.per is not None
        p.wait(nc.sync, Done(self.split, 2 * (n - RAW + 1), looped))
        nc.sync.dma_start(self.raw[r][0:rows, 0:cols], src).then_inc(self.landed[r], 16)
        landed = 16 * (n // RAW)
        if looped:
            nc.gpsimd.wait_ge(self.landed[r], self.split.turn * (16 * self.split.per // (2 * RAW)) + landed)
        else:
            nc.gpsimd.wait_ge(self.landed[r], landed)
        p.wait(nc.gpsimd, Done(self.used, n - PAIR + 1, looped))
        if looped:
            nc.gpsimd.sem_inc(self.passed, 1)
        raw, hi, lo = self.raw[r][0:rows, 0:cols], self.hi[s][0:rows, 0:cols], self.lo[s][0:rows, 0:cols]
        rounded = self.split.mark(nc.gpsimd.tensor_scalar(hi, raw, 1.0, 1.0, ALU.mult, ALU.mult))
        p.wait(nc.gpsimd, rounded)
        rest = self.split.mark(nc.gpsimd.tensor_tensor(lo, raw, hi.bitcast(F32), ALU.subtract))
        self.n += 1
        return self.hi[s], self.lo[s], rest

    def begin(self):
        self.first = self.n

    def finish(self, times):
        body = self.n - self.first
        assert body % RAW == 0
        self.n = self.first + body * times
        assert self.split.count == 2 * self.n and self.used.count == self.n


class Build:
    def __init__(self, nc, a, out, upto=99):
        self.nc, self.a = nc, a
        self.out = out
        p = self.p = Program(nc)
        at = nc.sbuf_base
        at = (at + 63) // 64 * 64
        self.map_start = at

        def place(name, cols, dt, offset):
            return nc.alloc_sbuf_tensor_at(name, [P, cols], dt, offset=offset)

        self.const = place("const", N_CONST, F32, at); at += N_CONST * 4 + (-N_CONST * 4) % 64
        self.param = place("param", N_PARAM, F32, at); at += N_PARAM * 4 + (-N_PARAM * 4) % 64
        self.misc = place("misc", 256, F32, at); at += 1024
        self.x = place("x", KD * T, F32, at); at += KD * T * 4
        self.w = Weights(p, at)
        at = self.w.end
        self.sc = []
        for i in range(7):
            self.sc.append(place(f"scratch{i}", T, F32, at)); at += T * 4
        self.u_at = at
        self.uhi = place("u_hi", KD * T, F32R, at)
        self.ulo = place("u_lo", KD * T, F32R, at + KD * T * 4)
        self.y = place("y", KD * T, F32, at)
        self.uf = place("u_f32", 2 * KD * T, F32, at)
        at += 2 * KD * T * 4
        self.big_at = at
        self.hhi = place("hidden_hi", KF * T, F32R, at)
        self.hlo = place("hidden_lo", KF * T, F32R, at + KF * T * 4)
        self.big = place("work", 2 * KF * T, F32, at)
        at += 2 * KF * T * 4
        self.map_end = at
        self.psum = nc.alloc_psum_tensor("psum", [P, 8 * T], F32)
        self.ps = [self.psum[:, b * T:(b + 1) * T] for b in range(8)]
        self.bank = [None] * 8
        self.spread_used = [None, None]
        self.y_tiles = self.y
        self.vt = [self.tile(self.big, n) for n in (4, 5)]

    def store(self):
        p, nc = self.p, self.nc
        self.settle(nc.sync)
        stored = nc.alloc_semaphore("stored")
        nc.sync.dma_start(self.out, self.x[:, :]).then_inc(stored, 16)
        nc.sync.wait_ge(stored, 16)

    def cst(self, c, n=P, rows=slice(0, P)):
        return self.const[rows, c:c + n]

    def par(self, name, k, rows=slice(0, P)):
        c = PARAMS[name] + k
        return self.param[rows, c:c + 1]


    def load(self):
        nc, p, a = self.nc, self.p, self.a
        self.loaded = nc.alloc_semaphore("loaded")
        n = 0
        for dst, src in ((self.const[:, :], a["const"]), (self.param[:, :], a["param"]), (self.x[:, :], a["x"])):
            nc.scalar.dma_start(dst, src).then_inc(self.loaded, 16)
            n += 16
        for e in (nc.tensor, nc.vector, nc.scalar):
            e.wait_ge(self.loaded, n)

    def mm3(self, out, hi, lo, cols, xhi, xlo, first, last):
        pe = self.nc.tensor
        pe.matmul(out, hi[:, cols], xhi, start=first, stop=False)
        pe.matmul(out, lo[:, cols], xhi, start=False, stop=False)
        return pe.matmul(out, hi[:, cols], xlo, start=False, stop=last)

    def token_sums(self, sq, ready, out, rows=P, first_wait=None):
        p, pe = self.p, self.nc.tensor
        p.wait(pe, ready, first_wait)
        for i in range(NT):
            m = pe.matmul(out(i), sq[0:rows, i * P:(i + 1) * P], self.cst(C_ONE, 1, slice(0, rows)), start=True, stop=True)
        return p.PE.mark(m)

    def rsqrt(self, src, dst, ready, n, factor=1.0):
        p, nc = self.p, self.nc
        f = 1.0 / (factor * factor)
        p.wait(nc.vector, ready)
        d = p.DVE.mark(nc.vector.tensor_scalar(dst, src, f / n, f * EPS, ALU.mult, ALU.add))
        p.wait(nc.scalar, d)
        d = p.ACT.mark(nc.scalar.activation(dst, dst, ACT.Sqrt))
        p.wait(nc.vector, d)
        return p.DVE.mark(nc.vector.reciprocal(dst, dst))

    def spread(self, cols, ready, diag, diag_free, bank, rows=P):
        p, nc = self.p, self.nc
        p.wait(nc.vector, ready, diag_free)
        d3 = diag[:, :].rearrange("p (i t) -> p i t", i=NT)
        ident = self.cst(C_ID).unsqueeze(1).broadcast_to([P, NT, P])
        d = p.DVE.mark(nc.vector.tensor_tensor(d3, ident, cols.unsqueeze(2).broadcast_to([P, NT, P]), ALU.mult))
        p.wait(nc.tensor, d, self.bank[bank])
        m = nc.tensor.matmul(self.ps[bank][0:rows, :], self.cst(C_ONE, rows), diag[:, :], start=True, stop=True)
        self.bank[bank] = p.PE.mark(m)
        return self.bank[bank]

    def tile(self, t, k):
        return t[:, k * T:(k + 1) * T]

    def stream_norm(self, gain):
        p, nc = self.p, self.nc
        self.settle(nc.vector)
        s, r = self.misc[:, 0:NT], self.misc[:, NT:2 * NT]
        if self.groups == 1:
            s, d = self.ps[4][:, 0:NT], self.sums
        else:
            view = self.ps[4][:, 0:KD * NT].rearrange("p (k i) -> p i k", i=NT)
            d = p.DVE.mark(nc.vector.tensor_reduce(s, view, AX.X, ALU.add))
        d = self.rsqrt(s, r, d, D)
        self.bank[4] = d
        rb = self.spread(r, d, self.sc[0], None, 5)
        p.wait(nc.vector, rb)
        done = []
        tmp_free = [None, None, None]
        for k in range(KD):
            t = self.sc[1 + k % 3]
            p.wait(nc.vector, tmp_free[k % 3])
            d = p.DVE.mark(nc.vector.scalar_tensor_tensor(out=t[:, :], in0=self.tile(self.x, k), scalar=gain(k),
                                                          in1=self.ps[5], op0=ALU.mult, op1=ALU.mult))
            p.wait(nc.scalar, d)
            h = p.ACT.mark(nc.scalar.copy(self.tile(self.uhi, k), t[:, :]))
            p.wait(nc.vector, h, d)
            l = p.DVE.mark(nc.vector.tensor_tensor(self.tile(self.ulo, k), t[:, :],
                                                   self.tile(self.uhi, k).bitcast(F32), ALU.subtract))
            tmp_free[k % 3] = l
            done.append([h, l])
        self.bank[5] = d
        self.u_ready = done
        return done

    def square_sums(self, k, ready, src, sq, sq_free, wait_bank=None):
        p, nc = self.p, self.nc
        p.wait(nc.scalar, ready, sq_free)
        d = p.ACT.mark(nc.scalar.activation(sq[:, :], src, ACT.Square))
        return self.token_sums(sq, [d], lambda i: self.ps[4][:, k * NT + i:k * NT + i + 1], first_wait=wait_bank)

    def first_sums(self):
        s = [None, None]
        for k in range(KD):
            s[k % 2] = self.square_sums(k, None, self.tile(self.x, k), self.sc[k % 2], s[k % 2])
        self.sums, self.groups = s[(KD - 1) % 2], KD


    def ffn(self, w_in, w_out, gain, post):
        p, nc = self.p, self.nc
        pe, act, dve = nc.tensor, nc.scalar, nc.vector
        u = self.stream_norm(gain)
        ps, W = self.ps, self.w
        p.wait(pe, self.bank[0:4], *u)
        sg, hm, acc, sq = self.sc[1:3], self.sc[3:5], self.sc[5], self.sc[6]
        self.settle(dve, act)
        zeroed = p.DVE.mark(dve.memset(acc[:, :], 0.0))
        W.begin()
        with p.loop(KF // 2, act=4, dve=4, split=8, used=4) as i:
            for j in range(2):
                sg_done, hi_done = p.ACT.ahead(2 * j + 1), p.ACT.ahead(2 * j + 2)
                hm_done, lo_done = p.DVE.ahead(2 * j + 1), p.DVE.ahead(2 * j + 2)
                for half, taken in ((0, sg_done), (1, hm_done)):
                    b = 2 * j + half
                    hi, lo, ready = W.chunk(w_in[i * 4 + b])
                    p.wait(pe, ready)
                    p.wait(pe, taken, back=1)
                    for k in range(KD):
                        m = self.mm3(ps[b], hi, lo, slice(k * P, (k + 1) * P), self.tile(self.uhi, k),
                                     self.tile(self.ulo, k), k == 0, k == KD - 1)
                    product = W.used.mark(m)
                    if half == 0:
                        p.wait(act, product)
                        p.wait(act, hm_done, back=1)
                        p.ACT.mark(act.activation(sg[j][:, :], ps[b], ACT.Silu))
                p.wait(dve, product, sg_done)
                p.wait(dve, hi_done, lo_done, back=1)
                p.DVE.mark(dve.tensor_tensor(hm[j][:, :], sg[j][:, :], ps[b], ALU.mult))
                at = bass.ds((i * 2 + j) * T, T)
                p.wait(act, hm_done)
                p.ACT.mark(act.copy(self.hhi[:, at], hm[j][:, :]))
                p.wait(dve, hi_done)
                p.DVE.mark(dve.tensor_tensor(self.hlo[:, at], hm[j][:, :], self.hhi[:, at].bitcast(F32), ALU.subtract))
        W.finish(KF // 2)
        self.into_stream(w_out, KD // 2, 2, 2, HALF, self.hhi, self.hlo, 0.5, post)

    def into_stream(self, w, turns, n_tiles, n_chunks, lhs, xhi, xlo, scale, post, tiles=None):
        p, nc = self.p, self.nc
        pe, act, dve = nc.tensor, nc.scalar, nc.vector
        ps, W = self.ps, self.w
        acc, sq = self.sc[5], self.sc[6]
        self.settle(pe, act, dve)
        zeroed = p.DVE.mark(dve.memset(acc[:, :], 0.0))
        p.wait(dve, zeroed)
        W.begin()
        per = n_tiles * n_chunks
        with p.loop(turns, act=n_tiles, dve=2 * n_tiles, split=2 * per, used=per) as i:
            for j in range(n_tiles):
                out_done, acc_done = p.DVE.ahead(2 * j + 1), p.DVE.ahead(2 * j + 2)
                for part in range(n_chunks):
                    hi, lo, ready = W.chunk(w[i * per + (n_chunks * j + part)])
                    p.wait(pe, ready)
                    if part == 0:
                        p.wait(pe, out_done, back=1)
                    for k in range(lhs):
                        kk = part * lhs + k
                        m = self.mm3(ps[j], hi, lo, slice(k * P, (k + 1) * P), self.tile(xhi, kk), self.tile(xlo, kk),
                                     kk == 0, kk == n_chunks * lhs - 1)
                    product = W.used.mark(m)
                at = bass.ds((i * n_tiles + j) * T, T)
                p.wait(dve, product)
                if post:
                    to = self.y_tiles[:, at]
                    p.DVE.mark(dve.tensor_copy(to, ps[j]))
                else:
                    to = self.x[:, at]
                    p.DVE.mark(dve.scalar_tensor_tensor(out=to, in0=ps[j], scalar=scale, in1=to, op0=ALU.mult, op1=ALU.add))
                before = (p.DVE.ahead(2 * n_tiles), 1) if j == 0 else (p.DVE.ahead(2 * j), 0)
                p.wait(act, before[0], back=before[1])
                p.wait(act, out_done)
                squared = p.ACT.mark(act.activation(sq[:, :], to, ACT.Square))
                p.wait(dve, before[0], back=before[1])
                p.wait(dve, squared)
                p.DVE.mark(dve.tensor_tensor(acc[:, :], acc[:, :], sq[:, :], ALU.add))
        W.finish(turns)
        done = [Done(p.ACT, p.ACT.count, False), Done(p.DVE, p.DVE.count, False)]
        self.bank[0:4] = [done] * 4
        self.sums = self.token_sums(acc, done, self.col, first_wait=self.bank[4])
        self.groups = 1
        if post:
            self.post_norm(post, scale)

    def post_norm(self, gain, factor):
        p, nc = self.p, self.nc
        act, dve = nc.scalar, nc.vector
        r = self.misc[:, NT:2 * NT]
        self.settle(dve)
        s, d = self.ps[4][:, 0:NT], self.sums
        if self.groups > 1:
            s = self.misc[:, 0:NT]
            p.wait(dve, d)
            d = p.DVE.mark(dve.tensor_reduce(s, self.ps[4][:, 0:KD * NT].rearrange("p (k i) -> p i k", i=NT), AX.X, ALU.add))
        d = self.rsqrt(s, r, d, D, factor)
        self.bank[4] = d
        rb = self.spread(r, d, self.sc[0], None, 5)
        p.wait(dve, rb)
        free = [None] * 3
        for k in range(KD):
            t = self.sc[1 + k % 3]
            p.wait(dve, free[k % 3])
            d = p.DVE.mark(dve.scalar_tensor_tensor(out=t[:, :], in0=self.tile(self.y_tiles, k), scalar=gain(k),
                                                    in1=self.ps[5], op0=ALU.mult, op1=ALU.mult))
            p.wait(dve, d)
            d = p.DVE.mark(dve.tensor_tensor(self.tile(self.x, k), self.tile(self.x, k), t[:, :], ALU.add))
            free[k % 3] = d
            self.sums = self.square_sums(k, d, self.tile(self.x, k), self.sc[4 + k % 2], self.sums if k > 1 else None)
        self.bank[5] = d
        self.groups = KD


    def project(self, w, first, turns, dst, func=None, tiles=KD):
        p, nc = self.p, self.nc
        pe, act, dve = nc.tensor, nc.scalar, nc.vector
        W, ps = self.w, self.ps
        self.settle(act, dve)
        p.wait(pe, self.bank[0:4], *self.u_ready)
        W.begin()
        by_act = 4 if func else 2
        with p.loop(turns, act=by_act, dve=4 - by_act, split=8, used=4) as i:
            for j in range(4):
                if func:
                    taken = p.ACT.ahead(j + 1)
                else:
                    taken = (p.ACT if j % 2 else p.DVE).ahead(j // 2 + 1)
                hi, lo, ready = W.chunk(w[i * 4 + (first + j)])
                p.wait(pe, ready)
                p.wait(pe, taken, back=1)
                for k in range(tiles):
                    m = self.mm3(ps[j], hi, lo, slice(k * P, (k + 1) * P), self.tile(self.uhi, k),
                                 self.tile(self.ulo, k), k == 0, k == tiles - 1)
                product = W.used.mark(m)
                to = dst[:, bass.ds((i * 4 + j) * T, T)]
                if func:
                    p.wait(act, product)
                    p.ACT.mark(act.activation(to, ps[j], func))
                elif j % 2:
                    p.wait(act, product)
                    p.ACT.mark(act.copy(to, ps[j]))
                else:
                    p.wait(dve, product)
                    p.DVE.mark(dve.tensor_copy(to, ps[j]))
        W.finish(turns)
        for j in range(4):
            self.bank[j] = [Done(p.ACT, p.ACT.count, False), Done(p.DVE, p.DVE.count, False)]

    def one_chunk(self, src, bank, x_pair, tiles, cols=P, out=None, ready=None, off=0):
        p = self.p
        hi, lo, split = self.w.chunk(src)
        p.wait(self.nc.tensor, split, self.bank[bank], ready)
        out = self.ps[bank][0:cols, :] if out is None else out
        for k in range(tiles):
            m = self.mm3(out, hi, lo, slice(off + k * cols, off + (k + 1) * cols), x_pair[0](k), x_pair[1](k), k == 0, k == tiles - 1)
        d = self.w.used.mark(m)
        self.bank[bank] = d
        return d

    def split_pair(self, src, hi, lo, ready, eng=None):
        p, nc = self.p, self.nc
        p.wait(nc.scalar, ready)
        h = p.ACT.mark(nc.scalar.copy(hi, src))
        p.wait(nc.vector, h, ready)
        l = p.DVE.mark(nc.vector.tensor_tensor(lo, src, hi.bitcast(F32), ALU.subtract))
        return [h, l]

    def U(self, n):
        return self.uf[:, n * 4 * T:(n + 1) * 4 * T]

    def B(self, n):
        return self.big[:, n * 4 * T:(n + 1) * 4 * T]

    def turn_tiles(self, src, n, bank0, dst, ready, rows=slice(0, P), cols=P):
        p, nc = self.p, self.nc
        p.wait(nc.tensor, ready, self.bank[bank0:bank0 + (n * cols + T - 1) // T])
        base = bank0 * T
        for q in range(n):
            m = nc.tensor.transpose(self.psum[:, base + q * cols:base + (q + 1) * cols],
                                    src[rows, q * P:(q + 1) * P], self.const[rows, C_ID + rows.start:C_ID + rows.stop])
        d = p.PE.mark(m)
        p.wait(nc.scalar, d)
        d = p.ACT.mark(nc.scalar.copy(dst, self.psum[:, base:base + n * cols]))
        for b in range(bank0, bank0 + (n * cols + T - 1) // T):
            self.bank[b] = d
        return d


    def gated_mixer(self):
        p, nc, a = self.p, self.nc, self.a
        self.stream_norm(lambda k: self.par("norm_pre", KD + k))
        gate_bias = self.misc[0:HEADS, 128:130]
        biased = nc.alloc_semaphore("gate_bias_loaded")
        nc.scalar.dma_start(gate_bias, a["gate_bias"]).then_inc(biased, 16)
        nc.vector.wait_ge(biased, 16)
        self.project(a["mix_in"], 0, 7, self.big)
        gates = self.one_chunk(a["mix_in"][28], 7, (lambda k: self.tile(self.uhi, k), lambda k: self.tile(self.ulo, k)), KD)
        self.settle(nc.scalar, nc.vector, nc.tensor)
        self.gate_rows = self.sc[4]
        p.wait(nc.vector, gates)
        self.bank[7] = p.DVE.mark(nc.vector.tensor_copy(self.gate_rows[:, :], self.ps[7]))
        self.hgrn2()
        self.mlstm(gates, gate_bias)
        self.settle(nc.scalar, nc.vector)
        self.u_ready = []
        self.y_tiles = self.big[:, 12 * T:(12 + KD) * T]
        for k in range(KD):
            src = self.B(0 if k < 4 else 2)[:, (k % 4) * T:(k % 4 + 1) * T]
            self.u_ready.append(self.split_pair(src, self.tile(self.uhi, k), self.tile(self.ulo, k), None))
        self.into_stream(a["mix_out"], 2, 4, 1, KD, self.uhi, self.ulo, 1.0, lambda k: self.par("norm_post", KD + k))

    def hgrn2(self):
        p, nc = self.p, self.nc
        pe, act, dve = nc.tensor, nc.scalar, nc.vector
        A, V, PE = p.ACT.mark, p.DVE.mark, p.PE.mark
        q, f, v_in, gate = self.B(0), self.B(1), self.B(2), self.B(3)
        logf, G = self.B(7), self.B(8)
        S, v = self.U(0), self.U(1)
        v_done = self.turn_tiles(v_in, 4 * NT, 0, v, None)
        sig = A(act.activation(f, f, ACT.Sigmoid))
        q_done = A(act.activation(q, q, ACT.Silu))
        gate_done = A(act.activation(gate, gate, ACT.Silu))
        mo_done = A(act.activation(self.B(6), self.B(6), ACT.Sigmoid))
        H = HEADS
        m = self.misc
        l0, l1 = (self.param[:, PARAMS["lb"] + H * k:PARAMS["lb"] + H * (k + 1)] for k in range(2))
        top, e, lb, rest = m[:, 32:36], m[:, 36:44], m[:, 44:48], m[:, 48:52]
        d = V(dve.tensor_tensor(top, l0, l1, ALU.max)); p.wait(dve, d)
        V(dve.tensor_tensor(e[:, 0:H], l0, top, ALU.subtract))
        d = V(dve.tensor_tensor(e[:, H:2 * H], l1, top, ALU.subtract)); p.wait(act, d)
        d = A(act.activation(e, e, ACT.Exp)); p.wait(dve, d)
        d = V(dve.tensor_tensor(lb, e[:, 0:H], e[:, H:2 * H], ALU.add)); p.wait(dve, d)
        d = V(dve.reciprocal(lb, lb)); p.wait(dve, d)
        d = V(dve.tensor_tensor(lb, lb, e[:, 0:H], ALU.mult)); p.wait(dve, d)
        d = V(dve.tensor_scalar(rest, lb, -1.0, 1.0, ALU.mult, ALU.add))
        p.wait(dve, d, sig)
        for h in range(H):
            t = slice(h * T, (h + 1) * T)
            d = V(dve.tensor_scalar(logf[:, t], f[:, t], rest[:, h:h + 1], lb[:, h:h + 1], ALU.mult, ALU.add))
        p.wait(dve, d)
        k = f
        k_done = V(dve.tensor_scalar(k, logf, -1.0, 1.0, ALU.mult, ALU.add))
        p.wait(act, k_done)
        d = A(act.activation(logf, logf, ACT.Ln))
        p.wait(dve, d)
        for h in range(H):
            t = slice(h * T, (h + 1) * T)
            G_done = V(dve.tensor_tensor_scan(G[:, t], self.cst(C_RESET, T), logf[:, t], 0.0, ALU.mult, ALU.add))
        z = V(dve.memset(S, 0.0))
        p.wait(dve, q_done, k_done, G_done, z)
        work = (self.B(9), self.B(10))
        used = [None, None]
        def square_masks(c):
            return self.cst(c).bitcast(U32).unsqueeze(1).broadcast_to([P, 4 * NT, P])
        def scores(n, lhs, rhs, ready, mask):
            b0 = 4 * (n % 2)
            p.wait(pe, ready, self.bank[b0:b0 + 4])
            for s in range(4 * NT):
                t = slice(s * P, (s + 1) * P)
                mm = pe.matmul(self.psum[:, b0 * T + s * P:b0 * T + (s + 1) * P], lhs[:, t], rhs(t), start=True, stop=True)
            done = PE(mm)
            p.wait(dve, done, scores.last)
            ps3 = self.psum[:, b0 * T:(b0 + 4) * T].rearrange("p (s t) -> p s t", t=P)
            scores.last = V(dve.copy_predicated(S.rearrange("p (s t) -> p s t", t=P), square_masks(mask), ps3))
            self.bank[b0:b0 + 4] = [scores.last] * 4
            return done
        scores.last = None
        d = V(dve.tensor_tensor(work[0], q, k, ALU.mult))
        used[0] = scores(0, work[0], lambda t: self.cst(C_ONE), d, C_ID)
        pending = None
        for n, half in enumerate(LEVELS):
            w = work[(n + 1) % 2]
            cut = lambda x: x.rearrange("p (c two h) -> p c two h", two=2, h=half)
            g4, w4, q4, k4 = cut(G), cut(w), cut(q), cut(k)
            blocks = H * T // (2 * half)
            g_end = g4[:, :, 0, half - 1:half].broadcast_to([P, blocks, half])
            p.wait(dve, used[(n + 1) % 2])
            V(dve.tensor_tensor(w4[:, :, 0, :], g_end, g4[:, :, 0, :], ALU.subtract))
            d = V(dve.tensor_tensor(w4[:, :, 1, :], g4[:, :, 1, :], g_end, ALU.subtract))
            p.wait(act, d)
            ex = A(act.activation(w, w, ACT.Exp))
            if pending is not None:
                used[pending[0] % 2] = scores(*pending[1:])
            p.wait(dve, ex)
            V(dve.tensor_tensor(w4[:, :, 0, :], w4[:, :, 0, :], k4[:, :, 0, :], ALU.mult))
            d = V(dve.tensor_tensor(w4[:, :, 1, :], w4[:, :, 1, :], q4[:, :, 1, :], ALU.mult))
            pending = (n + 1, n + 1, w, (lambda t, w=w: w[:, t]), d, C_LEVEL + n * P)
        used[pending[0] % 2] = scores(*pending[1:])
        G3 = G.rearrange("p (c t) -> p c t", t=CH)
        e_end = m[:, 64:64 + H * NC]
        d = A(act.activation(e_end, G3[:, :, CH - 1], ACT.Exp))
        kw, kt = work[0], work[1]
        p.wait(dve, used[0])
        d = V(dve.tensor_tensor(kw.rearrange("p (c t) -> p c t", t=CH), G3[:, :, CH - 1:CH].broadcast_to([P, H * NC, CH]), G3, ALU.subtract))
        p.wait(act, d)
        e_done = A(act.activation(kw, kw, ACT.Exp))
        qe = logf
        d = A(act.activation(qe, G, ACT.Exp))
        p.wait(dve, e_done)
        kw_done = V(dve.tensor_tensor(kw, kw, k, ALU.mult))
        p.wait(dve, d)
        qe_done = V(dve.tensor_tensor(qe, qe, q, ALU.mult))
        p.wait(act, used[1])
        kt_done = self.turn_tiles(kw, 4 * NT, 0, kt, [kw_done, used[1]])
        state = lambda c, h: self.uf[:, 8 * T + (c * H + h) * P:8 * T + (c * H + h + 1) * P]
        p.wait(pe, kt_done, v_done)
        made = []
        for c in range(NC - 1):
            b = c % 4
            rows = slice((c % 2) * CH, (c % 2 + 1) * CH)
            p.wait(pe, self.bank[b])
            for h in range(H):
                t = slice((h * NT + c // 2) * P, (h * NT + c // 2 + 1) * P)
                mm = pe.matmul(self.ps[b][:, h * P:(h + 1) * P], kt[rows, t], v[rows, t], start=True, stop=True)
            d = PE(mm)
            p.wait(dve, d)
            if c == 0:
                d = V(dve.tensor_copy(self.uf[:, 8 * T + H * P:8 * T + 2 * H * P], self.ps[b]))
            else:
                p.wait(dve, made[-1], e_done)
                for h in range(H):
                    d = V(dve.scalar_tensor_tensor(out=state(c + 1, h), in0=state(c, h), scalar=e_end[:, h * NC + c:h * NC + c + 1],
                                                   in1=self.ps[b][:, h * P:(h + 1) * P], op0=ALU.mult, op1=ALU.add))
            made.append(d)
            self.bank[b] = d
        p.wait(pe, scores.last, qe_done, made[-1])
        out = self.B(2)
        sq = self.sc[0:2]
        self.settle(act)
        o_free = None
        stats = []
        for h in range(H):
            b = 4 + h % 2
            p.wait(pe, self.bank[b])
            for i in range(NT):
                t = slice((h * NT + i) * P, (h * NT + i + 1) * P)
                mm = pe.matmul(self.ps[b][:, i * P:(i + 1) * P], v[:, t], S[:, t], start=True, stop=False)
                for c in (2 * i, 2 * i + 1):
                    if c:
                        mm = pe.matmul(self.ps[b][:, c * CH:(c + 1) * CH], state(c, h),
                                       qe[:, h * T + c * CH:h * T + (c + 1) * CH], start=False, stop=c % 2 == 1)
            d = PE(mm)
            p.wait(dve, d, v_done)
            t = slice(h * T, (h + 1) * T)
            o_done = V(dve.tensor_copy(out[:, t], self.ps[b]))
            self.bank[b] = o_done
            stats.append(self.head_sums(out[:, t], h, o_done, stats[-2] if h > 1 else None))
        self.head_norm(out, "hgrn_norm", stats[-1], None, gate, self.B(0), gate_done)
        self.mo_done = mo_done

    def head_sums(self, src, h, ready, sq_free):
        p, nc = self.p, self.nc
        sq = self.sc[h % 2]
        p.wait(nc.scalar, ready, sq_free)
        d = p.ACT.mark(nc.scalar.activation(sq[:, :], src, ACT.Square))
        return self.token_sums(sq, [d], lambda i: self.ps[6][:, h * NT + i:h * NT + i + 1], first_wait=self.bank[6])

    def head_norm(self, o, gain, ready, scale, gate, dst, gate_done):
        p, nc = self.p, self.nc
        dve = nc.vector
        n = HEADS * NT
        r = self.misc[:, 32:32 + n]
        self.settle(dve)
        if scale is None:
            d = self.rsqrt(self.ps[6][:, 0:n], r, ready, P)
        else:
            d = p.DVE.mark(dve.tensor_tensor(r, self.ps[6][:, 0:n], scale, ALU.mult))
            p.wait(dve, d)
            d = p.DVE.mark(dve.tensor_tensor(r, r, scale, ALU.mult))
            d = self.rsqrt(r, r, d, P)
            p.wait(dve, d)
            d = p.DVE.mark(dve.tensor_tensor(r, r, scale, ALU.mult))
        self.bank[6] = d
        for h in range(HEADS):
            t = slice(h * T, (h + 1) * T)
            rb = self.spread(r[:, h * NT:(h + 1) * NT], d, self.sc[2 + h % 2], self.spread_used[h % 2], 7 - h % 2 * 4)
            self.spread_used[h % 2] = rb
            p.wait(dve, rb, gate_done)
            e = p.DVE.mark(dve.scalar_tensor_tensor(out=dst[:, t], in0=o[:, t], scalar=self.par(gain, h),
                                                    in1=self.ps[7 - h % 2 * 4], op0=ALU.mult, op1=ALU.mult))
            self.bank[7 - h % 2 * 4] = e
            p.wait(dve, e)
            e = p.DVE.mark(dve.tensor_tensor(dst[:, t], dst[:, t], gate[:, t], ALU.mult))
        return e

    def mlstm(self, gates, gate_bias):
        p, nc = self.p, self.nc
        pe, act, dve = nc.tensor, nc.scalar, nc.vector
        A, V, PE = p.ACT.mark, p.DVE.mark, p.PE.mark
        H, m = HEADS, self.misc
        v_in, gate = self.B(5), self.B(6)
        v, qk, x = self.B(10), self.B(9), self.B(4)
        self.settle(act, dve, pe)
        v_done = self.turn_tiles(v_in, 4 * NT, 0, v, None)
        for t4 in range(4):
            xt, yt = self.tile(x, t4), self.tile(qk, t4)
            cw = lambda tap: self.par("conv_w", tap * 4 + t4)
            d = V(dve.tensor_scalar(yt, xt, cw(CONV - 1), self.par("conv_b", t4), ALU.mult, ALU.add))
            for lag in range(1, CONV):
                p.wait(dve, d)
                d = V(dve.scalar_tensor_tensor(out=yt[:, lag:T], in0=xt[:, 0:T - lag], scalar=cw(CONV - 1 - lag),
                                               in1=yt[:, lag:T], op0=ALU.mult, op1=ALU.add))
        p.wait(act, d)
        qk_done = A(act.activation(qk, qk, ACT.Silu))
        R = lambda n: self.sc[n][0:H, :]
        li, z, lf, B, w, M = (R(n) for n in (0, 1, 2, 3, 4, 5))
        d = V(dve.tensor_scalar(li, self.gate_rows[0:H, :], gate_bias[:, 0:1], None, ALU.add))
        d = V(dve.tensor_scalar(z, self.gate_rows[32:32 + H, :], gate_bias[:, 1:2], None, ALU.add))
        p.wait(act, d)
        d = A(act.activation(lf, z, ACT.Abs)); p.wait(act, d)
        d = A(act.activation(lf, lf, ACT.Exp, scale=-1.0)); p.wait(act, d)
        d = A(act.activation(lf, lf, ACT.Ln, bias=1.0)); p.wait(dve, d)
        d = V(dve.scalar_tensor_tensor(out=lf, in0=z, scalar=0.0, in1=lf, op0=ALU.min, op1=ALU.subtract)); p.wait(dve, d)
        ones = R(6)
        d = V(dve.memset(ones, 1.0)); p.wait(dve, d)
        d = V(dve.tensor_tensor_scan(B, ones, lf, 0.0, ALU.mult, ALU.add)); p.wait(dve, d)
        d = V(dve.tensor_tensor(w, li, B, ALU.subtract)); p.wait(dve, d)
        M_done = V(dve.tensor_tensor_scan(M, ones, w, 0.0, ALU.mult, ALU.max)); p.wait(dve, M_done)
        d = V(dve.tensor_tensor(z, B, M, ALU.add)); p.wait(act, d)
        em_done = A(act.activation(z, z, ACT.Exp, scale=-1.0))
        p.wait(pe, em_done, self.bank[6])
        for n, row in ((0, w), (1, z)):
            for i in range(NT):
                mm = pe.transpose(self.ps[6][:, 32 + (n * NT + i) * H:32 + (n * NT + i + 1) * H], row[:, i * P:(i + 1) * P],
                                  self.const[0:H, C_ID:C_ID + H])
        d = PE(mm)
        cols = m[:, 64:64 + 2 * NT * H]
        p.wait(act, d)
        cols_done = A(act.copy(cols, self.ps[6][:, 32:32 + 2 * NT * H]))
        self.bank[6] = cols_done
        w_col = lambda i, h: cols[:, i * H + h:i * H + h + 1]
        out = self.B(7)
        sum_w = self.ps[6][:, 128:128 + H * NT]
        stats = []
        p.wait(pe, qk_done, M_done, v_done)
        pair = (self.B(1), self.B(8))
        pv = [None, None]
        for h in range(H):
            E = pair[h % 2]
            rows = slice((h % 2) * ML_QK, (h % 2 + 1) * ML_QK)
            qh, kh = self.tile(qk, h // 2)[rows, :], self.tile(qk, 2 + h // 2)[rows, :]
            p.wait(pe, self.bank[7])
            rb = PE(pe.matmul(self.ps[7], self.const[0:H, C_SEL + h * P:C_SEL + (h + 1) * P], M, start=True, stop=True))
            p.wait(dve, rb, cols_done, pv[h % 2])
            for (i, t0, n, c) in CAUSAL:
                d = V(dve.tensor_scalar(E[:, c:c + n], self.ps[7][:, t0:t0 + n], w_col(i, h), 0.0, ALU.subtract, ALU.max))
            self.bank[7] = d
            p.wait(act, d)
            ex = A(act.activation(E[:, 0:N_CAUSAL], E[:, 0:N_CAUSAL], ACT.Exp, scale=-1.0))
            b0 = 3 * (h % 2)
            qk_ps = self.causal_product(b0, lambda i: kh[:, i * P:(i + 1) * P], lambda t0, n: qh[:, t0:t0 + n], None)
            p.wait(dve, ex, qk_ps)
            d = V(dve.scalar_tensor_tensor(out=E[:, 0:N_CAUSAL], in0=self.psum[:, b0 * T:b0 * T + N_CAUSAL], scalar=ML_QK ** -0.5,
                                           in1=E[:, 0:N_CAUSAL], op0=ALU.mult, op1=ALU.mult))
            self.bank[b0:b0 + 3] = [d] * 3
            p.wait(dve, d)
            d = self.mask_diagonals(E, C_LE)
            p.wait(pe, d, self.bank[b0], self.bank[6])
            bn = b0 + 2
            nd = PE(self.causal_values(self.ps[b0], lambda i: v[:, (h * NT + i) * P:(h * NT + i + 1) * P], E))
            for j in range(NT):
                for i in range(j + 1):
                    c = causal_column(i, j)
                    mm = pe.matmul(sum_w[:, h * NT + j:h * NT + j + 1], E[:, c:c + P], self.cst(C_ONE, 1), start=i == 0, stop=i == j)
            pv[h % 2] = PE(mm)
            p.wait(dve, nd)
            t = slice(h * T, (h + 1) * T)
            o_done = V(dve.tensor_copy(out[:, t], self.ps[b0]))
            self.bank[b0] = o_done
            if h == 0:
                self.settle(act)
            stats.append(self.head_sums(out[:, t], h, o_done, stats[-2] if h > 1 else None))
        scale = m[:, 96:96 + H * NT]
        neg = m[:, 112:112 + H * NT]
        self.settle(dve)
        d = V(dve.tensor_scalar(neg, sum_w, -1.0, None, ALU.mult)); p.wait(dve, d)
        d = V(dve.tensor_tensor(scale, sum_w, neg, ALU.max)); p.wait(dve, d)
        em = cols[:, NT * H:2 * NT * H].rearrange("p (i h) -> p h i", h=H)
        s3 = scale.rearrange("p (h i) -> p h i", h=H)
        d = V(dve.tensor_tensor(s3, s3, em, ALU.max)); p.wait(dve, d)
        d = V(dve.reciprocal(scale, scale)); p.wait(dve, d)
        self.head_norm(out, "mlstm_norm", [d, stats[-1]], scale, gate, self.B(2), self.mo_done)


    def attention_mixer(self):
        p, nc, a = self.p, self.nc, self.a
        pe, act, dve = nc.tensor, nc.scalar, nc.vector
        A, V, PE = p.ACT.mark, p.DVE.mark, p.PE.mark
        self.stream_norm(lambda k: self.par("mix_norm", k))
        pair = (lambda k: self.tile(self.uhi, k), lambda k: self.tile(self.ulo, k))
        self.project(a["proj_in"], 0, 4, self.big)
        for j in range(2):
            d = self.one_chunk(a["proj_in"][16 + j], j, pair, KD)
            p.wait(act, d)
            self.bank[j] = A(act.copy(self.tile(self.big, 16 + j), self.ps[j]))
        self.project(a["proj_in"], 18, 4, self.big[:, GATE_AT * T:], ACT.Sigmoid)
        self.settle(pe, act, dve)
        self.rope_tables()
        self.latents()
        self.mla()
        self.stick()
        self.merge()

    def rope_tables(self):
        p, nc = self.p, self.nc
        act, dve = nc.scalar, nc.vector
        A, V = p.ACT.mark, p.DVE.mark
        rows = slice(NOPE, QK)
        pos, ang, n, t = (self.sc[i][rows, :] for i in (0, 1, 2, 3))
        cos, sin = self.cos, self.sin = self.sc[5][rows, :], self.sc[6][rows, :]
        self.settle(act, dve)
        landed = nc.alloc_semaphore("positions_loaded")
        act.dma_start(pos.bitcast(I32), self.a["positions"].broadcast_to([ROPE, T])).then_inc(landed, 16)
        dve.wait_ge(landed, 16)
        d = V(dve.tensor_copy(ang, pos.bitcast(I32))); p.wait(dve, d)
        d = V(dve.tensor_scalar(ang, ang, self.const[rows, C_FREQ:C_FREQ + 1], None, ALU.mult)); p.wait(dve, d)
        magic = 1.5 * 2.0 ** 23
        d = V(dve.tensor_scalar(n, ang, 1.0 / (2 * np.pi), magic, ALU.mult, ALU.add)); p.wait(dve, d)
        d = V(dve.tensor_scalar(n, n, -magic, None, ALU.add)); p.wait(dve, d)
        c1 = 6.28125
        c2 = float(np.floor((2 * np.pi - c1) * 2 ** 22) / 2 ** 22)
        c3 = 2 * np.pi - c1 - c2
        for c in (c1, c2, c3):
            d = V(dve.scalar_tensor_tensor(out=ang, in0=n, scalar=-c, in1=ang, op0=ALU.mult, op1=ALU.add)); p.wait(dve, d)
        edge = 3.1415925
        d = V(dve.tensor_scalar(t, ang, float(np.pi / 2), None, ALU.add)); p.wait(dve, d)
        d = V(dve.tensor_scalar(n, t, float(np.pi), -2 * float(np.pi), ALU.is_gt, ALU.mult)); p.wait(dve, d)
        d = V(dve.tensor_tensor(t, t, n, ALU.add)); p.wait(dve, d)
        V(dve.tensor_scalar(t, t, edge, -edge, ALU.min, ALU.max))
        d = V(dve.tensor_scalar(ang, ang, edge, -edge, ALU.min, ALU.max)); p.wait(act, d)
        A(act.activation(cos, t, ACT.Sin))
        self.tables_done = A(act.activation(sin, ang, ACT.Sin))

    def latents(self):
        p, nc = self.p, self.nc
        dve = nc.vector
        self.settle(nc.scalar, dve)
        self.latent_ready = []
        for name, first, n in (("q_latent", 0, KCQ), ("kv_latent", KCQ, KCKV)):
            s = [None, None]
            for k in range(n):
                s[k % 2] = self.square_sums(first + k, None, self.tile(self.big, first + k), self.sc[k % 2], s[k % 2],
                                            wait_bank=self.bank[4])
            d = [x for x in s if x]
            sums, r = self.misc[:, 0:NT], self.misc[:, NT:2 * NT]
            self.settle(dve)
            view = self.ps[4][:, first * NT:(first + n) * NT].rearrange("p (k i) -> p i k", i=NT)
            d = p.DVE.mark(dve.tensor_reduce(sums, view, AX.X, ALU.add))
            self.bank[4] = d
            d = self.rsqrt(sums, r, d, n * P)
            rb = self.spread(r, d, self.sc[2], None, 5)
            for k in range(n):
                p.wait(dve, rb)
                t = self.tile(self.big, first + k)
                d = p.DVE.mark(dve.scalar_tensor_tensor(out=t, in0=t, scalar=self.par(name, k), in1=self.ps[5],
                                                        op0=ALU.mult, op1=ALU.mult))
                self.latent_ready += self.split_pair(t, self.tile(self.uhi, first + k), self.tile(self.ulo, first + k), d)
            self.bank[5] = d
            self.settle(nc.scalar, dve)

    def rotate(self, x, ready, bank, tmp):
        p, nc = self.p, self.nc
        rows = slice(NOPE, QK)
        p.wait(nc.tensor, ready, self.bank[bank])
        rot = self.ps[bank][rows, :]
        turned = p.PE.mark(nc.tensor.matmul(rot, self.const[rows, C_ROT:C_ROT + ROPE], x, start=True, stop=True))
        p.wait(nc.vector, turned, self.tables_done)
        p.DVE.mark(nc.vector.tensor_tensor(x, x, self.cos, ALU.mult))
        d = p.DVE.mark(nc.vector.tensor_tensor(tmp[rows, :], rot, self.sin, ALU.mult))
        self.bank[bank] = d
        p.wait(nc.vector, d)
        return p.DVE.mark(nc.vector.tensor_tensor(x, x, tmp[rows, :], ALU.add))

    def mla(self):
        p, nc, a = self.p, self.nc, self.a
        pe, act, dve = nc.tensor, nc.scalar, nc.vector
        A, V, PE = p.ACT.mark, p.DVE.mark, p.PE.mark
        q_gain, k_gain = self.misc[0:QK, 128:129], self.misc[0:QK, 129:130]
        landed = nc.alloc_semaphore("head_gains_loaded")
        act.dma_start(self.misc[0:QK, 128:130], a["head_gains"]).then_inc(landed, 16)
        dve.wait_ge(landed, 16)
        Q = [self.tile(self.big, 34 + h) for h in range(AH)]
        K = [self.tile(self.uf, n) for n in (5, 6, 7, 13, 14, 15)] + [self.tile(self.big, n) for n in (42, 43)]
        v = self.B(0)
        v_at = lambda h, i: v[:, (h * NT + i) * HV:(h * NT + i + 1) * HV]
        rope_rows = slice(NOPE, QK)
        kr = self.tile(self.big, KCQ + KCKV)[rope_rows, :]
        krot = self.sc[4]
        sq = self.sc[0:2]
        self.settle(act, dve)
        kr_sq = None
        for n in range(2):
            kr_sq = A(act.activation(self.sc[2 + n][rope_rows, :], kr, ACT.Square))
        d = V(dve.tensor_scalar(krot[rope_rows, :], kr, k_gain[rope_rows, :], None, ALU.mult))
        krot_done = self.rotate(krot[rope_rows, :], d, 3, self.sc[0])
        cq = (lambda k: self.tile(self.uhi, k), lambda k: self.tile(self.ulo, k))
        ckv = (lambda k: self.tile(self.uhi, KCQ + k), lambda k: self.tile(self.ulo, KCQ + k))
        sums = [None, None]
        q_done = []
        for g in range(2):
            hi, lo, ready = self.w.chunk(a["q_up"][g])
            p.wait(pe, ready, self.latent_ready)
            for j in range(4):
                h, b = 4 * g + j, j % 2
                p.wait(pe, self.bank[b])
                for k in range(KCQ):
                    m = self.mm3(self.ps[b][0:QK, :], hi, lo, slice((j * KCQ + k) * QK, (j * KCQ + k + 1) * QK), cq[0](k), cq[1](k),
                                 k == 0, k == KCQ - 1)
                d = self.w.used.mark(m) if j == 3 else PE(m)
                p.wait(act, d, sums[h % 2], krot_done)
                s = A(act.activation(sq[h % 2][0:QK, :], self.ps[b][0:QK, :], ACT.Square))
                p.wait(dve, s)
                g_done = V(dve.tensor_scalar(Q[h][0:QK, :], self.ps[b][0:QK, :], q_gain, None, ALU.mult))
                self.bank[b] = g_done
                sums[h % 2] = self.token_sums(sq[h % 2], s, lambda i: self.ps[6][:, h * NT + i:h * NT + i + 1], rows=QK,
                                              first_wait=self.bank[6])
                p.wait(dve, q_done[-2] if h > 1 else krot_done)
                q_done.append(self.rotate(Q[h][rope_rows, :], g_done, 2 + h % 2, self.vt[h % 2]))
        self.settle(act, dve)
        ksum, vt_used = [None, None], [None, None]
        k_done = []
        for g in range(2):
            hi, lo, ready = self.w.chunk(a["kv_up"][g])
            p.wait(pe, ready)
            for j in range(4):
                h, b = 4 * g + j, j % 2
                p.wait(pe, self.bank[b])
                for k in range(KCKV):
                    m = self.mm3(self.ps[b], hi, lo, slice((j * KCKV + k) * P, (j * KCKV + k + 1) * P), ckv[0](k), ckv[1](k),
                                 k == 0, k == KCKV - 1)
                d = self.w.used.mark(m) if j == 3 else PE(m)
                ks = self.sc[2 + h % 2]
                vt = self.vt[h % 2]
                p.wait(act, d, ksum[h % 2], vt_used[h % 2], kr_sq)
                A(act.activation(ks[0:NOPE, :], self.ps[b][0:NOPE, :], ACT.Square))
                s = A(act.copy(vt[NOPE:P, :], self.ps[b][NOPE:P, :]))
                p.wait(dve, s)
                k_done.append(V(dve.tensor_scalar(K[h][0:NOPE, :], self.ps[b][0:NOPE, :], k_gain[0:NOPE, :], None, ALU.mult)))
                self.bank[b] = k_done[-1]
                ksum[h % 2] = self.token_sums(ks, s, lambda i: self.ps[6][:, (AH + h) * NT + i:(AH + h) * NT + i + 1], rows=QK)
                p.wait(pe, self.bank[7])
                for i in range(NT):
                    m = pe.transpose(self.ps[7][:, i * HV:(i + 1) * HV], vt[NOPE:P, i * P:(i + 1) * P], self.const[NOPE:P, C_ID + NOPE:C_ID + P])
                vt_used[h % 2] = PE(m)
                p.wait(dve, vt_used[h % 2])
                self.bank[7] = V(dve.tensor_copy(v[:, h * NT * HV:(h + 1) * NT * HV], self.ps[7][:, 0:NT * HV]))
        v_done = self.bank[7]
        self.settle(act, dve)
        r = self.misc[:, 32:32 + 2 * AH * NT]
        d = self.rsqrt(self.ps[6][:, 0:2 * AH * NT], r, ksum, QK)
        self.bank[6] = d
        rq, rk = r[:, 0:AH * NT], r[:, AH * NT:2 * AH * NT]
        for h in range(AH):
            b = 4 + h % 2
            rb = self.spread(rk[:, h * NT:(h + 1) * NT], d, self.sc[h % 2], self.spread_used[h % 2], b, rows=P)
            self.spread_used[h % 2] = rb
            p.wait(dve, rb, k_done[h], krot_done)
            V(dve.tensor_tensor(K[h][0:NOPE, :], K[h][0:NOPE, :], self.ps[b][0:NOPE, :], ALU.mult))
            k_done[h] = self.bank[b] = V(dve.tensor_tensor(K[h][rope_rows, :], krot[rope_rows, :], self.ps[b][rope_rows, :], ALU.mult))
        p.wait(dve, d)
        rq_done = V(dve.tensor_scalar(rq, rq, QK ** -0.5, None, ALU.mult))
        probs = [self.uf[:, n * N_CAUSAL:(n + 1) * N_CAUSAL] for n in range(2)]
        turned = [self.uf[:, 8 * T + n * N_CAUSAL:8 * T + (n + 1) * N_CAUSAL] for n in range(2)]
        self.settle(pe, act, dve)
        mx, nb, rs = (self.misc[:, c:c + AH * NT] for c in (96, 130, 162))
        self.o_mla = [Q[2 * n] for n in range(AH // 2)]
        exps, divided, turned_used, probs_used = [None] * AH, [None] * AH, [None] * AH, [None] * AH

        def logits(h):
            p.wait(pe, self.bank[0:3], k_done[h], q_done[h])
            for i, c in ROWS:
                n = (i + 1) * P
                pe.matmul(self.psum[:, c:c + n], Q[h][0:QK, i * P:(i + 1) * P], K[h][0:QK, 0:n], start=True, stop=True)
                m = pe.matmul(self.psum[:, c + n - P:c + n], self.cst(C_ID), self.cst(C_NGT), start=False, stop=True,
                              skip_group_check=True)
            d = PE(m)
            p.wait(dve, d, rq_done)
            for i, c in ROWS:
                d = V(dve.tensor_reduce(mx[:, h * NT + i:h * NT + i + 1], self.psum[:, c:c + (i + 1) * P], AX.X, ALU.max))
            p.wait(dve, d)
            hs = slice(h * NT, (h + 1) * NT)
            d = V(dve.scalar_tensor_tensor(out=nb[:, hs], in0=mx[:, hs], scalar=-1.0, in1=rq[:, hs], op0=ALU.mult, op1=ALU.mult))
            p.wait(act, d, probs_used[h - 2] if h > 1 else None)
            for i, c in ROWS:
                x = h * NT + i
                e = A(act.activation(probs[h % 2][:, c:c + (i + 1) * P], self.psum[:, c:c + (i + 1) * P], ACT.Exp,
                                     bias=nb[:, x:x + 1], scale=rq[:, x:x + 1], accum_out=rs[:, x:x + 1]))
            exps[h] = e
            self.bank[0:3] = [e] * 3

        def values(h):
            hs = slice(h * NT, (h + 1) * NT)
            w, wt = probs[h % 2], turned[h % 2]
            p.wait(dve, exps[h])
            d = V(dve.reciprocal(rs[:, hs], rs[:, hs]))
            p.wait(dve, d)
            for i, c in ROWS:
                d = V(dve.tensor_scalar(w[:, c:c + (i + 1) * P], w[:, c:c + (i + 1) * P], rs[:, h * NT + i:h * NT + i + 1], None, ALU.mult))
            p.wait(pe, d, self.bank[3:6])
            for i, c in ROWS:
                for j in range(i + 1):
                    to = 3 * T + causal_column(j, i)
                    m = pe.transpose(self.psum[:, to:to + P], w[:, c + j * P:c + (j + 1) * P], self.cst(C_ID))
            d = probs_used[h] = PE(m)
            p.wait(dve, d, turned_used[h - 2] if h > 1 else None)
            d = V(dve.tensor_copy(wt, self.psum[:, 3 * T:3 * T + N_CAUSAL]))
            self.bank[3:6] = [d] * 3
            rows = slice(h % 2 * HV, (h % 2 + 1) * HV)
            p.wait(pe, d, v_done, self.bank[6 + h % 2])
            turned_used[h] = PE(self.causal_values(self.ps[6 + h % 2][rows, :], lambda i: v_at(h, i), wt))
            p.wait(act, turned_used[h])
            self.bank[6 + h % 2] = A(act.copy(self.o_mla[h // 2][rows, :], self.ps[6 + h % 2][rows, :]))

        for h in range(AH + 1):
            if h < AH:
                logits(h)
            if h:
                values(h - 1)

    def stick(self):
        p, nc = self.p, self.nc
        pe, act, dve = nc.tensor, nc.scalar, nc.vector
        A, V, PE = p.ACT.mark, p.DVE.mark, p.PE.mark
        self.settle(pe, act, dve)
        sq, sk, sv = (lambda n, f=f: self.tile(self.big, f + n) for f in (6, 10, 14))
        v = self.B(0)
        v_done = self.turn_tiles(self.big[:, 14 * T:18 * T], 4 * NT, 0, v, None)
        q_done = V(dve.tensor_scalar(self.big[:, 6 * T:10 * T], self.big[:, 6 * T:10 * T], HV ** -0.5, None, ALU.mult))
        soft = [self.uf[:, n * N_CAUSAL:(n + 1) * N_CAUSAL] for n in range(2)]
        weight = [self.uf[:, 8 * T + n * N_CAUSAL:8 * T + (n + 1) * N_CAUSAL] for n in range(2)]
        self.o_sb = [self.tile(self.uf, n) for n in (5, 6, 7, 13)]
        z_ps, e_ps = 0, 3 * T
        p.wait(pe, q_done, v_done)
        soft_done, soft_used, weight_used = [None] * AH, [None] * AH, [None] * AH

        def logits(h, base, stop):
            rows = slice(h % 2 * HV, (h % 2 + 1) * HV)
            for i, t0, n, c in CAUSAL:
                m = pe.matmul(self.psum[:, base + c:base + c + n], sk(h // 2)[rows, i * P:(i + 1) * P], sq(h // 2)[rows, t0:t0 + n],
                              start=stop or c in (0, T, 2 * T), stop=True, skip_group_check=not stop)
            return m

        def softplus(h):
            s = soft[h % 2]
            p.wait(pe, self.bank[0:3])
            d = PE(logits(h, z_ps, True))
            zs = self.psum[:, z_ps:z_ps + N_CAUSAL]
            p.wait(act, d, soft_used[h - 2] if h > 1 else None)
            d = A(act.activation(s, zs, ACT.Abs)); p.wait(act, d)
            d = A(act.activation(s, s, ACT.Exp, scale=-1.0)); p.wait(act, d)
            d = A(act.activation(s, s, ACT.Ln, bias=1.0)); p.wait(dve, d)
            d = V(dve.scalar_tensor_tensor(out=s, in0=zs, scalar=0.0, in1=s, op0=ALU.max, op1=ALU.add))
            self.bank[0:3] = [d] * 3
            p.wait(dve, d)
            soft_done[h] = self.mask_diagonals(s, C_LT)

        def weights(h):
            s, w = soft[h % 2], weight[h % 2]
            p.wait(pe, self.bank[3:6])
            logits(h, e_ps, False)
            p.wait(pe, soft_done[h])
            add = lambda c, n, lhs, rhs: pe.matmul(self.psum[:, e_ps + c:e_ps + c + n], self.cst(lhs), rhs,
                                                 start=False, stop=True, skip_group_check=True)
            for i, t0, n, c in CAUSAL:
                add(c, n, C_NSUF, s[:, c:c + n])
            for i in range(NT):
                for later in range(i + 1, NT):
                    for (i2, t0, n, c) in CAUSAL:
                        if i2 == later:
                            to = causal_column(i, t0 // P)
                            add(to, n, C_NONE, s[:, c:c + n])
            never = self.cst(C_NGE).unsqueeze(1).broadcast_to([P, NT, P])
            m = add(0, T, C_ID, never)
            d = soft_used[h] = PE(m)
            p.wait(act, d, weight_used[h - 2] if h > 1 else None)
            d = A(act.activation(w, self.psum[:, e_ps:e_ps + N_CAUSAL], ACT.Exp))
            self.bank[3:6] = [d] * 3
            rows = slice(h % 2 * HV, (h % 2 + 1) * HV)
            p.wait(pe, d, self.bank[6 + h % 2])
            v_at = lambda i: v[:, ((h // 2) * NT + i) * P + h % 2 * HV:((h // 2) * NT + i) * P + (h % 2 + 1) * HV]
            weight_used[h] = PE(self.causal_values(self.ps[6 + h % 2][rows, :], v_at, w))
            p.wait(dve, weight_used[h])
            self.bank[6 + h % 2] = V(dve.tensor_copy(self.o_sb[h // 2][rows, :], self.ps[6 + h % 2][rows, :]))

        for h in range(AH + 1):
            if h < AH:
                softplus(h)
            if h:
                weights(h - 1)

    def merge(self):
        p, nc, a = self.p, self.nc, self.a
        pe, act, dve = nc.tensor, nc.scalar, nc.vector
        A, V, PE = p.ACT.mark, p.DVE.mark, p.PE.mark
        W, ps = self.w, self.ps
        self.settle(pe, act, dve)
        moved = []
        for n in range(4):
            to = self.tile(self.big, n)
            moved.append(A(act.copy(to, self.o_sb[n])))
        ready = []
        p.wait(dve, moved)
        p.wait(act, moved)
        for n in range(KD):
            src = self.o_mla[n] if n < 4 else self.tile(self.big, n - 4)
            ready += self.split_pair(src, self.tile(self.uhi, n), self.tile(self.ulo, n), None)
        self.settle(pe, act, dve)
        t1, t2 = self.sc[0:2], self.sc[2:4]
        W.begin()
        with p.loop(2, act=4, dve=16, split=8, used=4) as i:
            for j in range(4):
                lo_done = p.DVE.ahead(4 * j + 4)
                before = lambda eng: (p.wait(eng, p.DVE.ahead(4 * j + 4 - 8)) if j > 1 else p.wait(eng, p.DVE.ahead(4 * j + 4 + 8), back=1))
                hi, lo, split = W.chunk(a["branch"][i * 4 + j])
                p.wait(pe, split)
                before(pe)
                b = 2 * (j % 2)
                for half in range(2):
                    for k in range(4):
                        m = self.mm3(ps[b + half], hi, lo, slice((4 * half + k) * P, (4 * half + k + 1) * P),
                                     self.tile(self.uhi, 4 * half + k), self.tile(self.ulo, 4 * half + k), k == 0, k == 3)
                product = W.used.mark(m)
                p.wait(dve, product)
                before(dve)
                x, y = t1[j % 2][:, :], t2[j % 2][:, :]
                g = lambda n: self.big[:, bass.ds((i * 4 + (GATE_AT + n * KD + j)) * T, T)]
                V(dve.tensor_tensor(x, ps[b], g(0), ALU.mult))
                d = V(dve.tensor_tensor(y, ps[b + 1], g(1), ALU.mult))
                p.wait(dve, d)
                d = V(dve.tensor_tensor(x, x, y, ALU.add))
                mhi, mlo = self.hhi[:, bass.ds((i * 4 + j) * T, T)], self.hlo[:, bass.ds((i * 4 + (LO_AT + j)) * T, T)]
                p.wait(act, d)
                d = A(act.copy(mhi, x))
                p.wait(dve, d)
                V(dve.tensor_tensor(mlo, x, mhi.bitcast(F32), ALU.subtract))
        W.finish(2)
        self.bank[0:4] = [[Done(p.ACT, p.ACT.count, False), Done(p.DVE, p.DVE.count, False)]] * 4
        self.into_stream(a["proj_out"], 2, 4, 1, KD, self.hhi, self.hlo[:, LO_AT * T:], 1.0, None)

    def embed(self):
        p, nc, a = self.p, self.nc, self.a
        pe, act, dve = nc.tensor, nc.scalar, nc.vector
        A, V = p.ACT.mark, p.DVE.mark
        W, ps = self.w, self.ps
        self.settle(act)
        landed = nc.alloc_semaphore("p_loaded")
        at = self.big[:, 30 * T:32 * T]
        act.dma_start(at, a["p"]).then_inc(landed, 16)
        act.wait_ge(landed, 16)
        dve.wait_ge(landed, 16)
        pairs = []
        for k in range(2):
            pairs += self.split_pair(at[:, k * T:(k + 1) * T], self.tile(self.hhi, k), self.tile(self.hlo, k), None)
        self.stream_norm(lambda k: self.par("ple_norm", k))
        self.settle(act, dve)
        g, t = self.sc[1:3], self.sc[3:5]
        p.wait(pe, pairs, self.bank[0:4], *self.u_ready)
        W.begin()
        with p.loop(2, act=4, dve=8, split=8, used=4) as i:
            for j in range(4):
                before = (p.DVE.ahead(2 * (j - 1)), 0) if j > 1 else (p.DVE.ahead(2 * (j + 3)), 1)
                hi, lo, split = W.chunk(a["embed"][i * 4 + j])
                p.wait(pe, split)
                p.wait(pe, before[0], back=before[1])
                b = 2 * (j % 2)
                for k in range(KD):
                    self.mm3(ps[b], hi, lo, slice(k * P, (k + 1) * P), self.tile(self.uhi, k), self.tile(self.ulo, k), k == 0, k == KD - 1)
                for k in range(2):
                    m = self.mm3(ps[b + 1], hi, lo, slice((KD + k) * P, (KD + k + 1) * P), self.tile(self.hhi, k), self.tile(self.hlo, k),
                                 k == 0, k == 1)
                product = W.used.mark(m)
                p.wait(act, product)
                p.wait(act, before[0], back=before[1])
                d = A(act.activation(g[j % 2][:, :], ps[b], ACT.Sigmoid))
                p.wait(dve, d)
                p.wait(dve, before[0], back=before[1])
                d = V(dve.tensor_tensor(t[j % 2][:, :], g[j % 2][:, :], ps[b + 1], ALU.mult))
                p.wait(dve, d)
                x = self.x[:, bass.ds((i * 4 + j) * T, T)]
                V(dve.tensor_tensor(x, x, t[j % 2][:, :], ALU.add))
        W.finish(2)


    def causal_product(self, b0, lhs, rhs, ready):
        p, pe = self.p, self.nc.tensor
        p.wait(pe, ready, self.bank[b0:b0 + 3])
        for (i, t0, n, c) in CAUSAL:
            m = pe.matmul(self.psum[:, b0 * T + c:b0 * T + c + n], lhs(i), rhs(t0, n), start=True, stop=True)
        d = p.PE.mark(m)
        self.bank[b0:b0 + 3] = [d] * 3
        return d

    def mask_diagonals(self, x, mask):
        x3 = x[:, 0:T].rearrange("p (i t) -> p i t", t=P)
        m3 = self.cst(mask).unsqueeze(1).broadcast_to([P, NT, P])
        return self.p.DVE.mark(self.nc.vector.tensor_tensor(x3, x3, m3, ALU.mult))

    def causal_values(self, out, v, w):
        blocks = sorted(CAUSAL, key=lambda x: (x[0], x[1]))
        for n, (i, t0, width, c) in enumerate(blocks):
            m = self.nc.tensor.matmul(out[:, t0:t0 + width], v(i), w[:, c:c + width], start=n == 0, stop=n == len(blocks) - 1,
                                      skip_group_check=True)
        return m

    def col(self, i):
        return self.ps[4][:, i:i + 1]

    def settle(self, *engines):
        p = self.p
        for e in engines:
            p.wait(e, [Done(line, line.count, False) for line in (p.PE, p.ACT, p.DVE, p.W.used)])


def block_program(nc, a, out, upto=99):
    b = Build(nc, a, out)
    b.load()
    b.first_sums()
    par = lambda name, first=0: (lambda k: b.par(name, first + k))
    b.ffn(a["ffn1_in"], a["ffn1_out"], par("norm_pre", 0), par("norm_post", 0))
    if upto == "f1":
        return b.store()
    b.gated_mixer()
    if upto == "m1":
        return b.store()
    b.y_tiles = b.y
    b.ffn(a["ffn2_in"], a["ffn2_out"], par("norm_pre", 2 * KD), par("norm_post", 2 * KD))
    if upto == "f2":
        return b.store()
    b.ffn(a["ffn3_in"], a["ffn3_out"], par("ffn1_norm"), None)
    if upto == "f3":
        return b.store()
    b.attention_mixer()
    if upto == "m2":
        return b.store()
    b.ffn(a["ffn4_in"], a["ffn4_out"], par("ffn2_norm"), None)
    if upto == "f4":
        return b.store()
    b.embed()
    b.store()


def lhs_tiles(w, cols=None):
    k, n = w.shape
    cols = cols or P
    return np.ascontiguousarray(w.reshape(k // P, P, n // cols, cols).transpose(2, 1, 0, 3)).reshape(n // cols, P, -1)


def columns(v):
    return np.ascontiguousarray(v.reshape(-1, P).T)


def ffn_in(w):
    t = lhs_tiles(w)
    return np.ascontiguousarray(t.reshape(2, KF, P, -1).transpose(1, 0, 2, 3)).reshape(2 * KF, P, -1)


def ffn_out(w):
    t = lhs_tiles(w)
    return np.ascontiguousarray(t.reshape(KD, P, 2, SLOT).transpose(0, 2, 1, 3)).reshape(2 * KD, P, SLOT)


def mix_in(w):
    n = w.shape[1] - 2 * HEADS
    gates = np.concatenate([w[:, n:n + HEADS], w[:, 0:32 - HEADS], w[:, n + HEADS:], w[:, 0:P - 32 - HEADS]], axis=1)
    return lhs_tiles(np.concatenate([w[:, :n], gates], axis=1))


def proj_in(w):
    n = KCQ * P + KCKV * P
    rope = np.concatenate([w[:, 0:NOPE], w[:, n:n + ROPE], w[:, 0:P - QK]], axis=1)
    return lhs_tiles(np.concatenate([w[:, :n], rope, w[:, n + ROPE:]], axis=1))


def head_tiles(w, cols):
    t = lhs_tiles(w, cols)
    return np.ascontiguousarray(t.reshape(2, 4, P, -1).transpose(0, 2, 1, 3)).reshape(2, P, -1)


def constants():
    c = np.zeros((P, N_CONST), np.float32)
    s, t = np.arange(P)[:, None], np.arange(P)[None, :]
    c[:, C_ID:C_ID + P] = s == t
    c[:, C_ONE:C_ONE + P] = 1
    c[:, C_LE:C_LE + P] = s <= t
    c[:, C_LT:C_LT + P] = s < t
    c[:, C_NSUF:C_NSUF + P] = -1.0 * (s >= t)
    c[:, C_NONE:C_NONE + P] = -1
    c[:, C_NGT:C_NGT + P] = NEVER * (t > s)
    c[:, C_NGE:C_NGE + P] = NEVER * (s >= t)
    for n, h in enumerate(LEVELS):
        c[:, C_LEVEL + n * P:C_LEVEL + (n + 1) * P] = (s // (2 * h) == t // (2 * h)) & (s % (2 * h) < h) & (t % (2 * h) >= h)
    c[:, C_RESET:C_RESET + T] = np.arange(T) % CH != 0
    for h in range(HEADS):
        c[h, C_SEL + h * P:C_SEL + (h + 1) * P] = 1
    r = np.arange(ROPE // 2)
    c[NOPE + ROPE // 2 + r, C_ROT + r] = -1
    c[NOPE + r, C_ROT + ROPE // 2 + r] = 1
    freq = (10000.0 ** (-(2.0 * r) / ROPE)).astype(np.float32)
    c[NOPE:QK, C_FREQ] = np.concatenate([freq, freq])
    return c


def layout(i):
    f = {k: np.asarray(v) for k, v in i.items()}
    pieces = {
        "norm_pre": columns(f["norm_pre"]), "norm_post": columns(f["norm_post"]),
        "conv_w": columns(f["conv_w"]), "conv_b": columns(f["conv_b"]), "lb": columns(f["hgrn_lb_logits"]),
        "hgrn_norm": columns(f["hgrn_norm"]), "mlstm_norm": columns(f["mlstm_norm"]),
        "ffn1_norm": columns(f["ffn1_norm_2"]), "mix_norm": columns(f["mix_norm_2"]),
        "q_latent": columns(f["q_latent_norm_2"]), "kv_latent": columns(f["kv_latent_norm_2"]),
        "ffn2_norm": columns(f["ffn2_norm_2"]), "ple_norm": columns(f["ple_norm_2"]),
    }
    return {
        "const": constants(),
        "param": np.concatenate([pieces[n] for n in PARAMS], axis=1),
        "x": np.ascontiguousarray(f["x"][0].T.reshape(KD, P, T).transpose(1, 0, 2)).reshape(P, KD * T),
        "ffn1_in": ffn_in(f["ffn1_w_in"][0]), "ffn1_out": ffn_out(f["ffn1_w_out"][0]),
        "mix_in": mix_in(f["w_mix_in"][0]), "mix_out": lhs_tiles(f["w_mix_out"][0]),
        "gate_bias": np.ascontiguousarray(f["mlstm_gate_bias"].reshape(2, HEADS).T),
        "ffn2_in": ffn_in(f["ffn2_w_in"][0]), "ffn2_out": ffn_out(f["ffn2_w_out"][0]),
        "ffn3_in": ffn_in(f["ffn1_w_in_2"][0]), "ffn3_out": ffn_out(f["ffn1_w_out_2"][0]),
        "proj_in": proj_in(f["w_in_2"][0]),
        "q_up": head_tiles(f["w_q_up_2"][0], QK), "kv_up": head_tiles(f["w_kv_up_2"][0], NOPE + HV),
        "head_gains": np.concatenate([f["q_head_norm_2"], f["k_head_norm_2"]]).T.copy(),
        "positions": f["positions_2"],
        "branch": np.concatenate([lhs_tiles(f["w_branch_mla_2"][0]), lhs_tiles(f["w_branch_sb_2"][0])], axis=2),
        "proj_out": lhs_tiles(f["w_out_2"][0]),
        "ffn4_in": ffn_in(f["ffn2_w_in_2"][0]), "ffn4_out": ffn_out(f["ffn2_w_out_2"][0]),
        "embed": np.concatenate([lhs_tiles(f["w_ple_gate_2"][0]), lhs_tiles(f["w_ple_proj_2"][0])], axis=2),
        "p": np.ascontiguousarray(f["p_2"][0, 0].T.reshape(2, P, T).transpose(1, 0, 2)).reshape(P, 2 * T),
    }


def kernel(**inputs):
    import concourse.bacc as bacc
    from concourse.bass_utils import run_bass_kernel_spmd

    nc = bacc.Bacc("TRN2", target_bir_lowering=False, num_devices=1)
    arrays = layout(inputs)
    aps = {n: nc.dram_tensor(f"in_{n}", v.shape, mybir.dt.from_np(v.dtype), kind="ExternalInput").ap() for n, v in arrays.items()}
    out = nc.dram_tensor("out", (P, KD * T), F32, kind="ExternalOutput").ap()
    block_program(nc, aps, out)
    r = run_bass_kernel_spmd(nc, [{f"in_{n}": v for n, v in arrays.items()}], core_ids=[0])
    y = r.results[0]["out"]
    return np.ascontiguousarray(y.reshape(P, KD, T).transpose(2, 1, 0)).reshape(1, T, D)
```

```python
from contextlib import ExitStack

import numpy as np
import concourse.bass as bass
from concourse import mybir
from concourse.alu_op_type import AluOpType as ALU

F32 = mybir.dt.float32
F32R = mybir.dt.float32r
I32 = mybir.dt.int32
U32 = mybir.dt.uint32
BF16 = mybir.dt.bfloat16
ACT = mybir.ActivationFunctionType
AX = mybir.AxisListType

P = 128
T = 512
NT = T // P
D = 1024
KD = D // P
DFF = 2816
KF = DFF // P
EPS = 1e-6

HEADS = 4
DK = 128
CH = 64
NC = T // CH
ML_QK = 64
CONV = 4

AH = 8
NOPE, ROPE, QK, HV = 64, 32, 96, 64
KCQ, KCKV = 3, 2

HALF = KF // 2
SLOT = HALF * P
RAW, PAIR = 4, 2
NEVER = -1e30

C_ID, C_ONE, C_LE, C_LT, C_NSUF, C_NONE, C_NGT, C_NGE, C_LEVEL = (i * P for i in range(9))
LEVELS = (1, 2, 4, 8, 16, 32)
C_RESET = C_LEVEL + len(LEVELS) * P
C_SEL = C_RESET + T
C_ROT = C_SEL + HEADS * P
C_FREQ = C_ROT + ROPE
N_CONST = C_FREQ + 1

PARAMS = {}
_n = 0
for _name, _w in (("norm_pre", 3 * KD), ("norm_post", 3 * KD), ("conv_w", CONV * HEADS), ("conv_b", HEADS),
                  ("lb", 2 * HEADS), ("hgrn_norm", HEADS), ("mlstm_norm", HEADS), ("ffn1_norm", KD),
                  ("mix_norm", KD), ("q_latent", KCQ), ("kv_latent", KCKV), ("ffn2_norm", KD), ("ple_norm", KD)):
    PARAMS[_name] = _n
    _n += _w
N_PARAM = _n


CAUSAL = [(i, i * P, P, i * P) for i in range(NT)] + [(0, P, 3 * P, T), (2, 3 * P, P, T + 3 * P), (1, 2 * P, 2 * P, 2 * T)]
N_CAUSAL = 2 * T + 2 * P


def causal_column(i, j):
    if i == j:
        return i * P
    return next(c + j * P - t0 for (n, t0, w, c) in CAUSAL[NT:] if n == i)


SUMMED = [(T, P, 0, 1), (T + P, 2 * T, P, 2), (T + P, 2 * P, T + P, 2), (T + 2 * P, 3 * P, 0, 2),
          (2 * T, 2 * P, T + P, 2), (2 * T + P, 3 * P, 0, 1)]

ROWS = [(3, 0), (2, T), (0, T + 3 * P), (1, 2 * T)]
GATE_AT = 18
LO_AT = 12


def ds(at, n):
    return slice(at, at + n) if isinstance(at, int) else bass.ds(at, n)


class Done:

    def __init__(self, line, count, looped):
        self.line, self.count, self.looped = line, count, looped


class Line:

    def __init__(self, nc, name, credit=0):
        self.sem = nc.alloc_semaphore(name)
        self.count = credit
        self.per = None
        self.turn = None

    def mark(self, ins):
        ins.then_inc(self.sem, 1)
        self.count += 1
        return Done(self, self.count, self.per is not None)

    def ahead(self, k):
        return Done(self, self.start + k, self.per is not None)


class Program:

    def __init__(self, nc):
        self.nc = nc
        self.pe, self.act, self.dve, self.pool = nc.tensor, nc.scalar, nc.vector, nc.gpsimd
        credit = 64
        self.PE, self.ACT, self.DVE = (Line(nc, n, credit) for n in ("pe_done", "act_done", "dve_done"))
        for e, line in ((self.pe, self.PE), (self.act, self.ACT), (self.dve, self.DVE)):
            e.sem_inc(line.sem, credit)
        self.POOL = Line(nc, "pool_done")
        self.lines = [self.PE, self.ACT, self.DVE, self.POOL]
        self.once = False
        self.known = {}

    def wait(self, eng, *dones, back=0):
        if back and self.once:
            return
        most = {}
        queue = list(dones)
        while queue:
            d = queue.pop()
            if isinstance(d, (list, tuple)):
                queue += d
            elif d is not None:
                most[(d.line, d.looped)] = max(most.get((d.line, d.looped), 0), d.count)
        for (line, looped), count in most.items():
            if looped and line.per is not None:
                assert count - back * line.per >= 0
                eng.wait_ge(line.sem, line.turn * line.per + (count - back * line.per))
            else:
                key = (id(eng), line)
                if self.known.get(key, -1) >= count:
                    continue
                eng.wait_ge(line.sem, count)
                if line.per is None:
                    self.known[key] = count

    def loop(self, times, **per):
        return Loop(self, times, per)

    def turns(self, n, body, **per):
        self.once = True
        for line in self.lines:
            line.start = line.count
        body(0)
        self.once = False
        for name, count in per.items():
            line = named_line(self, name)
            assert line.count - line.start == count, (name, line.count - line.start, count)
        self.W.begin()
        with self.loop(n - 1, **per) as i:
            body(i + 1)
        self.W.finish(n - 1)


class Loop:

    def __init__(self, prog, times, per):
        self.prog, self.times = prog, times
        self.per = {named_line(prog, k): v for k, v in per.items()}

    def __enter__(self):
        self.fori = self.prog.nc.Fori(0, self.times)
        i = self.fori.__enter__()
        for line in self.prog.lines:
            line.start, line.per, line.turn = line.count, self.per.get(line, 0), i
        return i

    def __exit__(self, *exc):
        self.fori.__exit__(*exc)
        for line in self.prog.lines:
            assert exc[0] or line.count - line.start == line.per, (line.count - line.start, line.per)
            line.count = line.start + self.times * line.per
            line.per = line.turn = None


def named_line(prog, name):
    return {"pe": prog.PE, "act": prog.ACT, "dve": prog.DVE, "split": prog.W.split, "used": prog.W.used}[name]


class Weights:

    def __init__(self, prog, at):
        nc = self.nc = prog.nc
        self.p = prog
        self.raw, self.hi, self.lo = [], [], []
        for s in range(RAW):
            self.raw.append(nc.alloc_sbuf_tensor_at(f"w_raw{s}", [P, SLOT], F32, offset=at))
            at += SLOT * 4
        for s in range(PAIR):
            self.hi.append(nc.alloc_sbuf_tensor_at(f"w_hi{s}", [P, SLOT], F32R, offset=at))
            self.lo.append(nc.alloc_sbuf_tensor_at(f"w_lo{s}", [P, SLOT], F32R, offset=at + SLOT * 4))
            at += SLOT * 8
        self.end = at
        self.passed = nc.alloc_semaphore("w_passed")
        self.landed = [nc.alloc_semaphore(f"w_landed{s}") for s in range(RAW)]
        self.n = RAW
        self.split = Line(nc, "w_split", 2 * RAW)
        self.used = Line(nc, "w_used", RAW)
        nc.gpsimd.sem_inc(self.split.sem, 2 * RAW)
        nc.tensor.sem_inc(self.used.sem, RAW)
        prog.lines += [self.split, self.used]
        prog.W = self

    def chunk(self, src, rows=P):
        p, nc, cols = self.p, self.nc, src.shape[-1]
        n = self.n
        r, s = n % RAW, n % PAIR
        looped = self.split.per is not None
        p.wait(nc.sync, Done(self.split, 2 * (n - RAW + 1), looped))
        nc.sync.dma_start(self.raw[r][0:rows, 0:cols], src).then_inc(self.landed[r], 16)
        landed = 16 * (n // RAW)
        if looped:
            nc.gpsimd.wait_ge(self.landed[r], self.split.turn * (16 * self.split.per // (2 * RAW)) + landed)
        else:
            nc.gpsimd.wait_ge(self.landed[r], landed)
        p.wait(nc.gpsimd, Done(self.used, n - PAIR + 1, looped))
        if looped:
            nc.gpsimd.sem_inc(self.passed, 1)
        raw, hi, lo = self.raw[r][0:rows, 0:cols], self.hi[s][0:rows, 0:cols], self.lo[s][0:rows, 0:cols]
        rounded = self.split.mark(nc.gpsimd.tensor_scalar(hi, raw, 1.0, 1.0, ALU.mult, ALU.mult))
        p.wait(nc.gpsimd, rounded)
        rest = self.split.mark(nc.gpsimd.tensor_tensor(lo, raw, hi.bitcast(F32), ALU.subtract))
        self.n += 1
        return self.hi[s], self.lo[s], rest

    def begin(self):
        self.first = self.n

    def finish(self, times):
        body = self.n - self.first
        assert body % RAW == 0
        self.n = self.first + body * times
        assert self.split.count == 2 * self.n and self.used.count == self.n


class Build:
    def __init__(self, nc, a, out, upto=99):
        self.nc, self.a = nc, a
        self.out = out
        p = self.p = Program(nc)
        at = nc.sbuf_base
        at = (at + 63) // 64 * 64
        self.map_start = at

        def place(name, cols, dt, offset):
            return nc.alloc_sbuf_tensor_at(name, [P, cols], dt, offset=offset)

        self.const = place("const", N_CONST, F32, at); at += N_CONST * 4 + (-N_CONST * 4) % 64
        self.param = place("param", N_PARAM, F32, at); at += N_PARAM * 4 + (-N_PARAM * 4) % 64
        self.misc = place("misc", 256, F32, at); at += 1024
        self.x = place("x", KD * T, F32, at); at += KD * T * 4
        self.w = Weights(p, at)
        at = self.w.end
        self.sums_at = at + 6 * T * 4
        self.sc = []
        for i in range(7):
            self.sc.append(place(f"scratch{i}", T, F32, at)); at += T * 4
        self.scf = place("scratch_f32", 7 * T, F32, at - 7 * T * 4)
        self.uhi = place("u_hi", KD * T, F32R, at)
        self.ulo = place("u_lo", KD * T, F32R, at + KD * T * 4)
        self.y = place("y", KD * T, F32, at)
        self.uf = place("u_f32", 2 * KD * T, F32, at)
        at += 2 * KD * T * 4
        self.big_at = at
        self.hhi = place("hidden_hi", KF * T, F32R, at)
        self.hlo = place("hidden_lo", KF * T, F32R, at + KF * T * 4)
        self.big = place("work", 2 * KF * T, F32, at)
        at += 2 * KF * T * 4
        self.map_end = at
        self.sums_lhs = place("sums_lhs", 2 * P, F32R, self.sums_at)
        self.psum = nc.alloc_psum_tensor("psum", [P, 8 * T], F32)
        self.ps = [self.psum[:, b * T:(b + 1) * T] for b in range(8)]
        self.bank = [None] * 8
        self.spread_used = [None, None]
        self.y_tiles = self.y
        self.vt = [self.tile(self.big, n) for n in (4, 5)]

    def store(self):
        p, nc = self.p, self.nc
        self.settle(nc.sync)
        stored = nc.alloc_semaphore("stored")
        nc.sync.dma_start(self.out, self.x[:, :]).then_inc(stored, 16)
        nc.sync.wait_ge(stored, 16)

    def cst(self, c, n=P, rows=slice(0, P)):
        return self.const[rows, c:c + n]

    def par(self, name, k, rows=slice(0, P)):
        c = PARAMS[name] + k
        return self.param[rows, c:c + 1]


    def load(self):
        nc, p, a = self.nc, self.p, self.a
        first = nc.alloc_semaphore("first_constants_loaded")
        self.consts_landed = nc.alloc_semaphore("constants_loaded")
        self.x_landed = [nc.alloc_semaphore(f"x{k}_loaded") for k in range(KD)]
        nc.scalar.dma_start(self.const[:, 0:2 * P], a["const"][:, 0:2 * P]).then_inc(first, 16)
        nc.scalar.dma_start(self.param[:, :], a["param"]).then_inc(first, 16)
        for k in range(KD):
            nc.scalar.dma_start(self.tile(self.x, k), a["x"][:, k * T:(k + 1) * T]).then_inc(self.x_landed[k], 16)
        nc.scalar.dma_start(self.const[:, 2 * P:], a["const"][:, 2 * P:]).then_inc(self.consts_landed, 16)
        for e in (nc.tensor, nc.vector, nc.scalar):
            e.wait_ge(first, 32)

    def mm3(self, out, hi, lo, cols, xhi, xlo, first, last):
        pe = self.nc.tensor
        pe.matmul(out, hi[:, cols], xhi, start=first, stop=False)
        pe.matmul(out, lo[:, cols], xhi, start=False, stop=False)
        return pe.matmul(out, hi[:, cols], xlo, start=False, stop=last)

    def token_sums(self, sq, ready, out, rows=P, first_wait=None):
        p, pe = self.p, self.nc.tensor
        p.wait(pe, ready, first_wait)
        for i in range(NT):
            m = pe.matmul(out(i), sq[0:rows, i * P:(i + 1) * P], self.cst(C_ONE, 1, slice(0, rows)), start=True, stop=True)
        return p.PE.mark(m)

    def rsqrt(self, src, dst, ready, n, factor=1.0):
        p, nc = self.p, self.nc
        f = 1.0 / (factor * factor)
        p.wait(nc.vector, ready)
        d = p.DVE.mark(nc.vector.tensor_scalar(dst, src, f / n, f * EPS, ALU.mult, ALU.add))
        p.wait(nc.scalar, d)
        d = p.ACT.mark(nc.scalar.activation(dst, dst, ACT.Sqrt))
        p.wait(nc.vector, d)
        return p.DVE.mark(nc.vector.reciprocal(dst, dst))

    def spread(self, cols, ready, diag, diag_free, bank, rows=P):
        p, nc = self.p, self.nc
        p.wait(nc.vector, ready, diag_free)
        d3 = diag[:, :].rearrange("p (i t) -> p i t", i=NT)
        ident = self.cst(C_ID).unsqueeze(1).broadcast_to([P, NT, P])
        d = p.DVE.mark(nc.vector.tensor_tensor(d3, ident, cols.unsqueeze(2).broadcast_to([P, NT, P]), ALU.mult))
        p.wait(nc.tensor, d, self.bank[bank])
        m = nc.tensor.matmul(self.ps[bank][0:rows, :], self.cst(C_ONE, rows), diag[:, :], start=True, stop=True)
        self.bank[bank] = p.PE.mark(m)
        return self.bank[bank]

    def tile(self, t, k):
        return t[:, k * T:(k + 1) * T]

    def pair_tile(self, k, gain, ready, at=None):
        p, nc = self.p, self.nc
        at = slice(k * T, (k + 1) * T) if at is None else at
        hi, lo, x = self.uhi[:, at], self.ulo[:, at], self.x[:, at]
        p.wait(nc.scalar, ready)
        h = p.ACT.mark(nc.scalar.activation(hi, x, ACT.Copy, scale=gain))
        p.wait(nc.vector, h, ready)
        l = p.DVE.mark(nc.vector.scalar_tensor_tensor(out=lo, in0=x, scalar=gain, in1=hi.bitcast(F32), op0=ALU.mult,
                                                      op1=ALU.subtract))
        return [h, l]

    def from_stream(self, gain):
        def landed(k):
            for e in (self.nc.scalar, self.nc.vector):
                e.wait_ge(self.x_landed[k], 16)
        self.produce_with(landed, gain)

    def produce_with(self, update, gain):
        p, nc = self.p, self.nc
        rounded = {}

        def front(k):
            ready = update(k)
            at = slice(k * T, (k + 1) * T)
            p.wait(nc.scalar, ready)
            h = p.ACT.mark(nc.scalar.activation(self.uhi[:, at], self.x[:, at], ACT.Copy, scale=gain(k)))
            rounded[k] = h, ready

        def produce(k):
            if k == 0:
                front(0)
            if k + 1 < KD:
                front(k + 1)
            h, ready = rounded[k]
            at = slice(k * T, (k + 1) * T)
            p.wait(nc.vector, h, ready)
            l = p.DVE.mark(nc.vector.scalar_tensor_tensor(out=self.ulo[:, at], in0=self.x[:, at], scalar=gain(k),
                                                          in1=self.uhi[:, at].bitcast(F32), op0=ALU.mult, op1=ALU.subtract))
            return self.squared(k, ready), [h, l]
        self.produce, self.sq_used = produce, [None, None]

    def squared(self, k, ready):
        p, nc = self.p, self.nc
        sq = self.sc[4 + k % 2]
        p.wait(nc.scalar, ready, self.sq_used[k % 2])
        return sq, p.ACT.mark(nc.scalar.activation(sq[:, :], self.tile(self.x, k), ACT.Square))

    def first_chunk(self, bank, hi, lo, last=True):
        p = self.p
        for k in range(KD):
            if self.produce:
                (sq, squared), ready = self.produce(k)
                p.wait(self.nc.tensor, ready)
            m = self.mm3(bank, hi, lo, slice(k * P, (k + 1) * P), self.tile(self.uhi, k), self.tile(self.ulo, k), k == 0, k == KD - 1)
            if k == KD - 1:
                d = self.w.used.mark(m) if last else None
            if self.produce:
                p.wait(self.nc.tensor, squared, self.bank[4])
                self.sums = self.sq_used[k % 2] = p.PE.mark(
                    self.nc.tensor.matmul(self.ps[4], self.cst(C_ONE), sq[:, :], start=k == 0, stop=k == KD - 1))
        return d

    def factor(self):
        p, nc = self.p, self.nc
        act, dve = nc.scalar, nc.vector
        self.settle(dve)
        self.rb = self.sc[0][:, :]
        if self.produce:
            self.settle(act)
            self.bank[4] = self.rsqrt(self.ps[4], self.rb, self.sums, D)
        else:
            r = self.misc[:, NT:2 * NT]
            d = self.rsqrt(self.ps[4][:, 0:NT], r, self.sums, D)
            self.bank[4] = d
            rb = self.spread(r, d, self.sc[6], None, 5)
            p.wait(act, rb)
            self.bank[5] = p.ACT.mark(act.copy(self.rb, self.ps[5]))
        self.settle(act, dve)
        self.produce = None

    def square_sums(self, k, ready, src, sq, sq_free, wait_bank=None):
        p, nc = self.p, self.nc
        p.wait(nc.scalar, ready, sq_free)
        d = p.ACT.mark(nc.scalar.activation(sq[:, :], src, ACT.Square))
        return self.token_sums(sq, [d], lambda i: self.ps[4][:, k * NT + i:k * NT + i + 1], first_wait=wait_bank)


    def ffn(self, w_in, w_out, post, next_gain):
        p, nc = self.p, self.nc
        pe, act, dve = nc.tensor, nc.scalar, nc.vector
        ps, W = self.ps, self.w
        sg, hm = self.sc[1:3], self.sc[3:5]
        p.wait(pe, self.bank[0:4])

        def turn(i):
            for j in range(2):
                for half in range(2):
                    b = 2 * j + half
                    hi, lo, ready = W.chunk(w_in[i * 4 + b])
                    p.wait(pe, ready)
                    if p.once and b == 0:
                        product = self.first_chunk(ps[b], hi, lo)
                        self.factor()
                        for line in (p.ACT, p.DVE):
                            line.start = line.count
                    else:
                        p.wait(pe, p.DVE.ahead(4 * j + 1 + half), back=1)
                        for k in range(KD):
                            m = self.mm3(ps[b], hi, lo, slice(k * P, (k + 1) * P), self.tile(self.uhi, k),
                                         self.tile(self.ulo, k), k == 0, k == KD - 1)
                        product = W.used.mark(m)
                    to = (sg, hm)[half][j][:, :]
                    p.wait(dve, product)
                    if half == 0:
                        p.wait(dve, p.DVE.ahead(4 * j + 3), back=1)
                    else:
                        p.wait(dve, p.ACT.ahead(2 * j + 2), p.DVE.ahead(4 * j + 4), back=1)
                    normed = p.DVE.mark(dve.tensor_tensor(to, ps[b], self.rb, ALU.mult))
                    if half == 0:
                        p.wait(act, normed)
                        p.ACT.mark(act.activation(to, to, ACT.Silu))
                p.wait(dve, normed, p.ACT.ahead(2 * j + 1))
                d = p.DVE.mark(dve.tensor_tensor(hm[j][:, :], hm[j][:, :], sg[j][:, :], ALU.mult))
                at = ds((i * 2 + j) * T, T)
                p.wait(act, d)
                d = p.ACT.mark(act.copy(self.hhi[:, at], hm[j][:, :]))
                p.wait(dve, d)
                p.DVE.mark(dve.tensor_tensor(self.hlo[:, at], hm[j][:, :], self.hhi[:, at].bitcast(F32), ALU.subtract))

        p.turns(KF // 2, turn, act=4, dve=8, split=8, used=4)
        self.into_stream(w_out, KD // 2, 2, 2, HALF, self.hhi, self.hlo, 0.5, post, next_gain)

    def into_stream(self, w, turns, n_tiles, n_chunks, lhs, xhi, xlo, scale, post, next_gain):
        p, nc = self.p, self.nc
        pe, act, dve = nc.tensor, nc.scalar, nc.vector
        ps, W = self.ps, self.w
        acc, sq = self.sc[5], self.sc[6]
        self.settle(pe, act, dve)
        zeroed = p.DVE.mark(dve.memset(acc[:, :], 0.0))
        p.wait(act, zeroed)
        rooted = p.ACT.mark(act.activation(acc[:, 0:1], acc[:, 0:1], ACT.Sqrt))
        p.wait(dve, zeroed, rooted)
        W.begin()
        per = n_tiles * n_chunks
        na, nd = (1, 2) if post else (2, 3)
        with p.loop(turns, act=na * n_tiles, dve=nd * n_tiles, split=2 * per, used=per) as i:
            for j in range(n_tiles):
                out_done = p.DVE.ahead(nd * j + 1)
                for part in range(n_chunks):
                    hi, lo, ready = W.chunk(w[i * per + (n_chunks * j + part)])
                    p.wait(pe, ready)
                    if part == 0:
                        p.wait(pe, out_done, back=1)
                    for k in range(lhs):
                        kk = part * lhs + k
                        m = self.mm3(ps[j], hi, lo, slice(k * P, (k + 1) * P), self.tile(xhi, kk), self.tile(xlo, kk),
                                     kk == 0, kk == n_chunks * lhs - 1)
                    product = W.used.mark(m)
                at = ds((i * n_tiles + j) * T, T)
                p.wait(dve, product)
                if post:
                    to = self.y_tiles[:, at]
                    p.DVE.mark(dve.tensor_copy(to, ps[j]))
                else:
                    to = self.x[:, at]
                    p.DVE.mark(dve.scalar_tensor_tensor(out=to, in0=ps[j], scalar=scale, in1=to, op0=ALU.mult, op1=ALU.add))
                before = (p.DVE.ahead(nd * (n_tiles - 1) + 2), 1) if j == 0 else (p.DVE.ahead(nd * (j - 1) + 2), 0)
                p.wait(act, before[0], back=before[1])
                p.wait(act, out_done)
                squared = p.ACT.mark(act.activation(sq[:, :], to, ACT.Square))
                p.wait(dve, before[0], back=before[1])
                p.wait(dve, squared)
                p.DVE.mark(dve.tensor_tensor(acc[:, :], acc[:, :], sq[:, :], ALU.add))
                if not post:
                    self.pair_tile(None, self.gain_at(next_gain, i * n_tiles + j), out_done, at=at)
        W.finish(turns)
        done = [Done(p.ACT, p.ACT.count, False), Done(p.DVE, p.DVE.count, False)]
        self.bank[0:4] = [done] * 4
        self.sums = self.token_sums(acc, done, self.col, first_wait=self.bank[4])
        self.produce = None
        if post:
            self.post_norm(post, scale, next_gain)

    def gain_at(self, name, k):
        name, first = name
        return self.param[:, ds(k + (PARAMS[name] + first), 1)]

    def post_norm(self, gain, factor, next_gain):
        p, nc = self.p, self.nc
        act, dve = nc.scalar, nc.vector
        r = self.misc[:, NT:2 * NT]
        self.settle(dve, act)
        s, d = self.ps[4][:, 0:NT], self.sums
        d = self.rsqrt(s, r, d, D, factor)
        self.bank[4] = d
        rb = self.spread(r, d, self.sc[6], None, 5)
        p.wait(dve, rb)
        y_tiles = self.y_tiles
        free = [None] * 2

        def update(k):
            t = self.sc[1 + k % 2]
            p.wait(dve, free[k % 2])
            d = p.DVE.mark(dve.scalar_tensor_tensor(out=t[:, :], in0=self.tile(y_tiles, k), scalar=gain(k),
                                                    in1=self.ps[5], op0=ALU.mult, op1=ALU.mult))
            self.bank[5] = d
            p.wait(nc.gpsimd, d)
            free[k % 2] = p.POOL.mark(nc.gpsimd.tensor_tensor(self.tile(self.x, k), self.tile(self.x, k), t[:, :], ALU.add))
            return free[k % 2]
        self.produce_with(update, lambda k: self.gain_at(next_gain, k))

    def settle(self, *engines):
        p = self.p
        for e in engines:
            p.wait(e, [Done(line, line.count, False) for line in (p.PE, p.ACT, p.DVE, p.W.used)])


    def project(self, w, first, turns, dst, func=None):
        p, nc = self.p, self.nc
        pe, act, dve = nc.tensor, nc.scalar, nc.vector
        W, ps = self.w, self.ps
        p.wait(pe, self.bank[0:4])

        def turn(i):
            for j in range(4):
                hi, lo, ready = W.chunk(w[i * 4 + (first + j)])
                p.wait(pe, ready)
                if p.once and j == 0 and self.fresh:
                    product = self.first_chunk(ps[j], hi, lo)
                    self.factor()
                    self.fresh = False
                    for line in (p.ACT, p.DVE):
                        line.start = line.count
                else:
                    p.wait(pe, p.DVE.ahead(j + 1), back=1)
                    for k in range(KD):
                        m = self.mm3(ps[j], hi, lo, slice(k * P, (k + 1) * P), self.tile(self.uhi, k),
                                     self.tile(self.ulo, k), k == 0, k == KD - 1)
                    product = W.used.mark(m)
                to = dst[:, ds((i * 4 + j) * T, T)]
                p.wait(dve, product)
                d = p.DVE.mark(dve.tensor_tensor(to, ps[j], self.rb, ALU.mult))
                if func:
                    p.wait(act, d)
                    p.ACT.mark(act.activation(to, to, func))

        p.turns(turns, turn, act=4 if func else 0, dve=4, split=8, used=4)
        self.bank[0:4] = [[Done(p.ACT, p.ACT.count, False), Done(p.DVE, p.DVE.count, False)]] * 4

    def one_chunk(self, src, bank, x_pair, tiles, cols=P, out=None, ready=None, off=0):
        p = self.p
        hi, lo, split = self.w.chunk(src)
        p.wait(self.nc.tensor, split, self.bank[bank], ready)
        out = self.ps[bank][0:cols, :] if out is None else out
        for k in range(tiles):
            m = self.mm3(out, hi, lo, slice(off + k * cols, off + (k + 1) * cols), x_pair[0](k), x_pair[1](k), k == 0, k == tiles - 1)
        d = self.w.used.mark(m)
        self.bank[bank] = d
        return d

    def split_pair(self, src, hi, lo, ready, eng=None):
        p, nc = self.p, self.nc
        p.wait(nc.scalar, ready)
        h = p.ACT.mark(nc.scalar.copy(hi, src))
        p.wait(nc.vector, h, ready)
        l = p.DVE.mark(nc.vector.tensor_tensor(lo, src, hi.bitcast(F32), ALU.subtract))
        return [h, l]

    def U(self, n):
        return self.uf[:, n * 4 * T:(n + 1) * 4 * T]

    def B(self, n):
        return self.big[:, n * 4 * T:(n + 1) * 4 * T]

    def turn_tiles(self, src, n, bank0, dst, ready, rows=slice(0, P), cols=P):
        p, nc = self.p, self.nc
        p.wait(nc.tensor, ready, self.bank[bank0:bank0 + (n * cols + T - 1) // T])
        base = bank0 * T
        for q in range(n):
            m = nc.tensor.transpose(self.psum[:, base + q * cols:base + (q + 1) * cols],
                                    src[rows, q * P:(q + 1) * P], self.const[rows, C_ID + rows.start:C_ID + rows.stop])
        d = p.PE.mark(m)
        p.wait(nc.scalar, d)
        d = p.ACT.mark(nc.scalar.copy(dst, self.psum[:, base:base + n * cols]))
        for b in range(bank0, bank0 + (n * cols + T - 1) // T):
            self.bank[b] = d
        return d


    def gated_mixer(self):
        p, nc, a = self.p, self.nc, self.a
        self.gate_bias = self.misc[0:HEADS, 128:130]
        biased = nc.alloc_semaphore("gate_bias_loaded")
        nc.scalar.dma_start(self.gate_bias, a["gate_bias"]).then_inc(biased, 16)
        nc.vector.wait_ge(biased, 16)
        for e in (nc.tensor, nc.vector, nc.scalar):
            e.wait_ge(self.consts_landed, 16)
        self.fresh = True
        self.project(a["mix_in"], 0, 2, self.big)
        self.settle(nc.scalar, nc.vector, nc.tensor)
        self.gate_rows = self.sc[5]
        tiles = list(range(8, 28))
        self.to_fill = [(n, self.tile(self.big, n)) for n in tiles]
        self.to_fill.insert(8, (28, self.gate_rows[:, :]))
        self.filled, self.in_psum, self.n_fill = {}, [], 0
        self.hgrn2()
        self.mlstm()
        self.settle(nc.scalar, nc.vector)
        self.u_ready = []
        self.y_tiles = self.big[:, 12 * T:(12 + KD) * T]
        for k in range(KD):
            src = self.B(0 if k < 4 else 2)[:, (k % 4) * T:(k % 4 + 1) * T]
            self.u_ready.append(self.split_pair(src, self.tile(self.uhi, k), self.tile(self.ulo, k), None))
        p.wait(nc.tensor, self.u_ready)
        self.into_stream(a["mix_out"], 2, 4, 1, KD, self.uhi, self.ulo, 1.0, lambda k: self.par("norm_post", KD + k),
                         ("norm_pre", 2 * KD))

    def fill(self, n):
        p, pe = self.p, self.nc.tensor
        for _ in range(n):
            index, to = self.to_fill[self.n_fill]
            b = 4 + self.n_fill % 4
            self.n_fill += 1
            self.leave_psum(3)
            hi, lo, split = self.w.chunk(self.a["mix_in"][index])
            p.wait(pe, split, self.bank[b])
            for k in range(KD):
                m = self.mm3(self.ps[b], hi, lo, slice(k * P, (k + 1) * P), self.tile(self.uhi, k), self.tile(self.ulo, k),
                             k == 0, k == KD - 1)
            self.in_psum.append((index, b, to, self.w.used.mark(m)))

    def leave_psum(self, keep):
        p, dve = self.p, self.nc.vector
        while len(self.in_psum) > keep:
            index, b, to, product = self.in_psum.pop(0)
            p.wait(dve, product)
            self.bank[b] = self.filled[index] = p.DVE.mark(dve.tensor_tensor(to, self.ps[b], self.rb, ALU.mult))

    def hgrn2(self):
        p, nc = self.p, self.nc
        pe, act, dve = nc.tensor, nc.scalar, nc.vector
        A, V, PE = p.ACT.mark, p.DVE.mark, p.PE.mark
        q, f, v_in, gate = self.B(0), self.B(1), self.B(2), self.B(3)
        logf, G = self.B(7), self.B(8)
        S = self.scf[:, T:5 * T]
        sig = A(act.activation(f, f, ACT.Sigmoid))
        q_done = A(act.activation(q, q, ACT.Silu))
        H = HEADS
        m = self.misc
        l0, l1 = (self.param[:, PARAMS["lb"] + H * k:PARAMS["lb"] + H * (k + 1)] for k in range(2))
        top, e, lb, rest = m[:, 32:36], m[:, 36:44], m[:, 44:48], m[:, 48:52]
        d = V(dve.tensor_tensor(top, l0, l1, ALU.max)); p.wait(dve, d)
        V(dve.tensor_tensor(e[:, 0:H], l0, top, ALU.subtract))
        d = V(dve.tensor_tensor(e[:, H:2 * H], l1, top, ALU.subtract)); p.wait(act, d)
        d = A(act.activation(e, e, ACT.Exp)); p.wait(dve, d)
        d = V(dve.tensor_tensor(lb, e[:, 0:H], e[:, H:2 * H], ALU.add)); p.wait(dve, d)
        d = V(dve.reciprocal(lb, lb)); p.wait(dve, d)
        d = V(dve.tensor_tensor(lb, lb, e[:, 0:H], ALU.mult)); p.wait(dve, d)
        d = V(dve.tensor_scalar(rest, lb, -1.0, 1.0, ALU.mult, ALU.add))
        self.fill(2)
        p.wait(dve, d, sig)
        for h in range(H):
            t = slice(h * T, (h + 1) * T)
            d = V(dve.tensor_scalar(logf[:, t], f[:, t], rest[:, h:h + 1], lb[:, h:h + 1], ALU.mult, ALU.add))
        p.wait(dve, d)
        k = f
        k_done = V(dve.tensor_scalar(k, logf, -1.0, 1.0, ALU.mult, ALU.add))
        p.wait(act, k_done)
        logf_done = A(act.activation(logf, logf, ACT.Ln))
        self.fill(1)
        work = (self.B(9), self.B(10), self.B(7))
        z = V(dve.memset(S, 0.0))
        p.wait(dve, q_done, k_done)
        multiplied = {0: V(dve.tensor_tensor(work[0], q, k, ALU.mult))}
        p.wait(dve, logf_done)
        for h in range(H):
            t = slice(h * T, (h + 1) * T)
            G_done = V(dve.tensor_tensor_scan(G[:, t], self.cst(C_RESET, T), logf[:, t], 0.0, ALU.mult, ALU.add))
        p.wait(dve, G_done, z)
        self.leave_psum(1)
        self.fill(2)
        exps, scored, copied = {}, {}, {}
        last = len(LEVELS)
        G3 = G.rearrange("p (c t) -> p c t", t=CH)
        e_end = m[:, 64:64 + H * NC]

        def cut(x, half):
            return x.rearrange("p (c two h) -> p c two h", two=2, h=half)

        def exponents(n):
            w = work[n % 3]
            p.wait(dve, scored.get(n - 3), G_done)
            if n <= last:
                half = LEVELS[n - 1]
                g4, w4 = cut(G, half), cut(w, half)
                g_end = g4[:, :, 0, half - 1:half].broadcast_to([P, H * T // (2 * half), half])
                V(dve.tensor_tensor(w4[:, :, 0, :], g_end, g4[:, :, 0, :], ALU.subtract))
                d = V(dve.tensor_tensor(w4[:, :, 1, :], g4[:, :, 1, :], g_end, ALU.subtract))
            elif n == last + 1:
                ends.append(A(act.activation(e_end, G3[:, :, CH - 1], ACT.Exp)))
                d = V(dve.tensor_tensor(w.rearrange("p (c t) -> p c t", t=CH), G3[:, :, CH - 1:CH].broadcast_to([P, H * NC, CH]),
                                        G3, ALU.subtract))
            else:
                d, w_from = scored[n - 3], G
            p.wait(act, d)
            exps[n] = A(act.activation(w, w if n <= last + 1 else w_from, ACT.Exp))

        def multiply(n):
            w = work[n % 3]
            p.wait(dve, exps[n])
            if n <= last:
                half = LEVELS[n - 1]
                w4, q4, k4 = cut(w, half), cut(q, half), cut(k, half)
                V(dve.tensor_tensor(w4[:, :, 0, :], w4[:, :, 0, :], k4[:, :, 0, :], ALU.mult))
                multiplied[n] = V(dve.tensor_tensor(w4[:, :, 1, :], w4[:, :, 1, :], q4[:, :, 1, :], ALU.mult))
            else:
                multiplied[n] = V(dve.tensor_tensor(w, w, k if n == last + 1 else q, ALU.mult))

        def score(n):
            w = work[n % 3]
            p.wait(pe, multiplied[n], self.bank[0:4])
            for s in range(4 * NT):
                t = slice(s * P, (s + 1) * P)
                mm = pe.matmul(self.psum[:, s * P:(s + 1) * P], w[:, t], w[:, t] if n else self.cst(C_ONE), start=True, stop=True)
            scored[n] = PE(mm)

        def keep(n):
            p.wait(dve, scored[n], copied.get(n - 1))
            mask = self.cst(C_LEVEL + (n - 1) * P if n else C_ID).bitcast(U32).unsqueeze(1).broadcast_to([P, 4 * NT, P])
            ps3 = self.psum[:, 0:4 * T].rearrange("p (s t) -> p s t", t=P)
            copied[n] = V(dve.copy_predicated(S.rearrange("p (s t) -> p s t", t=P), mask, ps3))
            self.bank[0:4] = [copied[n]] * 4

        ends = []
        exponents(1)
        for n in range(last + 1):
            self.leave_psum(0)
            if n:
                keep(n - 1)
            exponents(n + 2)
            multiply(n + 1)
            self.fill(2 if 0 < n else 1)
            score(n)
            if n == 3:
                p.wait(act, self.filled[15])
                gate_done = A(act.activation(gate, gate, ACT.Silu))
        keep(last)
        multiply(last + 2)
        kw, qe = work[(last + 1) % 3], work[(last + 2) % 3]
        e_done, qe_done = ends[0], multiplied[last + 2]
        kt, v = self.B(9), self.B(8)
        p.wait(act, scored[last])
        kt_done = self.turn_tiles(kw, 4 * NT, 0, kt, [multiplied[last + 1], scored[last]])
        self.fill(1)
        p.wait(act, multiplied[last + 1])
        v_done = self.turn_tiles(v_in, 4 * NT, 0, v, self.filled[11])
        self.fill(1)
        state = lambda c, h: self.big[:, ((c - 1) * H + h) * P:((c - 1) * H + h + 1) * P]
        conv = self.convolve(kt_done)
        p.wait(pe, kt_done, v_done)
        made = []
        for c in range(NC - 1):
            b = c % 4
            rows = slice((c % 2) * CH, (c % 2 + 1) * CH)
            p.wait(pe, self.bank[b])
            for h in range(H):
                t = slice((h * NT + c // 2) * P, (h * NT + c // 2 + 1) * P)
                mm = pe.matmul(self.ps[b][:, h * P:(h + 1) * P], kt[rows, t], v[rows, t], start=True, stop=True)
            d = PE(mm)
            if self.n_fill < len(self.to_fill) and c % 2 == 1:
                self.fill(1)
            p.wait(dve, d)
            if c == 0:
                p.wait(dve, qe_done)
                d = V(dve.tensor_copy(self.big[:, 0:T], self.ps[b]))
            else:
                p.wait(dve, made[-1], e_done)
                for h in range(H):
                    d = V(dve.scalar_tensor_tensor(out=state(c + 1, h), in0=state(c, h), scalar=e_end[:, h * NC + c:h * NC + c + 1],
                                                   in1=self.ps[b][:, h * P:(h + 1) * P], op0=ALU.mult, op1=ALU.add))
            made.append(d)
            self.bank[b] = d
            next(conv, None)
        self.leave_psum(0)
        assert self.n_fill == len(self.to_fill)
        for _ in conv:
            pass
        rows_done = self.gate_sequences()
        p.wait(pe, copied[last], qe_done, made[-1])
        out = self.B(2)
        self.sq = (self.sc[0], self.sc[6])
        self.settle(act)
        stats, squares = [], []
        for h in range(H):
            b = 4 + h % 2
            p.wait(pe, self.bank[b])
            for i in range(NT):
                t = slice((h * NT + i) * P, (h * NT + i + 1) * P)
                mm = pe.matmul(self.ps[b][:, i * P:(i + 1) * P], v[:, t], S[:, t], start=True, stop=False)
                for c in (2 * i, 2 * i + 1):
                    if c:
                        mm = pe.matmul(self.ps[b][:, c * CH:(c + 1) * CH], state(c, h),
                                       qe[:, h * T + c * CH:h * T + (c + 1) * CH], start=False, stop=c % 2 == 1)
            d = PE(mm)
            p.wait(dve, d, v_done)
            t = slice(h * T, (h + 1) * T)
            o_done = V(dve.tensor_copy(out[:, t], self.ps[b]))
            self.bank[b] = o_done
            squares.append(self.head_squares(out[:, t], h, o_done, stats[h - 2] if h > 1 else None))
            if h:
                stats.append(self.head_sums(h - 1, squares[h - 1]))
            next(rows_done, None)
        stats.append(self.head_sums(HEADS - 1, squares[-1]))
        for _ in rows_done:
            pass
        self.head_norm(out, "hgrn_norm", stats[-1], None, gate, self.B(0), gate_done)

    def head_squares(self, src, h, ready, sq_free):
        p, act = self.p, self.nc.scalar
        p.wait(act, ready, sq_free)
        return p.ACT.mark(act.activation(self.sq[h % 2][:, :], src, ACT.Square))

    def head_sums(self, h, squared):
        return self.token_sums(self.sq[h % 2], [squared], lambda i: self.ps[6][:, h * NT + i:h * NT + i + 1],
                               first_wait=self.bank[6])

    def head_norm(self, o, gain, ready, scale, gate, dst, gate_done):
        p, nc = self.p, self.nc
        dve = nc.vector
        n = HEADS * NT
        r = self.misc[:, 32:32 + n]
        self.settle(dve)
        if scale is None:
            d = self.rsqrt(self.ps[6][:, 0:n], r, ready, P)
        else:
            d = p.DVE.mark(dve.tensor_tensor(r, self.ps[6][:, 0:n], scale, ALU.mult))
            p.wait(dve, d)
            d = p.DVE.mark(dve.tensor_tensor(r, r, scale, ALU.mult))
            d = self.rsqrt(r, r, d, P)
            p.wait(dve, d)
            d = p.DVE.mark(dve.tensor_tensor(r, r, scale, ALU.mult))
        self.bank[6] = d

        def spread(h):
            self.spread_used[h % 2] = self.spread(r[:, h * NT:(h + 1) * NT], d, self.sc[2 + h % 2], self.spread_used[h % 2],
                                                  7 - h % 2 * 4)
            return self.spread_used[h % 2]

        rb = spread(0)
        for h in range(HEADS):
            t = slice(h * T, (h + 1) * T)
            following = spread(h + 1) if h + 1 < HEADS else None
            p.wait(dve, rb, gate_done)
            rb = following
            e = p.DVE.mark(dve.scalar_tensor_tensor(out=dst[:, t], in0=o[:, t], scalar=self.par(gain, h),
                                                    in1=self.ps[7 - h % 2 * 4], op0=ALU.mult, op1=ALU.mult))
            self.bank[7 - h % 2 * 4] = e
            p.wait(dve, e)
            e = p.DVE.mark(dve.tensor_tensor(dst[:, t], dst[:, t], gate[:, t], ALU.mult))
        return e

    def convolve(self, free):
        p, nc = self.p, self.nc
        act, dve = nc.scalar, nc.vector
        x, self.qk = self.B(4), self.B(10)
        self.qk_done = []
        for n in range(4):
            xt, yt = self.tile(x, n), self.tile(self.qk, n)
            cw = lambda tap: self.par("conv_w", tap * 4 + n)
            p.wait(dve, free, self.filled[16 + n])
            d = p.DVE.mark(dve.tensor_scalar(yt, xt, cw(CONV - 1), self.par("conv_b", n), ALU.mult, ALU.add))
            for lag in range(1, CONV):
                p.wait(dve, d)
                d = p.DVE.mark(dve.scalar_tensor_tensor(out=yt[:, lag:T], in0=xt[:, 0:T - lag], scalar=cw(CONV - 1 - lag),
                                                        in1=yt[:, lag:T], op0=ALU.mult, op1=ALU.add))
            p.wait(act, d)
            self.qk_done.append(p.ACT.mark(act.activation(yt, yt, ACT.Silu)))
            yield

    def gate_sequences(self):
        p, nc = self.p, self.nc
        act, dve = nc.scalar, nc.vector
        A, V = p.ACT.mark, p.DVE.mark
        H, gate_bias = HEADS, self.gate_bias
        R = lambda n: self.tile(self.uf, n)[0:H, :]
        li, z, lf, B, w, M, ones = (R(n) for n in range(7))
        self.rows = w, z, M
        p.wait(dve, self.filled[27])
        V(dve.tensor_scalar(li, self.gate_rows[0:H, :], gate_bias[:, 0:1], None, ALU.add))
        z_done = V(dve.tensor_scalar(z, self.gate_rows[32:32 + H, :], gate_bias[:, 1:2], None, ALU.add))
        one = V(dve.memset(ones, 1.0))
        p.wait(act, z_done)
        d = A(act.activation(lf, z, ACT.Abs)); p.wait(act, d)
        d = A(act.activation(lf, lf, ACT.Exp, scale=-1.0)); p.wait(act, d)
        d = A(act.activation(lf, lf, ACT.Ln, bias=1.0))
        self.mo_done = A(act.activation(self.B(6), self.B(6), ACT.Sigmoid))
        yield
        p.wait(dve, d, one)
        d = V(dve.scalar_tensor_tensor(out=lf, in0=z, scalar=0.0, in1=lf, op0=ALU.min, op1=ALU.subtract)); p.wait(dve, d)
        d = V(dve.tensor_tensor_scan(B, ones, lf, 0.0, ALU.mult, ALU.add))
        yield
        p.wait(dve, d)
        d = V(dve.tensor_tensor(w, li, B, ALU.subtract)); p.wait(dve, d)
        self.M_done = V(dve.tensor_tensor_scan(M, ones, w, 0.0, ALU.mult, ALU.max))
        yield
        p.wait(dve, self.M_done)
        d = V(dve.tensor_tensor(z, B, M, ALU.add)); p.wait(act, d)
        self.em_done = A(act.activation(z, z, ACT.Exp, scale=-1.0))

    def mlstm(self):
        p, nc = self.p, self.nc
        pe, act, dve = nc.tensor, nc.scalar, nc.vector
        A, V, PE = p.ACT.mark, p.DVE.mark, p.PE.mark
        H, m = HEADS, self.misc
        v_in, gate = self.B(5), self.B(6)
        v, qk = self.B(9), self.qk
        w, z, M = self.rows
        v_done = self.turn_tiles(v_in, 4 * NT, 0, v, self.filled[23])
        p.wait(pe, self.em_done, self.bank[6])
        for n, row in ((0, w), (1, z)):
            for i in range(NT):
                mm = pe.transpose(self.ps[6][:, 32 + (n * NT + i) * H:32 + (n * NT + i + 1) * H], row[:, i * P:(i + 1) * P],
                                  self.const[0:H, C_ID:C_ID + H])
        d = PE(mm)
        cols = m[:, 64:64 + 2 * NT * H]
        p.wait(act, d)
        cols_done = A(act.copy(cols, self.ps[6][:, 32:32 + 2 * NT * H]))
        self.bank[6] = cols_done
        w_col = lambda i, h: cols[:, i * H + h:i * H + h + 1]
        out = self.B(7)
        sum_w = self.ps[6][:, 128:128 + H * NT]
        stats = []
        p.wait(pe, self.qk_done, self.M_done, v_done)
        self.settle(act, dve)
        pair = (self.B(1), self.B(8))
        pv = [None, None]
        decayed, products, weighted, squares = {}, {}, {}, []

        def decays(h):
            E = pair[h % 2]
            rows = slice((h % 2) * ML_QK, (h % 2 + 1) * ML_QK)
            qh, kh = self.tile(qk, h // 2)[rows, :], self.tile(qk, 2 + h // 2)[rows, :]
            p.wait(pe, self.bank[7])
            rb = PE(pe.matmul(self.ps[7], self.const[0:H, C_SEL + h * P:C_SEL + (h + 1) * P], M, start=True, stop=True))
            p.wait(dve, rb, cols_done, pv[h % 2])
            for (i, t0, n, c) in CAUSAL:
                d = V(dve.tensor_scalar(E[:, c:c + n], self.ps[7][:, t0:t0 + n], w_col(i, h), 0.0, ALU.subtract, ALU.max))
            self.bank[7] = d
            p.wait(act, d)
            decayed[h] = A(act.activation(E[:, 0:N_CAUSAL], E[:, 0:N_CAUSAL], ACT.Exp, scale=-1.0))
            b0 = 3 * (h % 2)
            products[h] = self.causal_product(b0, lambda i: kh[:, i * P:(i + 1) * P], lambda t0, n: qh[:, t0:t0 + n], None)

        def weigh(h):
            E, b0 = pair[h % 2], 3 * (h % 2)
            p.wait(dve, decayed[h], products[h])
            d = V(dve.scalar_tensor_tensor(out=E[:, 0:N_CAUSAL], in0=self.psum[:, b0 * T:b0 * T + N_CAUSAL], scalar=ML_QK ** -0.5,
                                           in1=E[:, 0:N_CAUSAL], op0=ALU.mult, op1=ALU.mult))
            self.bank[b0:b0 + 3] = [d] * 3
            p.wait(dve, d)
            weighted[h] = self.mask_diagonals(E, C_LE)

        decays(0)
        weigh(0)
        decays(1)
        for h in range(H):
            E, b0 = pair[h % 2], 3 * (h % 2)
            p.wait(pe, weighted[h], self.bank[b0], self.bank[6])
            nd = PE(self.causal_values(self.ps[b0], lambda i: v[:, (h * NT + i) * P:(h * NT + i + 1) * P], E))
            for j in range(NT):
                for i in range(j + 1):
                    c = causal_column(i, j)
                    mm = pe.matmul(sum_w[:, h * NT + j:h * NT + j + 1], E[:, c:c + P], self.cst(C_ONE, 1), start=i == 0, stop=i == j)
            pv[h % 2] = PE(mm)
            if h + 1 < H:
                weigh(h + 1)
            p.wait(dve, nd)
            t = slice(h * T, (h + 1) * T)
            o_done = V(dve.tensor_copy(out[:, t], self.ps[b0]))
            self.bank[b0] = o_done
            if h == 0:
                self.settle(act)
            squares.append(self.head_squares(out[:, t], h, o_done, stats[h - 2] if h > 1 else None))
            if h:
                stats.append(self.head_sums(h - 1, squares[h - 1]))
            if h + 2 < H:
                decays(h + 2)
        stats.append(self.head_sums(H - 1, squares[-1]))
        scale = m[:, 96:96 + H * NT]
        neg = m[:, 112:112 + H * NT]
        self.settle(dve)
        d = V(dve.tensor_scalar(neg, sum_w, -1.0, None, ALU.mult)); p.wait(dve, d)
        d = V(dve.tensor_tensor(scale, sum_w, neg, ALU.max)); p.wait(dve, d)
        em = cols[:, NT * H:2 * NT * H].rearrange("p (i h) -> p h i", h=H)
        s3 = scale.rearrange("p (h i) -> p h i", h=H)
        d = V(dve.tensor_tensor(s3, s3, em, ALU.max)); p.wait(dve, d)
        d = V(dve.reciprocal(scale, scale)); p.wait(dve, d)
        self.head_norm(out, "mlstm_norm", [d, stats[-1]], scale, gate, self.B(2), self.mo_done)


    def attention_mixer(self):
        p, nc, a = self.p, self.nc, self.a
        pe, act, dve = nc.tensor, nc.scalar, nc.vector
        A, V, PE = p.ACT.mark, p.DVE.mark, p.PE.mark
        pair = (lambda k: self.tile(self.uhi, k), lambda k: self.tile(self.ulo, k))
        self.fresh = True
        self.project(a["proj_in"], 0, 4, self.big)
        for j in range(2):
            d = self.one_chunk(a["proj_in"][16 + j], j, pair, KD)
            p.wait(dve, d)
            self.bank[j] = V(dve.tensor_tensor(self.tile(self.big, 16 + j), self.ps[j], self.rb, ALU.mult))
        self.rope_tables()
        self.latent_norms()
        self.project(a["proj_in"], 18, 4, self.big[:, GATE_AT * T:], ACT.Sigmoid)
        self.settle(pe, act, dve)
        self.latent_ready = []
        for k in range(KCQ + KCKV):
            self.latent_ready += self.split_pair(self.tile(self.big, k), self.tile(self.uhi, k), self.tile(self.ulo, k), None)
        self.make_heads()
        self.attend()
        self.merge()

    def rope_tables(self):
        p, nc = self.p, self.nc
        act, dve = nc.scalar, nc.vector
        A, V = p.ACT.mark, p.DVE.mark
        rows = slice(NOPE, QK)
        pos, ang, n, t = (self.sc[i][rows, :] for i in (4, 1, 2, 3))
        cos, sin = self.cos, self.sin = self.sc[5][rows, :], self.sc[6][rows, :]
        self.settle(act, dve)
        landed = nc.alloc_semaphore("positions_loaded")
        act.dma_start(pos.bitcast(I32), self.a["positions"].broadcast_to([ROPE, T])).then_inc(landed, 16)
        dve.wait_ge(landed, 16)
        d = V(dve.tensor_copy(ang, pos.bitcast(I32))); p.wait(dve, d)
        d = V(dve.tensor_scalar(ang, ang, self.const[rows, C_FREQ:C_FREQ + 1], None, ALU.mult)); p.wait(dve, d)
        magic = 1.5 * 2.0 ** 23
        d = V(dve.tensor_scalar(n, ang, 1.0 / (2 * np.pi), magic, ALU.mult, ALU.add)); p.wait(dve, d)
        d = V(dve.tensor_scalar(n, n, -magic, None, ALU.add)); p.wait(dve, d)
        c1 = 6.28125
        c2 = float(np.floor((2 * np.pi - c1) * 2 ** 22) / 2 ** 22)
        c3 = 2 * np.pi - c1 - c2
        for c in (c1, c2, c3):
            d = V(dve.scalar_tensor_tensor(out=ang, in0=n, scalar=-c, in1=ang, op0=ALU.mult, op1=ALU.add)); p.wait(dve, d)
        edge = 3.1415925
        d = V(dve.tensor_scalar(t, ang, float(np.pi / 2), None, ALU.add)); p.wait(dve, d)
        d = V(dve.tensor_scalar(n, t, float(np.pi), -2 * float(np.pi), ALU.is_gt, ALU.mult)); p.wait(dve, d)
        d = V(dve.tensor_tensor(t, t, n, ALU.add)); p.wait(dve, d)
        V(dve.tensor_scalar(t, t, edge, -edge, ALU.min, ALU.max))
        d = V(dve.tensor_scalar(ang, ang, edge, -edge, ALU.min, ALU.max)); p.wait(act, d)
        A(act.activation(cos, t, ACT.Sin))
        self.tables_done = A(act.activation(sin, ang, ACT.Sin))

    def latent_norms(self):
        p, nc = self.p, self.nc
        dve = nc.vector
        self.settle(nc.scalar, dve)
        n = KCQ + KCKV
        used = [None, None]
        for k in range(n):
            used[k % 2] = self.square_sums(k, None, self.tile(self.big, k), self.sc[1 + k % 2], used[k % 2], wait_bank=self.bank[4])
        sums, r = self.misc[:, 0:2 * NT], self.misc[:, 2 * NT:4 * NT]
        p.wait(dve, used)
        parts = (("q_latent", 0, KCQ), ("kv_latent", KCQ, KCKV))
        for m, (name, first, count) in enumerate(parts):
            view = self.ps[4][:, first * NT:(first + count) * NT].rearrange("p (k i) -> p i k", i=NT)
            d = p.DVE.mark(dve.tensor_reduce(sums[:, m * NT:(m + 1) * NT], view, AX.X, ALU.add))
            p.wait(dve, d)
            d = p.DVE.mark(dve.tensor_scalar(sums[:, m * NT:(m + 1) * NT], sums[:, m * NT:(m + 1) * NT], 1.0 / (count * P), None, ALU.mult))
        self.bank[4] = d
        d = self.rsqrt(sums, r, d, 1)
        rb = [self.spread(r[:, m * NT:(m + 1) * NT], d, self.sc[3 + m], None, 5 + 2 * m) for m in range(2)]
        for m, (name, first, count) in enumerate(parts):
            p.wait(dve, rb[m])
            for k in range(count):
                t = self.tile(self.big, first + k)
                d = p.DVE.mark(dve.scalar_tensor_tensor(out=t, in0=t, scalar=self.par(name, k), in1=self.ps[5 + 2 * m],
                                                        op0=ALU.mult, op1=ALU.mult))
            self.bank[5 + 2 * m] = d

    def rotate(self, x, ready, bank, tmp):
        p, nc = self.p, self.nc
        rows = slice(NOPE, QK)
        p.wait(nc.tensor, ready, self.bank[bank])
        rot = self.ps[bank][rows, :]
        turned = p.PE.mark(nc.tensor.matmul(rot, self.const[rows, C_ROT:C_ROT + ROPE], x, start=True, stop=True))
        p.wait(nc.vector, turned, self.tables_done)
        p.DVE.mark(nc.vector.tensor_tensor(x, x, self.cos, ALU.mult))
        d = p.DVE.mark(nc.vector.tensor_tensor(tmp[rows, :], rot, self.sin, ALU.mult))
        self.bank[bank] = d
        p.wait(nc.vector, d)
        return p.DVE.mark(nc.vector.tensor_tensor(x, x, tmp[rows, :], ALU.add))

    def make_heads(self):
        p, nc, a = self.p, self.nc, self.a
        pe, act, dve = nc.tensor, nc.scalar, nc.vector
        A, V, PE = p.ACT.mark, p.DVE.mark, p.PE.mark
        q_gain, k_gain = self.misc[0:QK, 128:129], self.misc[0:QK, 129:130]
        landed = nc.alloc_semaphore("head_gains_loaded")
        act.dma_start(self.misc[0:QK, 128:130], a["head_gains"]).then_inc(landed, 16)
        dve.wait_ge(landed, 16)
        self.Q = Q = [self.tile(self.big, 34 + h) for h in range(AH)]
        self.K = K = [self.tile(self.uf, n) for n in (5, 6, 7, 13, 14, 15)] + [self.tile(self.big, n) for n in (42, 43)]
        v = self.B(0)
        rope_rows = slice(NOPE, QK)
        self.settle(pe, act, dve)
        kr = self.tile(self.big, KCQ + KCKV)[rope_rows, :]
        krot = self.sc[4]
        sq = self.sc[0:2]
        for n in range(2):
            kr_sq = A(act.activation(self.sc[2 + n][rope_rows, :], kr, ACT.Square))
        d = V(dve.tensor_scalar(krot[rope_rows, :], kr, k_gain[rope_rows, :], None, ALU.mult))
        krot_done = self.rotate(krot[rope_rows, :], d, 3, self.sc[0])
        at = lambda first: (lambda k: self.tile(self.uhi, first + k), lambda k: self.tile(self.ulo, first + k))

        def products(name, heads_cols, tiles, first):
            xhi, xlo = at(first)
            chunk = None
            for h in range(AH):
                if h % 4 == 0:
                    hi, lo, ready = self.w.chunk(a[name][h // 4])
                    p.wait(pe, ready, self.latent_ready)
                b = h % 2
                p.wait(pe, self.bank[b])
                for k in range(tiles):
                    c = (h % 4 * tiles + k) * heads_cols
                    m = self.mm3(self.ps[b][0:heads_cols, :], hi, lo, slice(c, c + heads_cols), xhi(k), xlo(k), k == 0, k == tiles - 1)
                yield h, b, (self.w.used.mark(m) if h % 4 == 3 else PE(m))

        sums, q_done = [None, None], []

        def after_q(h, b, d):
            p.wait(act, d, sums[h % 2], krot_done)
            s = A(act.activation(sq[h % 2][0:QK, :], self.ps[b][0:QK, :], ACT.Square))
            p.wait(dve, s)
            g_done = self.bank[b] = V(dve.tensor_scalar(Q[h][0:QK, :], self.ps[b][0:QK, :], q_gain, None, ALU.mult))
            return h, s, g_done

        def finish_q(h, s, g_done):
            sums[h % 2] = self.token_sums(sq[h % 2], s, lambda i: self.ps[6][:, h * NT + i:h * NT + i + 1], rows=QK,
                                          first_wait=self.bank[6])
            p.wait(dve, q_done[-2] if h > 1 else krot_done)
            q_done.append(self.rotate(Q[h][rope_rows, :], g_done, 2 + h % 2, self.vt[h % 2]))

        before = None
        for x in products("q_up", QK, KCQ, 0):
            x = after_q(*x)
            if before:
                finish_q(*before)
            before = x
        finish_q(*before)
        self.settle(act, dve)
        ksum, vt_used, self.k_done = [None, None], [None, None], []

        def after_k(h, b, d):
            ks, vt = self.sc[2 + h % 2], self.vt[h % 2]
            p.wait(act, d, ksum[h % 2], vt_used[h % 2], kr_sq)
            A(act.activation(ks[0:NOPE, :], self.ps[b][0:NOPE, :], ACT.Square))
            s = A(act.copy(vt[NOPE:P, :], self.ps[b][NOPE:P, :]))
            p.wait(dve, s)
            self.bank[b] = V(dve.tensor_scalar(K[h][0:NOPE, :], self.ps[b][0:NOPE, :], k_gain[0:NOPE, :], None, ALU.mult))
            self.k_done.append(self.bank[b])
            return h, s

        def finish_k(h, s):
            ks, vt = self.sc[2 + h % 2], self.vt[h % 2]
            ksum[h % 2] = self.token_sums(ks, s, lambda i: self.ps[6][:, (AH + h) * NT + i:(AH + h) * NT + i + 1], rows=QK)
            b = 7 - 2 * (h % 2)
            p.wait(pe, self.bank[b])
            for i in range(NT):
                m = pe.transpose(self.ps[b][:, i * HV:(i + 1) * HV], vt[NOPE:P, i * P:(i + 1) * P], self.const[NOPE:P, C_ID + NOPE:C_ID + P])
            vt_used[h % 2] = PE(m)
            p.wait(dve, vt_used[h % 2])
            self.bank[b] = V(dve.tensor_copy(v[:, h * NT * HV:(h + 1) * NT * HV], self.ps[b][:, 0:NT * HV]))

        before = None
        for x in products("kv_up", P, KCKV, KCQ):
            x = after_k(*x)
            if before:
                finish_k(*before)
            before = x
        finish_k(*before)
        r = self.misc[:, 32:32 + 2 * AH * NT]
        self.settle(dve)
        d = self.rsqrt(self.ps[6][:, 0:2 * AH * NT], r, ksum, QK)
        self.bank[6] = d
        sv = self.big[:, 14 * T:18 * T]
        self.rq, rk = r[:, 0:AH * NT], r[:, AH * NT:2 * AH * NT]
        self.settle(act)

        def spread_k(h):
            self.spread_used[h % 2] = self.spread(rk[:, h * NT:(h + 1) * NT], d, self.sc[h % 2], self.spread_used[h % 2], 4 + h % 2)
            return self.spread_used[h % 2]

        rb = spread_k(0)
        self.turn_tiles(sv, 4 * NT, 0, sv, None)
        for h in range(AH):
            b = 4 + h % 2
            following = spread_k(h + 1) if h + 1 < AH else None
            p.wait(dve, rb, self.k_done[h], krot_done)
            V(dve.tensor_tensor(K[h][0:NOPE, :], K[h][0:NOPE, :], self.ps[b][0:NOPE, :], ALU.mult))
            self.bank[b] = V(dve.tensor_tensor(K[h][rope_rows, :], krot[rope_rows, :], self.ps[b][rope_rows, :], ALU.mult))
            rb = following
        V(dve.tensor_scalar(self.rq, self.rq, QK ** -0.5, None, ALU.mult))
        V(dve.tensor_scalar(self.big[:, 6 * T:10 * T], self.big[:, 6 * T:10 * T], HV ** -0.5, None, ALU.mult))
        self.settle(dve)
        masks = self.sc[5][:, :].bitcast(BF16)
        self.id16, self.ngt16, self.nge16 = (masks[:, n * P:(n + 1) * P] for n in range(3))
        for to, c in ((self.id16, C_ID), (self.ngt16, C_NGT), (self.nge16, C_NGE)):
            V(dve.tensor_copy(to, self.cst(c)))
        self.nsuf, self.none = self.sums_lhs[:, 0:P], self.sums_lhs[:, P:2 * P]
        for to, c in ((self.nsuf, C_NSUF), (self.none, C_NONE)):
            V(dve.tensor_copy(to, self.cst(c)))

    def attend(self):
        p, nc, a = self.p, self.nc, self.a
        pe, act, dve = nc.tensor, nc.scalar, nc.vector
        A, V, PE = p.ACT.mark, p.DVE.mark, p.PE.mark
        Q, K, rq, v = self.Q, self.K, self.rq, self.B(0)
        sq, sk = (lambda n, f=f: self.tile(self.big, f + n) for f in (6, 10))
        sv = self.big[:, 14 * T:18 * T]
        row = lambda t, n: t[:, n * N_CAUSAL:(n + 1) * N_CAUSAL]
        probs, turned = row(self.uf, 0), row(self.uf, 1)
        z = [row(self.uf[:, 8 * T:], n) for n in range(2)]
        soft = [row(self.scf, n) for n in range(2)]
        free_pair = self.w.n % PAIR
        soft_hi, soft_lo = self.w.hi[1 - free_pair][:, 0:N_CAUSAL], self.w.lo[1 - free_pair][:, 0:N_CAUSAL]
        mx, nb, rs = (self.misc[:, c:c + AH * NT] for c in (96, 130, 162))
        self.o_mla, self.o_sb = [Q[n] for n in range(AH // 2)], [sq(n) for n in range(AH // 2)]
        self.settle(pe, act, dve)
        A0, B0 = 0, 3 * T
        none = [None] * AH
        scaled, exps, divided, turned_done, turned_used, probs_used = (list(none) for _ in range(6))
        z_done, ln_done, soft_used, softs, weights_done, weights_used = (list(none) for _ in range(6))
        half = lambda h: slice(h % 2 * HV, (h % 2 + 1) * HV)
        prior = lambda x, h, n: x[h - n] if h >= n else None

        def logits(h):
            p.wait(pe, self.bank[0:3])
            for i, c in ROWS:
                n = (i + 1) * P
                pe.matmul(self.psum[:, c:c + n], Q[h][0:QK, i * P:(i + 1) * P], K[h][0:QK, 0:n], start=True, stop=True)
                m = pe.matmul(self.psum[:, c + n - P:c + n], self.id16, self.ngt16, start=False, stop=True, skip_group_check=True)
            p.wait(dve, PE(m))
            for i, c in ROWS:
                d = V(dve.tensor_reduce(mx[:, h * NT + i:h * NT + i + 1], self.psum[:, c:c + (i + 1) * P], AX.X, ALU.max))
            p.wait(dve, d)
            hs = slice(h * NT, (h + 1) * NT)
            d = V(dve.scalar_tensor_tensor(out=nb[:, hs], in0=mx[:, hs], scalar=-1.0, in1=rq[:, hs], op0=ALU.mult, op1=ALU.mult))
            scaled[h] = d
            self.bank[0:3] = [d] * 3

        def exponents(h):
            p.wait(act, scaled[h], prior(probs_used, h, 1))
            for i, c in ROWS:
                x = h * NT + i
                exps[h] = A(act.activation(probs[:, c:c + (i + 1) * P], self.psum[:, c:c + (i + 1) * P], ACT.Exp,
                                           bias=nb[:, x:x + 1], scale=rq[:, x:x + 1], accum_out=rs[:, x:x + 1]))
            self.bank[0:3] = [exps[h]] * 3

        def divide(h):
            hs = slice(h * NT, (h + 1) * NT)
            p.wait(dve, exps[h])
            d = V(dve.reciprocal(rs[:, hs], rs[:, hs]))
            p.wait(dve, d)
            for i, c in ROWS:
                w = probs[:, c:c + (i + 1) * P]
                d = V(dve.tensor_scalar(w, w, rs[:, h * NT + i:h * NT + i + 1], None, ALU.mult))
            divided[h] = d

        def transpose(h):
            p.wait(pe, divided[h], self.bank[3:6])
            for i, c in ROWS:
                for j in range(i + 1):
                    to = B0 + causal_column(j, i)
                    m = pe.transpose(self.psum[:, to:to + P], probs[:, c + j * P:c + (j + 1) * P], self.cst(C_ID))
            probs_used[h] = PE(m)
            p.wait(dve, probs_used[h], prior(turned_used, h, 1))
            turned_done[h] = V(dve.tensor_copy(turned, self.psum[:, B0:B0 + N_CAUSAL]))
            self.bank[3:6] = [turned_done[h]] * 3

        def mla_values(h):
            p.wait(pe, turned_done[h], self.bank[6])
            v_at = lambda i: v[:, (h * NT + i) * HV:(h * NT + i + 1) * HV]
            turned_used[h] = PE(self.causal_values(self.ps[6][half(h), :], v_at, turned))
            p.wait(dve, turned_used[h])
            self.bank[6] = V(dve.tensor_copy(self.o_mla[h // 2][half(h), :], self.ps[6][half(h), :]))

        def stick_logits(h):
            p.wait(pe, self.bank[0:3])
            for i, t0, n, c in CAUSAL:
                m = pe.matmul(self.psum[:, A0 + c:A0 + c + n], sk(h // 2)[half(h), i * P:(i + 1) * P], sq(h // 2)[half(h), t0:t0 + n],
                              start=True, stop=True)
            s, zh = soft[h % 2], z[h % 2]
            p.wait(act, PE(m), prior(weights_used, h, 2))
            z_done[h] = A(act.copy(zh, self.psum[:, A0:A0 + N_CAUSAL]))
            self.bank[0:3] = [z_done[h]] * 3
            p.wait(act, z_done[h], prior(softs, h, 2))
            d = A(act.activation(s, zh, ACT.Abs)); p.wait(act, d)
            ln_done[h] = A(act.activation(s, s, ACT.Exp, scale=-1.0))

        def logarithm(h):
            s = soft[h % 2]
            p.wait(act, ln_done[h])
            ln_done[h] = A(act.activation(s, s, ACT.Ln, bias=1.0))

        def softplus(h):
            s, zh = soft[h % 2], z[h % 2]
            p.wait(dve, ln_done[h], z_done[h])
            d = V(dve.scalar_tensor_tensor(out=s, in0=zh, scalar=0.0, in1=s, op0=ALU.max, op1=ALU.add))
            p.wait(dve, d)
            softs[h] = self.mask_diagonals(s, C_LT)

        def split(h):
            s, d = soft[h % 2], softs[h]
            p.wait(act, d, prior(soft_used, h, 1))
            d = A(act.copy(soft_hi, s))
            p.wait(dve, d, prior(soft_used, h, 1))
            softs[h] = [d, V(dve.tensor_tensor(soft_lo, s, soft_hi.bitcast(F32), ALU.subtract))]

        def stick_sums(h):
            p.wait(pe, self.bank[3:6])
            first = {}

            def add(c, n, lhs, rhs):
                b = c // T
                m = pe.matmul(self.psum[:, B0 + c:B0 + c + n], lhs, rhs, start=b not in first, stop=True, skip_group_check=b in first)
                first[b] = True
                return m
            for part, ready in zip((soft_hi, soft_lo), softs[h]):
                p.wait(pe, ready)
                for c in range(0, N_CAUSAL, T):
                    n = min(T, N_CAUSAL - c)
                    add(c, n, self.nsuf, part[:, c:c + n])
                for c, first_from, step, blocks in SUMMED:
                    if step == 0:
                        rhs = part[:, first_from:first_from + P].unsqueeze(1).broadcast_to([P, blocks, P])
                    elif step == P:
                        rhs = part[:, first_from:first_from + blocks * P]
                    else:
                        rhs = part.rearrange("p (b t) -> p b t", t=step)[:, :, first_from:first_from + P]
                    add(c, blocks * P, self.none, rhs)
            m = add(0, T, self.id16, self.nge16.unsqueeze(1).broadcast_to([P, NT, P]))
            soft_used[h] = PE(m)
            zh = z[h % 2]
            p.wait(dve, soft_used[h])
            d = V(dve.tensor_tensor(zh, zh, self.psum[:, B0:B0 + N_CAUSAL], ALU.add))
            self.bank[3:6] = [d] * 3
            p.wait(act, d)
            weights_done[h] = A(act.activation(zh, zh, ACT.Exp))

        def stick_values(h):
            p.wait(pe, weights_done[h], self.bank[7])
            v_at = lambda i: sv[:, ((h // 2) * NT + i) * P + h % 2 * HV:((h // 2) * NT + i) * P + (h % 2 + 1) * HV]
            weights_used[h] = PE(self.causal_values(self.ps[7][half(h), :], v_at, z[h % 2]))
            p.wait(dve, weights_used[h])
            self.bank[7] = V(dve.tensor_copy(self.o_sb[h // 2][half(h), :], self.ps[7][half(h), :]))

        def following(h):
            stick_logits(h)
            if h:
                stick_sums(h - 1)
            logits(h)
            logarithm(h)
            if h:
                transpose(h - 1)
                stick_values(h - 1)
            softplus(h)
            if h:
                mla_values(h - 1)
            exponents(h)
            split(h)
            divide(h)

        for h in range(AH):
            following(h)
        stick_sums(AH - 1)
        transpose(AH - 1)
        stick_values(AH - 1)
        mla_values(AH - 1)
        p.wait(nc.gpsimd, soft_used[AH - 1], softs[AH - 1])

    def merge(self):
        p, nc, a = self.p, self.nc, self.a
        pe, act, dve = nc.tensor, nc.scalar, nc.vector
        A, V, PE = p.ACT.mark, p.DVE.mark, p.PE.mark
        W, ps = self.w, self.ps
        self.settle(pe, act, dve)
        ready = []
        for n in range(KD):
            src = self.o_mla[n] if n < 4 else self.o_sb[n - 4]
            ready += self.split_pair(src, self.tile(self.uhi, n), self.tile(self.ulo, n), None)
        self.settle(pe, act, dve)
        t1, t2 = self.sc[0:2], self.sc[2:4]
        W.begin()
        with p.loop(2, act=4, dve=16, split=8, used=4) as i:
            for j in range(4):
                lo_done = p.DVE.ahead(4 * j + 4)
                before = lambda eng: (p.wait(eng, p.DVE.ahead(4 * j + 4 - 8)) if j > 1 else p.wait(eng, p.DVE.ahead(4 * j + 4 + 8), back=1))
                hi, lo, split = W.chunk(a["branch"][i * 4 + j])
                p.wait(pe, split)
                before(pe)
                b = 2 * (j % 2)
                for half in range(2):
                    for k in range(4):
                        m = self.mm3(ps[b + half], hi, lo, slice((4 * half + k) * P, (4 * half + k + 1) * P),
                                     self.tile(self.uhi, 4 * half + k), self.tile(self.ulo, 4 * half + k), k == 0, k == 3)
                product = W.used.mark(m)
                p.wait(dve, product)
                before(dve)
                x, y = t1[j % 2][:, :], t2[j % 2][:, :]
                g = lambda n: self.big[:, ds((i * 4 + (GATE_AT + n * KD + j)) * T, T)]
                V(dve.tensor_tensor(x, ps[b], g(0), ALU.mult))
                d = V(dve.tensor_tensor(y, ps[b + 1], g(1), ALU.mult))
                p.wait(dve, d)
                d = V(dve.tensor_tensor(x, x, y, ALU.add))
                mhi, mlo = self.hhi[:, ds((i * 4 + j) * T, T)], self.hlo[:, ds((i * 4 + (LO_AT + j)) * T, T)]
                p.wait(act, d)
                d = A(act.copy(mhi, x))
                p.wait(dve, d)
                V(dve.tensor_tensor(mlo, x, mhi.bitcast(F32), ALU.subtract))
        W.finish(2)
        self.bank[0:4] = [[Done(p.ACT, p.ACT.count, False), Done(p.DVE, p.DVE.count, False)]] * 4
        self.into_stream(a["proj_out"], 2, 4, 1, KD, self.hhi, self.hlo[:, LO_AT * T:], 1.0, None, ("ffn2_norm", 0))

    def embed(self):
        p, nc, a = self.p, self.nc, self.a
        pe, act, dve = nc.tensor, nc.scalar, nc.vector
        A, V = p.ACT.mark, p.DVE.mark
        W, ps = self.w, self.ps
        self.settle(act)
        landed = nc.alloc_semaphore("p_loaded")
        at = self.big[:, 30 * T:32 * T]
        act.dma_start(at, a["p"]).then_inc(landed, 16)
        act.wait_ge(landed, 16)
        dve.wait_ge(landed, 16)
        pairs = []
        for k in range(2):
            pairs += self.split_pair(at[:, k * T:(k + 1) * T], self.tile(self.hhi, k), self.tile(self.hlo, k), None)
        g, t = self.sc[1:3], self.sc[3:5]
        p.wait(pe, pairs, self.bank[0:4])

        def turn(i):
            for j in range(4):
                before = (p.DVE.ahead(3 * (j - 1)), 0) if j > 1 else (p.DVE.ahead(3 * (j + 3)), 1)
                hi, lo, split = W.chunk(a["embed"][i * 4 + j])
                p.wait(pe, split)
                b = 2 * (j % 2)
                if p.once and j == 0:
                    product = self.first_chunk(ps[b], hi, lo, last=False)
                    self.factor()
                    for line in (p.ACT, p.DVE):
                        line.start = line.count
                else:
                    p.wait(pe, before[0], back=before[1])
                    for k in range(KD):
                        self.mm3(ps[b], hi, lo, slice(k * P, (k + 1) * P), self.tile(self.uhi, k), self.tile(self.ulo, k), k == 0, k == KD - 1)
                for k in range(2):
                    m = self.mm3(ps[b + 1], hi, lo, slice((KD + k) * P, (KD + k + 1) * P), self.tile(self.hhi, k), self.tile(self.hlo, k),
                                 k == 0, k == 1)
                product = W.used.mark(m)
                gt, tt = g[j % 2][:, :], t[j % 2][:, :]
                p.wait(dve, product)
                p.wait(dve, before[0], back=before[1])
                d = V(dve.tensor_tensor(gt, ps[b], self.rb, ALU.mult))
                p.wait(act, d)
                d = A(act.activation(gt, gt, ACT.Sigmoid))
                p.wait(dve, d)
                d = V(dve.tensor_tensor(tt, gt, ps[b + 1], ALU.mult))
                p.wait(dve, d)
                x = self.x[:, ds((i * 4 + j) * T, T)]
                V(dve.tensor_tensor(x, x, tt, ALU.add))

        p.turns(2, turn, act=4, dve=12, split=8, used=4)


    def causal_product(self, b0, lhs, rhs, ready):
        p, pe = self.p, self.nc.tensor
        p.wait(pe, ready, self.bank[b0:b0 + 3])
        for (i, t0, n, c) in CAUSAL:
            m = pe.matmul(self.psum[:, b0 * T + c:b0 * T + c + n], lhs(i), rhs(t0, n), start=True, stop=True)
        d = p.PE.mark(m)
        self.bank[b0:b0 + 3] = [d] * 3
        return d

    def mask_diagonals(self, x, mask):
        x3 = x[:, 0:T].rearrange("p (i t) -> p i t", t=P)
        m3 = self.cst(mask).unsqueeze(1).broadcast_to([P, NT, P])
        return self.p.DVE.mark(self.nc.vector.tensor_tensor(x3, x3, m3, ALU.mult))

    def causal_values(self, out, v, w):
        blocks = sorted(CAUSAL, key=lambda x: (x[0], x[1]))
        for n, (i, t0, width, c) in enumerate(blocks):
            m = self.nc.tensor.matmul(out[:, t0:t0 + width], v(i), w[:, c:c + width], start=n == 0, stop=n == len(blocks) - 1,
                                      skip_group_check=True)
        return m

    def col(self, i):
        return self.ps[4][:, i:i + 1]

    def settle(self, *engines):
        p = self.p
        for e in engines:
            p.wait(e, [Done(line, line.count, False) for line in (p.PE, p.ACT, p.DVE, p.W.used)])


def block_program(nc, a, out, upto=99):
    b = Build(nc, a, out)
    b.load()
    par = lambda name, first=0: (lambda k: b.par(name, first + k))
    b.from_stream(par("norm_pre"))
    b.ffn(a["ffn1_in"], a["ffn1_out"], par("norm_post", 0), ("norm_pre", KD))
    b.gated_mixer()
    b.y_tiles = b.y
    b.ffn(a["ffn2_in"], a["ffn2_out"], par("norm_post", 2 * KD), ("ffn1_norm", 0))
    b.ffn(a["ffn3_in"], a["ffn3_out"], None, ("mix_norm", 0))
    b.attention_mixer()
    b.ffn(a["ffn4_in"], a["ffn4_out"], None, ("ple_norm", 0))
    b.embed()
    b.store()


def lhs_tiles(w, cols=None):
    k, n = w.shape
    cols = cols or P
    return np.ascontiguousarray(w.reshape(k // P, P, n // cols, cols).transpose(2, 1, 0, 3)).reshape(n // cols, P, -1)


def columns(v):
    return np.ascontiguousarray(v.reshape(-1, P).T)


def ffn_in(w):
    t = lhs_tiles(w)
    return np.ascontiguousarray(t.reshape(2, KF, P, -1).transpose(1, 0, 2, 3)).reshape(2 * KF, P, -1)


def ffn_out(w):
    t = lhs_tiles(w)
    return np.ascontiguousarray(t.reshape(KD, P, 2, SLOT).transpose(0, 2, 1, 3)).reshape(2 * KD, P, SLOT)


def mix_in(w):
    n = w.shape[1] - 2 * HEADS
    gates = np.concatenate([w[:, n:n + HEADS], w[:, 0:32 - HEADS], w[:, n + HEADS:], w[:, 0:P - 32 - HEADS]], axis=1)
    return lhs_tiles(np.concatenate([w[:, :n], gates], axis=1))


def proj_in(w):
    n = KCQ * P + KCKV * P
    rope = np.concatenate([w[:, 0:NOPE], w[:, n:n + ROPE], w[:, 0:P - QK]], axis=1)
    return lhs_tiles(np.concatenate([w[:, :n], rope, w[:, n + ROPE:]], axis=1))


def head_tiles(w, cols):
    t = lhs_tiles(w, cols)
    return np.ascontiguousarray(t.reshape(2, 4, P, -1).transpose(0, 2, 1, 3)).reshape(2, P, -1)


def constants():
    c = np.zeros((P, N_CONST), np.float32)
    s, t = np.arange(P)[:, None], np.arange(P)[None, :]
    c[:, C_ID:C_ID + P] = s == t
    c[:, C_ONE:C_ONE + P] = 1
    c[:, C_LE:C_LE + P] = s <= t
    c[:, C_LT:C_LT + P] = s < t
    c[:, C_NSUF:C_NSUF + P] = -1.0 * (s >= t)
    c[:, C_NONE:C_NONE + P] = -1
    c[:, C_NGT:C_NGT + P] = NEVER * (t > s)
    c[:, C_NGE:C_NGE + P] = NEVER * (s >= t)
    for n, h in enumerate(LEVELS):
        c[:, C_LEVEL + n * P:C_LEVEL + (n + 1) * P] = (s // (2 * h) == t // (2 * h)) & (s % (2 * h) < h) & (t % (2 * h) >= h)
    c[:, C_RESET:C_RESET + T] = np.arange(T) % CH != 0
    for h in range(HEADS):
        c[h, C_SEL + h * P:C_SEL + (h + 1) * P] = 1
    r = np.arange(ROPE // 2)
    c[NOPE + ROPE // 2 + r, C_ROT + r] = -1
    c[NOPE + r, C_ROT + ROPE // 2 + r] = 1
    freq = (10000.0 ** (-(2.0 * r) / ROPE)).astype(np.float32)
    c[NOPE:QK, C_FREQ] = np.concatenate([freq, freq])
    return c


def layout(i):
    f = {k: np.asarray(v) for k, v in i.items()}
    pieces = {
        "norm_pre": columns(f["norm_pre"]), "norm_post": columns(f["norm_post"]),
        "conv_w": columns(f["conv_w"]), "conv_b": columns(f["conv_b"]), "lb": columns(f["hgrn_lb_logits"]),
        "hgrn_norm": columns(f["hgrn_norm"]), "mlstm_norm": columns(f["mlstm_norm"]),
        "ffn1_norm": columns(f["ffn1_norm_2"]), "mix_norm": columns(f["mix_norm_2"]),
        "q_latent": columns(f["q_latent_norm_2"]), "kv_latent": columns(f["kv_latent_norm_2"]),
        "ffn2_norm": columns(f["ffn2_norm_2"]), "ple_norm": columns(f["ple_norm_2"]),
    }
    return {
        "const": constants(),
        "param": np.concatenate([pieces[n] for n in PARAMS], axis=1),
        "x": np.ascontiguousarray(f["x"][0].T.reshape(KD, P, T).transpose(1, 0, 2)).reshape(P, KD * T),
        "ffn1_in": ffn_in(f["ffn1_w_in"][0]), "ffn1_out": ffn_out(f["ffn1_w_out"][0]),
        "mix_in": mix_in(f["w_mix_in"][0]), "mix_out": lhs_tiles(f["w_mix_out"][0]),
        "gate_bias": np.ascontiguousarray(f["mlstm_gate_bias"].reshape(2, HEADS).T),
        "ffn2_in": ffn_in(f["ffn2_w_in"][0]), "ffn2_out": ffn_out(f["ffn2_w_out"][0]),
        "ffn3_in": ffn_in(f["ffn1_w_in_2"][0]), "ffn3_out": ffn_out(f["ffn1_w_out_2"][0]),
        "proj_in": proj_in(f["w_in_2"][0]),
        "q_up": head_tiles(f["w_q_up_2"][0], QK), "kv_up": head_tiles(f["w_kv_up_2"][0], NOPE + HV),
        "head_gains": np.concatenate([f["q_head_norm_2"], f["k_head_norm_2"]]).T.copy(),
        "positions": f["positions_2"],
        "branch": np.concatenate([lhs_tiles(f["w_branch_mla_2"][0]), lhs_tiles(f["w_branch_sb_2"][0])], axis=2),
        "proj_out": lhs_tiles(f["w_out_2"][0]),
        "ffn4_in": ffn_in(f["ffn2_w_in_2"][0]), "ffn4_out": ffn_out(f["ffn2_w_out_2"][0]),
        "embed": np.concatenate([lhs_tiles(f["w_ple_gate_2"][0]), lhs_tiles(f["w_ple_proj_2"][0])], axis=2),
        "p": np.ascontiguousarray(f["p_2"][0, 0].T.reshape(2, P, T).transpose(1, 0, 2)).reshape(P, 2 * T),
    }


def kernel(**inputs):
    import concourse.bacc as bacc
    from concourse.bass_utils import run_bass_kernel_spmd

    nc = bacc.Bacc("TRN2", target_bir_lowering=False, num_devices=1)
    arrays = layout(inputs)
    aps = {n: nc.dram_tensor(f"in_{n}", v.shape, mybir.dt.from_np(v.dtype), kind="ExternalInput").ap() for n, v in arrays.items()}
    out = nc.dram_tensor("out", (P, KD * T), F32, kind="ExternalOutput").ap()
    block_program(nc, aps, out)
    r = run_bass_kernel_spmd(nc, [{f"in_{n}": v for n, v in arrays.items()}], core_ids=[0])
    y = r.results[0]["out"]
    return np.ascontiguousarray(y.reshape(P, KD, T).transpose(2, 1, 0)).reshape(1, T, D)
```

```python
from contextlib import ExitStack

import numpy as np
import concourse.bass as bass
from concourse import mybir
from concourse.alu_op_type import AluOpType as ALU

F32 = mybir.dt.float32
F32R = mybir.dt.float32r
I32 = mybir.dt.int32
U32 = mybir.dt.uint32
BF16 = mybir.dt.bfloat16
ACT = mybir.ActivationFunctionType
AX = mybir.AxisListType

P = 128
T = 512
NT = T // P
D = 1024
KD = D // P
DFF = 2816
KF = DFF // P
EPS = 1e-6

HEADS = 4
DK = 128
CH = 64
NC = T // CH
ML_QK = 64
CONV = 4

AH = 8
NOPE, ROPE, QK, HV = 64, 32, 96, 64
KCQ, KCKV = 3, 2

HALF = KF // 2
SLOT = HALF * P
RAW, PAIR = 4, 2
NEVER = -1e30

C_ID, C_ONE, C_LE, C_LT, C_NSUF, C_NONE, C_NGT, C_NGE, C_LEVEL = (i * P for i in range(9))
LEVELS = (1, 2, 4, 8, 16, 32)
C_RESET = C_LEVEL + len(LEVELS) * P
C_SEL = C_RESET + T
C_ROT = C_SEL + HEADS * P
C_FREQ = C_ROT + ROPE
N_CONST = C_FREQ + 1

PARAMS = {}
_n = 0
for _name, _w in (("norm_pre", 3 * KD), ("norm_post", 3 * KD), ("conv_w", CONV * HEADS), ("conv_b", HEADS),
                  ("lb", 2 * HEADS), ("hgrn_norm", HEADS), ("mlstm_norm", HEADS), ("ffn1_norm", KD),
                  ("mix_norm", KD), ("q_latent", KCQ), ("kv_latent", KCKV), ("ffn2_norm", KD), ("ple_norm", KD)):
    PARAMS[_name] = _n
    _n += _w
N_PARAM = _n


CAUSAL = [(i, i * P, P, i * P) for i in range(NT)] + [(0, P, 3 * P, T), (2, 3 * P, P, T + 3 * P), (1, 2 * P, 2 * P, 2 * T)]
N_CAUSAL = 2 * T + 2 * P


def causal_column(i, j):
    if i == j:
        return i * P
    return next(c + j * P - t0 for (n, t0, w, c) in CAUSAL[NT:] if n == i)


SUMMED = [(T, P, 0, 1), (T + P, 2 * T, P, 2), (T + P, 2 * P, T + P, 2), (T + 2 * P, 3 * P, 0, 2),
          (2 * T, 2 * P, T + P, 2), (2 * T + P, 3 * P, 0, 1)]

ROWS = [(3, 0), (2, T), (0, T + 3 * P), (1, 2 * T)]
GATE_AT = 18
LATENT_AT = KF - 2 * (KCQ + KCKV)
LO_AT = 12


def ds(at, n):
    return slice(at, at + n) if isinstance(at, int) else bass.ds(at, n)


class Done:

    def __init__(self, line, count, looped):
        self.line, self.count, self.looped = line, count, looped


class Line:

    def __init__(self, nc, name, credit=0):
        self.sem = nc.alloc_semaphore(name)
        self.count = credit
        self.per = None
        self.turn = None

    def mark(self, ins):
        ins.then_inc(self.sem, 1)
        self.count += 1
        return Done(self, self.count, self.per is not None)

    def ahead(self, k):
        return Done(self, self.start + k, self.per is not None)


class Program:

    def __init__(self, nc):
        self.nc = nc
        self.pe, self.act, self.dve, self.pool = nc.tensor, nc.scalar, nc.vector, nc.gpsimd
        credit = 64
        self.PE, self.ACT, self.DVE = (Line(nc, n, credit) for n in ("pe_done", "act_done", "dve_done"))
        for e, line in ((self.pe, self.PE), (self.act, self.ACT), (self.dve, self.DVE)):
            e.sem_inc(line.sem, credit)
        self.POOL = Line(nc, "pool_done")
        self.lines = [self.PE, self.ACT, self.DVE, self.POOL]
        self.once = False
        self.known = {}

    def wait(self, eng, *dones, back=0):
        if back and self.once:
            return
        most = {}
        queue = list(dones)
        while queue:
            d = queue.pop()
            if isinstance(d, (list, tuple)):
                queue += d
            elif d is not None:
                most[(d.line, d.looped)] = max(most.get((d.line, d.looped), 0), d.count)
        for (line, looped), count in most.items():
            if looped and line.per is not None:
                assert count - back * line.per >= 0
                eng.wait_ge(line.sem, line.turn * line.per + (count - back * line.per))
            else:
                key = (id(eng), line)
                if self.known.get(key, -1) >= count:
                    continue
                eng.wait_ge(line.sem, count)
                if line.per is None:
                    self.known[key] = count

    def loop(self, times, **per):
        return Loop(self, times, per)

    def turns(self, n, body, **per):
        self.once = True
        for line in self.lines:
            line.start = line.count
        body(0)
        self.once = False
        for name, count in per.items():
            line = named_line(self, name)
            assert line.count - line.start >= count, (name, line.count - line.start, count)
        self.W.begin()
        with self.loop(n - 1, **per) as i:
            body(i + 1)
        self.W.finish(n - 1)


class Loop:

    def __init__(self, prog, times, per):
        self.prog, self.times = prog, times
        self.per = {named_line(prog, k): v for k, v in per.items()}

    def __enter__(self):
        self.fori = self.prog.nc.Fori(0, self.times)
        i = self.fori.__enter__()
        for line in self.prog.lines:
            line.start, line.per, line.turn = line.count, self.per.get(line, 0), i
        return i

    def __exit__(self, *exc):
        self.fori.__exit__(*exc)
        for line in self.prog.lines:
            assert exc[0] or line.count - line.start == line.per, (line.count - line.start, line.per)
            line.count = line.start + self.times * line.per
            line.per = line.turn = None


def named_line(prog, name):
    return {"pe": prog.PE, "act": prog.ACT, "dve": prog.DVE, "split": prog.W.split, "used": prog.W.used}[name]


class Weights:

    def __init__(self, prog, at):
        nc = self.nc = prog.nc
        self.p = prog
        self.raw, self.hi, self.lo = [], [], []
        for s in range(RAW):
            self.raw.append(nc.alloc_sbuf_tensor_at(f"w_raw{s}", [P, SLOT], F32, offset=at))
            at += SLOT * 4
        for s in range(PAIR):
            self.hi.append(nc.alloc_sbuf_tensor_at(f"w_hi{s}", [P, SLOT], F32R, offset=at))
            self.lo.append(nc.alloc_sbuf_tensor_at(f"w_lo{s}", [P, SLOT], F32R, offset=at + SLOT * 4))
            at += SLOT * 8
        self.end = at
        self.passed = nc.alloc_semaphore("w_passed")
        self.landed = [nc.alloc_semaphore(f"w_landed{s}") for s in range(RAW)]
        self.n = RAW
        self.split = Line(nc, "w_split", 2 * RAW)
        self.used = Line(nc, "w_used", RAW)
        nc.gpsimd.sem_inc(self.split.sem, 2 * RAW)
        nc.tensor.sem_inc(self.used.sem, RAW)
        prog.lines += [self.split, self.used]
        prog.W = self

    def chunk(self, src, rows=P):
        p, nc, cols = self.p, self.nc, src.shape[-1]
        n = self.n
        r, s = n % RAW, n % PAIR
        looped = self.split.per is not None
        p.wait(nc.sync, Done(self.split, 2 * (n - RAW + 1), looped))
        nc.sync.dma_start(self.raw[r][0:rows, 0:cols], src).then_inc(self.landed[r], 16)
        landed = 16 * (n // RAW)
        if looped:
            nc.gpsimd.wait_ge(self.landed[r], self.split.turn * (16 * self.split.per // (2 * RAW)) + landed)
        else:
            nc.gpsimd.wait_ge(self.landed[r], landed)
        p.wait(nc.gpsimd, Done(self.used, n - PAIR + 1, looped))
        if looped:
            nc.gpsimd.sem_inc(self.passed, 1)
        raw, hi, lo = self.raw[r][0:rows, 0:cols], self.hi[s][0:rows, 0:cols], self.lo[s][0:rows, 0:cols]
        rounded = self.split.mark(nc.gpsimd.tensor_scalar(hi, raw, 1.0, 1.0, ALU.mult, ALU.mult))
        p.wait(nc.gpsimd, rounded)
        rest = self.split.mark(nc.gpsimd.tensor_tensor(lo, raw, hi.bitcast(F32), ALU.subtract))
        self.n += 1
        return self.hi[s], self.lo[s], rest

    def begin(self):
        self.first = self.n

    def finish(self, times):
        body = self.n - self.first
        assert body % RAW == 0
        self.n = self.first + body * times
        assert self.split.count == 2 * self.n and self.used.count == self.n


class Build:
    def __init__(self, nc, a, out):
        self.nc, self.a = nc, a
        self.out = out
        p = self.p = Program(nc)
        at = nc.sbuf_base
        at = (at + 63) // 64 * 64
        self.map_start = at

        def place(name, cols, dt, offset):
            return nc.alloc_sbuf_tensor_at(name, [P, cols], dt, offset=offset)

        self.const = place("const", N_CONST, F32, at); at += N_CONST * 4 + (-N_CONST * 4) % 64
        self.param = place("param", N_PARAM, F32, at); at += N_PARAM * 4 + (-N_PARAM * 4) % 64
        self.misc = place("misc", 256, F32, at); at += 1024
        self.x = place("x", KD * T, F32, at); at += KD * T * 4
        self.w = Weights(p, at)
        at = self.w.end
        self.sums_at = at + 6 * T * 4
        self.sc = []
        for i in range(7):
            self.sc.append(place(f"scratch{i}", T, F32, at)); at += T * 4
        self.scf = place("scratch_f32", 7 * T, F32, at - 7 * T * 4)
        self.uhi = place("u_hi", KD * T, F32R, at)
        self.ulo = place("u_lo", KD * T, F32R, at + KD * T * 4)
        self.y = place("y", KD * T, F32, at)
        self.uf = place("u_f32", 2 * KD * T, F32, at)
        at += 2 * KD * T * 4
        self.big_at = at
        self.hhi = place("hidden_hi", KF * T, F32R, at)
        self.hlo = place("hidden_lo", KF * T, F32R, at + KF * T * 4)
        self.big = place("work", 2 * KF * T, F32, at)
        at += 2 * KF * T * 4
        self.map_end = at
        self.sums_lhs = place("sums_lhs", 2 * P, F32R, self.sums_at)
        self.psum = nc.alloc_psum_tensor("psum", [P, 8 * T], F32)
        self.ps = [self.psum[:, b * T:(b + 1) * T] for b in range(8)]
        self.bank = [None] * 8
        self.spread_used = [None, None]
        self.y_tiles = self.y
        self.vt = [self.tile(self.big, n) for n in (4, 5)]

    def store(self):
        self.nc.sync.wait_ge(self.stored, 16 * KD)

    def cst(self, c, n=P, rows=slice(0, P)):
        return self.const[rows, c:c + n]

    def par(self, name, k, rows=slice(0, P)):
        c = PARAMS[name] + k
        return self.param[rows, c:c + 1]


    def load(self):
        nc, p, a = self.nc, self.p, self.a
        first = nc.alloc_semaphore("first_constants_loaded")
        self.consts_landed = nc.alloc_semaphore("constants_loaded")
        self.x_landed = [nc.alloc_semaphore(f"x{k}_loaded") for k in range(KD)]
        nc.scalar.dma_start(self.const[:, 0:2 * P], a["const"][:, 0:2 * P]).then_inc(first, 16)
        nc.scalar.dma_start(self.param[:, :], a["param"]).then_inc(first, 16)
        for k in range(KD):
            nc.scalar.dma_start(self.tile(self.x, k), a["x"][:, k * T:(k + 1) * T]).then_inc(self.x_landed[k], 16)
        nc.scalar.dma_start(self.const[:, 2 * P:], a["const"][:, 2 * P:]).then_inc(self.consts_landed, 16)
        for e in (nc.tensor, nc.vector, nc.scalar):
            e.wait_ge(first, 32)

    def mm3(self, out, hi, lo, cols, xhi, xlo, first, last):
        pe = self.nc.tensor
        pe.matmul(out, hi[:, cols], xhi, start=first, stop=False)
        pe.matmul(out, lo[:, cols], xhi, start=False, stop=False)
        return pe.matmul(out, hi[:, cols], xlo, start=False, stop=last)

    def token_sums(self, sq, ready, out, rows=P, first_wait=None):
        p, pe = self.p, self.nc.tensor
        p.wait(pe, ready, first_wait)
        for i in range(NT):
            m = pe.matmul(out(i), sq[0:rows, i * P:(i + 1) * P], self.cst(C_ONE, 1, slice(0, rows)), start=True, stop=True)
        return p.PE.mark(m)

    def rsqrt(self, src, dst, ready, n, factor=1.0):
        p, nc = self.p, self.nc
        f = 1.0 / (factor * factor)
        p.wait(nc.vector, ready)
        d = p.DVE.mark(nc.vector.tensor_scalar(dst, src, f / n, f * EPS, ALU.mult, ALU.add))
        p.wait(nc.scalar, d)
        d = p.ACT.mark(nc.scalar.activation(dst, dst, ACT.Sqrt))
        p.wait(nc.vector, d)
        return p.DVE.mark(nc.vector.reciprocal(dst, dst))

    def spread(self, cols, ready, diag, diag_free, bank, rows=P):
        p, nc = self.p, self.nc
        p.wait(nc.vector, ready, diag_free)
        d3 = diag[:, :].rearrange("p (i t) -> p i t", i=NT)
        ident = self.cst(C_ID).unsqueeze(1).broadcast_to([P, NT, P])
        d = p.DVE.mark(nc.vector.tensor_tensor(d3, ident, cols.unsqueeze(2).broadcast_to([P, NT, P]), ALU.mult))
        p.wait(nc.tensor, d, self.bank[bank])
        m = nc.tensor.matmul(self.ps[bank][0:rows, :], self.cst(C_ONE, rows), diag[:, :], start=True, stop=True)
        self.bank[bank] = p.PE.mark(m)
        return self.bank[bank]

    def tile(self, t, k):
        return t[:, k * T:(k + 1) * T]

    def pair_tile(self, k, gain, ready, at=None):
        p, nc = self.p, self.nc
        at = slice(k * T, (k + 1) * T) if at is None else at
        hi, lo, x = self.uhi[:, at], self.ulo[:, at], self.x[:, at]
        h = p.ACT.mark(nc.scalar.activation(hi, x, ACT.Copy, scale=gain))
        p.wait(nc.vector, h, ready)
        l = p.DVE.mark(nc.vector.scalar_tensor_tensor(out=lo, in0=x, scalar=gain, in1=hi.bitcast(F32), op0=ALU.mult,
                                                      op1=ALU.subtract))
        return [h, l]

    def from_stream(self, gain):
        def landed(k):
            for e in (self.nc.scalar, self.nc.vector):
                e.wait_ge(self.x_landed[k], 16)
        self.produce_with(landed, gain)

    def produce_with(self, update, gain):
        p, nc = self.p, self.nc
        rounded = {}

        def front(k):
            ready = update(k)
            at = slice(k * T, (k + 1) * T)
            p.wait(nc.scalar, ready)
            h = p.ACT.mark(nc.scalar.activation(self.uhi[:, at], self.x[:, at], ACT.Copy, scale=gain(k)))
            rounded[k] = h, ready

        def produce(k):
            if k == 0:
                front(0)
            if k + 1 < KD:
                front(k + 1)
            h, ready = rounded[k]
            at = slice(k * T, (k + 1) * T)
            p.wait(nc.vector, h, ready)
            l = p.DVE.mark(nc.vector.scalar_tensor_tensor(out=self.ulo[:, at], in0=self.x[:, at], scalar=gain(k),
                                                          in1=self.uhi[:, at].bitcast(F32), op0=ALU.mult, op1=ALU.subtract))
            return self.squared(k, ready), [h, l]
        self.produce, self.sq_used = produce, [None, None]

    def squared(self, k, ready):
        p, nc = self.p, self.nc
        sq = self.sc[4 + k % 2]
        p.wait(nc.scalar, ready, self.sq_used[k % 2])
        return sq, p.ACT.mark(nc.scalar.activation(sq[:, :], self.tile(self.x, k), ACT.Square))

    def first_chunk(self, bank, hi, lo, last=True):
        p = self.p
        for k in range(KD):
            if self.produce:
                (sq, squared), ready = self.produce(k)
                p.wait(self.nc.tensor, ready)
            elif k == KD - 1:
                p.wait(self.nc.tensor, self.last_pair)
            m = self.mm3(bank, hi, lo, slice(k * P, (k + 1) * P), self.tile(self.uhi, k), self.tile(self.ulo, k), k == 0, k == KD - 1)
            if k == KD - 1:
                d = self.w.used.mark(m) if last else None
            if self.produce:
                p.wait(self.nc.tensor, squared, self.bank[4])
                self.sums = self.sq_used[k % 2] = p.PE.mark(
                    self.nc.tensor.matmul(self.ps[4], self.cst(C_ONE), sq[:, :], start=k == 0, stop=k == KD - 1))
        return d

    def factor(self):
        p, nc = self.p, self.nc
        act, dve = nc.scalar, nc.vector
        self.settle(dve)
        self.rb = self.sc[0][:, :]
        if self.produce:
            self.settle(act)
            self.bank[4] = self.rsqrt(self.ps[4], self.rb, self.sums, D)
        else:
            r = self.misc[:, NT:2 * NT]
            self.sums = self.token_sums(self.sc[5], self.squares_added, self.col, first_wait=self.bank[4])
            d = self.rsqrt(self.ps[4][:, 0:NT], r, self.sums, D)
            self.bank[4] = d
            rb = self.spread(r, d, self.sc[1], None, 5)
            p.wait(act, rb)
            self.bank[5] = p.ACT.mark(act.copy(self.rb, self.ps[5]))
        self.settle(act, dve)
        self.produce = None


    def ffn(self, w_in, w_out, post, next_gain, then=None):
        p, nc = self.p, self.nc
        pe, act, dve = nc.tensor, nc.scalar, nc.vector
        ps, W = self.ps, self.w
        sg, hm = self.sc[1:3], self.sc[3:5]
        p.wait(pe, self.bank[0:4])

        def turn(i):
            for j in range(2):
                for half in range(2):
                    b = 2 * j + half
                    hi, lo, ready = W.chunk(w_in[i * 4 + b])
                    p.wait(pe, ready)
                    if p.once and b == 0:
                        product = self.first_chunk(ps[b], hi, lo)
                        self.factor()
                        for line in (p.ACT, p.DVE):
                            line.start = line.count
                    else:
                        p.wait(pe, p.DVE.ahead(4 * j + 1 + half), back=1)
                        for k in range(KD):
                            m = self.mm3(ps[b], hi, lo, slice(k * P, (k + 1) * P), self.tile(self.uhi, k),
                                         self.tile(self.ulo, k), k == 0, k == KD - 1)
                        product = W.used.mark(m)
                    to = (sg, hm)[half][j][:, :]
                    p.wait(dve, product)
                    if half == 0:
                        p.wait(dve, p.DVE.ahead(4 * j + 3), back=1)
                    else:
                        p.wait(dve, p.ACT.ahead(2 * j + 2), p.DVE.ahead(4 * j + 4), back=1)
                    normed = p.DVE.mark(dve.tensor_tensor(to, ps[b], self.rb, ALU.mult))
                    if half == 0:
                        p.wait(act, normed)
                        p.ACT.mark(act.activation(to, to, ACT.Silu))
                p.wait(dve, normed, p.ACT.ahead(2 * j + 1))
                d = p.DVE.mark(dve.tensor_tensor(hm[j][:, :], hm[j][:, :], sg[j][:, :], ALU.mult))
                at = ds((i * 2 + j) * T, T)
                p.wait(act, d)
                d = p.ACT.mark(act.copy(self.hhi[:, at], hm[j][:, :]))
                p.wait(dve, d)
                p.DVE.mark(dve.tensor_tensor(self.hlo[:, at], hm[j][:, :], self.hhi[:, at].bitcast(F32), ALU.subtract))

        p.turns(KF // 2, turn, act=4, dve=8, split=8, used=4)
        if then:
            then()
        free = Done(p.DVE, p.DVE.count - 6, False)
        hidden = [Done(p.ACT, p.ACT.count, False), Done(p.DVE, p.DVE.count, False)]
        self.into_stream(w_out, KD // 2, 2, 2, HALF, self.hhi, self.hlo, 0.5, post, next_gain, (free, hidden, HALF))

    def into_stream(self, w, turns, n_tiles, n_chunks, lhs, xhi, xlo, scale, post, next_gain, inputs=None):
        p, nc = self.p, self.nc
        pe, act, dve = nc.tensor, nc.scalar, nc.vector
        ps, W = self.ps, self.w
        acc, sq = self.sc[5], self.sc[6]
        if inputs:
            p.wait(pe, inputs[0])
        else:
            self.settle(pe)
        self.settle(act, dve)
        zeroed = p.DVE.mark(dve.memset(acc[:, :], 0.0))
        p.wait(act, zeroed)
        rooted = p.ACT.mark(act.activation(acc[:, 0:1], acc[:, 0:1], ACT.Sqrt))
        p.wait(dve, zeroed, rooted)
        W.begin()
        per = n_tiles * n_chunks
        na, nd = (1, 2) if post else (2, 3)
        with p.loop(turns, act=na * n_tiles, dve=nd * n_tiles, split=2 * per, used=per) as i:
            for j in range(n_tiles):
                out_done = p.DVE.ahead(nd * j + 1)
                for part in range(n_chunks):
                    hi, lo, ready = W.chunk(w[i * per + (n_chunks * j + part)])
                    p.wait(pe, ready)
                    if part == 0:
                        p.wait(pe, out_done, back=1)
                    for k in range(lhs):
                        kk = part * lhs + k
                        if inputs and j == 0 and kk == inputs[2]:
                            p.wait(pe, inputs[1])
                        m = self.mm3(ps[j], hi, lo, slice(k * P, (k + 1) * P), self.tile(xhi, kk), self.tile(xlo, kk),
                                     kk == 0, kk == n_chunks * lhs - 1)
                    product = W.used.mark(m)
                at = ds((i * n_tiles + j) * T, T)
                p.wait(dve, product)
                if post:
                    to = self.y_tiles[:, at]
                    p.DVE.mark(dve.tensor_copy(to, ps[j]))
                else:
                    to = self.x[:, at]
                    p.DVE.mark(dve.scalar_tensor_tensor(out=to, in0=ps[j], scalar=scale, in1=to, op0=ALU.mult, op1=ALU.add))
                before = (p.DVE.ahead(nd * n_tiles), 1) if j == 0 else (p.DVE.ahead(nd * j), 0)
                p.wait(act, out_done)
                act.sem_inc(W.passed, 1)
                if not post:
                    self.pair_tile(None, self.gain_at(next_gain, i * n_tiles + j), out_done, at=at)
                squared = p.ACT.mark(act.activation(sq[:, :], to, ACT.Square))
                p.wait(dve, before[0], back=before[1])
                p.wait(dve, squared)
                p.DVE.mark(dve.tensor_tensor(acc[:, :], acc[:, :], sq[:, :], ALU.add))
        W.finish(turns)
        done = [Done(p.ACT, p.ACT.count, False), Done(p.DVE, p.DVE.count, False)]
        self.produce = None
        if post:
            self.bank[0:4] = [done] * 4
            self.sums = self.token_sums(acc, done, self.col, first_wait=self.bank[4])
            self.post_norm(post, scale, next_gain)
        else:
            self.bank[0:4] = [Done(p.DVE, p.DVE.count - 2, False)] * 4
            self.last_pair = Done(p.DVE, p.DVE.count - 1, False)
            self.squares_added = done

    def gain_at(self, name, k):
        name, first = name
        return self.param[:, ds(k + (PARAMS[name] + first), 1)]

    def post_norm(self, gain, factor, next_gain):
        p, nc = self.p, self.nc
        act, dve = nc.scalar, nc.vector
        r = self.misc[:, NT:2 * NT]
        self.settle(dve, act)
        s, d = self.ps[4][:, 0:NT], self.sums
        d = self.rsqrt(s, r, d, D, factor)
        self.bank[4] = d
        rb = self.spread(r, d, self.sc[6], None, 5)
        p.wait(dve, rb)
        y_tiles = self.y_tiles
        free = [None] * 2

        def update(k):
            t = self.sc[1 + k % 2]
            p.wait(dve, free[k % 2])
            d = p.DVE.mark(dve.scalar_tensor_tensor(out=t[:, :], in0=self.tile(y_tiles, k), scalar=gain(k),
                                                    in1=self.ps[5], op0=ALU.mult, op1=ALU.mult))
            self.bank[5] = d
            p.wait(nc.gpsimd, d)
            free[k % 2] = p.POOL.mark(nc.gpsimd.tensor_tensor(self.tile(self.x, k), self.tile(self.x, k), t[:, :], ALU.add))
            return free[k % 2]
        self.produce_with(update, lambda k: self.gain_at(next_gain, k))

    def settle(self, *engines):
        p = self.p
        for e in engines:
            p.wait(e, [Done(line, line.count, False) for line in (p.PE, p.ACT, p.DVE, p.W.used)])


    def project(self, w, first, turns, dst, func=None, then=None, between=iter(())):
        p, nc = self.p, self.nc
        pe, act, dve = nc.tensor, nc.scalar, nc.vector
        W, ps = self.w, self.ps
        p.wait(pe, self.bank[0:4])

        def turn(i):
            for j in range(4):
                hi, lo, ready = W.chunk(w[i * 4 + (first + j)])
                p.wait(pe, ready)
                if p.once and j == 0 and self.fresh:
                    product = self.first_chunk(ps[j], hi, lo)
                    self.factor()
                    self.fresh = False
                    if then:
                        then()
                    for line in (p.ACT, p.DVE):
                        line.start = line.count
                else:
                    p.wait(pe, p.DVE.ahead(j + 1), back=1)
                    for k in range(KD):
                        m = self.mm3(ps[j], hi, lo, slice(k * P, (k + 1) * P), self.tile(self.uhi, k),
                                     self.tile(self.ulo, k), k == 0, k == KD - 1)
                    product = W.used.mark(m)
                to = dst[:, ds((i * 4 + j) * T, T)]
                p.wait(dve, product)
                d = p.DVE.mark(dve.tensor_tensor(to, ps[j], self.rb, ALU.mult))
                if func:
                    p.wait(act, d)
                    p.ACT.mark(act.activation(to, to, func))
                if p.once:
                    next(between, None)

        p.turns(turns, turn, act=4 if func else 0, dve=4, split=8, used=4)
        self.bank[0:4] = [[Done(p.ACT, p.ACT.count, False), Done(p.DVE, p.DVE.count, False)]] * 4

    def one_chunk(self, src, bank, x_pair, tiles, cols=P, out=None, ready=None, off=0):
        p = self.p
        hi, lo, split = self.w.chunk(src)
        p.wait(self.nc.tensor, split, self.bank[bank], ready)
        out = self.ps[bank][0:cols, :] if out is None else out
        for k in range(tiles):
            m = self.mm3(out, hi, lo, slice(off + k * cols, off + (k + 1) * cols), x_pair[0](k), x_pair[1](k), k == 0, k == tiles - 1)
        d = self.w.used.mark(m)
        self.bank[bank] = d
        return d

    def split_pair(self, src, hi, lo, ready, eng=None):
        p, nc = self.p, self.nc
        p.wait(nc.scalar, ready)
        h = p.ACT.mark(nc.scalar.copy(hi, src))
        p.wait(nc.vector, h, ready)
        l = p.DVE.mark(nc.vector.tensor_tensor(lo, src, hi.bitcast(F32), ALU.subtract))
        return [h, l]

    def U(self, n):
        return self.uf[:, n * 4 * T:(n + 1) * 4 * T]

    def B(self, n):
        return self.big[:, n * 4 * T:(n + 1) * 4 * T]

    def turn_tiles(self, src, n, bank0, dst, ready, rows=slice(0, P), cols=P):
        p, nc = self.p, self.nc
        p.wait(nc.tensor, ready, self.bank[bank0:bank0 + (n * cols + T - 1) // T])
        base = bank0 * T
        for q in range(n):
            m = nc.tensor.transpose(self.psum[:, base + q * cols:base + (q + 1) * cols],
                                    src[rows, q * P:(q + 1) * P], self.const[rows, C_ID + rows.start:C_ID + rows.stop])
        d = p.PE.mark(m)
        p.wait(nc.scalar, d)
        d = p.ACT.mark(nc.scalar.copy(dst, self.psum[:, base:base + n * cols]))
        for b in range(bank0, bank0 + (n * cols + T - 1) // T):
            self.bank[b] = d
        return d


    def gated_mixer(self):
        p, nc, a = self.p, self.nc, self.a
        self.gate_bias = self.misc[0:HEADS, 128:130]
        biased = nc.alloc_semaphore("gate_bias_loaded")
        nc.scalar.dma_start(self.gate_bias, a["gate_bias"]).then_inc(biased, 16)
        nc.vector.wait_ge(biased, 16)
        for e in (nc.tensor, nc.vector, nc.scalar):
            e.wait_ge(self.consts_landed, 16)
        self.fresh = True
        self.project(a["mix_in"], 0, 2, self.big)
        self.settle(nc.scalar, nc.vector, nc.tensor)
        self.gate_rows = self.sc[5]
        tiles = list(range(8, 28))
        self.to_fill = [(n, self.tile(self.big, n)) for n in tiles]
        self.to_fill.insert(8, (28, self.gate_rows[:, :]))
        self.filled, self.in_psum, self.n_fill = {}, [], 0
        self.mixed = []
        self.hgrn2()
        self.mlstm()
        self.y_tiles = self.big[:, 12 * T:(12 + KD) * T]
        inputs = ([self.mixed[0:HEADS], self.bank[0:4]], self.mixed[HEADS:], HEADS)
        self.into_stream(a["mix_out"], 2, 4, 1, KD, self.uhi, self.ulo, 1.0, lambda k: self.par("norm_post", KD + k),
                         ("norm_pre", 2 * KD), inputs)

    def fill(self, n):
        p, pe = self.p, self.nc.tensor
        for _ in range(n):
            index, to = self.to_fill[self.n_fill]
            b = 4 + self.n_fill % 4
            self.n_fill += 1
            self.leave_psum(3)
            hi, lo, split = self.w.chunk(self.a["mix_in"][index])
            p.wait(pe, split, self.bank[b])
            for k in range(KD):
                m = self.mm3(self.ps[b], hi, lo, slice(k * P, (k + 1) * P), self.tile(self.uhi, k), self.tile(self.ulo, k),
                             k == 0, k == KD - 1)
            self.in_psum.append((index, b, to, self.w.used.mark(m)))

    def leave_psum(self, keep):
        p, dve = self.p, self.nc.vector
        while len(self.in_psum) > keep:
            index, b, to, product = self.in_psum.pop(0)
            p.wait(dve, product)
            self.bank[b] = self.filled[index] = p.DVE.mark(dve.tensor_tensor(to, self.ps[b], self.rb, ALU.mult))

    def hgrn2(self):
        p, nc = self.p, self.nc
        pe, act, dve = nc.tensor, nc.scalar, nc.vector
        A, V, PE = p.ACT.mark, p.DVE.mark, p.PE.mark
        q, f, v_in, gate = self.B(0), self.B(1), self.B(2), self.B(3)
        logf, G = self.B(7), self.B(8)
        S = self.scf[:, T:5 * T]
        sig = A(act.activation(f, f, ACT.Sigmoid))
        q_done = A(act.activation(q, q, ACT.Silu))
        H = HEADS
        m = self.misc
        l0, l1 = (self.param[:, PARAMS["lb"] + H * k:PARAMS["lb"] + H * (k + 1)] for k in range(2))
        top, e, lb, rest = m[:, 32:36], m[:, 36:44], m[:, 44:48], m[:, 48:52]
        d = V(dve.tensor_tensor(top, l0, l1, ALU.max)); p.wait(dve, d)
        V(dve.tensor_tensor(e[:, 0:H], l0, top, ALU.subtract))
        d = V(dve.tensor_tensor(e[:, H:2 * H], l1, top, ALU.subtract)); p.wait(act, d)
        d = A(act.activation(e, e, ACT.Exp)); p.wait(dve, d)
        d = V(dve.tensor_tensor(lb, e[:, 0:H], e[:, H:2 * H], ALU.add)); p.wait(dve, d)
        d = V(dve.reciprocal(lb, lb)); p.wait(dve, d)
        d = V(dve.tensor_tensor(lb, lb, e[:, 0:H], ALU.mult)); p.wait(dve, d)
        d = V(dve.tensor_scalar(rest, lb, -1.0, 1.0, ALU.mult, ALU.add))
        self.fill(2)
        p.wait(dve, d, sig)
        for h in range(H):
            t = slice(h * T, (h + 1) * T)
            d = V(dve.tensor_scalar(logf[:, t], f[:, t], rest[:, h:h + 1], lb[:, h:h + 1], ALU.mult, ALU.add))
        p.wait(dve, d)
        k = f
        k_done = V(dve.tensor_scalar(k, logf, -1.0, 1.0, ALU.mult, ALU.add))
        p.wait(act, k_done)
        logf_done = A(act.activation(logf, logf, ACT.Ln))
        self.fill(1)
        work = (self.B(9), self.B(10), self.B(7))
        z = V(dve.memset(S, 0.0))
        p.wait(dve, q_done, k_done)
        multiplied = {0: V(dve.tensor_tensor(work[0], q, k, ALU.mult))}
        p.wait(dve, logf_done)
        for h in range(H):
            t = slice(h * T, (h + 1) * T)
            G_done = V(dve.tensor_tensor_scan(G[:, t], self.cst(C_RESET, T), logf[:, t], 0.0, ALU.mult, ALU.add))
        p.wait(dve, G_done, z)
        self.leave_psum(1)
        self.fill(2)
        exps, scored, copied = {}, {}, {}
        last = len(LEVELS)
        G3 = G.rearrange("p (c t) -> p c t", t=CH)
        e_end = m[:, 64:64 + H * NC]

        def cut(x, half):
            return x.rearrange("p (c two h) -> p c two h", two=2, h=half)

        def exponents(n):
            w = work[n % 3]
            p.wait(dve, scored.get(n - 3), G_done)
            if n <= last:
                half = LEVELS[n - 1]
                g4, w4 = cut(G, half), cut(w, half)
                g_end = g4[:, :, 0, half - 1:half].broadcast_to([P, H * T // (2 * half), half])
                V(dve.tensor_tensor(w4[:, :, 0, :], g_end, g4[:, :, 0, :], ALU.subtract))
                d = V(dve.tensor_tensor(w4[:, :, 1, :], g4[:, :, 1, :], g_end, ALU.subtract))
            elif n == last + 1:
                ends.append(A(act.activation(e_end, G3[:, :, CH - 1], ACT.Exp)))
                d = V(dve.tensor_tensor(w.rearrange("p (c t) -> p c t", t=CH), G3[:, :, CH - 1:CH].broadcast_to([P, H * NC, CH]),
                                        G3, ALU.subtract))
            else:
                d, w_from = scored[n - 3], G
            p.wait(act, d)
            exps[n] = A(act.activation(w, w if n <= last + 1 else w_from, ACT.Exp))

        def multiply(n):
            w = work[n % 3]
            p.wait(dve, exps[n])
            if n <= last:
                half = LEVELS[n - 1]
                w4, q4, k4 = cut(w, half), cut(q, half), cut(k, half)
                V(dve.tensor_tensor(w4[:, :, 0, :], w4[:, :, 0, :], k4[:, :, 0, :], ALU.mult))
                multiplied[n] = V(dve.tensor_tensor(w4[:, :, 1, :], w4[:, :, 1, :], q4[:, :, 1, :], ALU.mult))
            else:
                multiplied[n] = V(dve.tensor_tensor(w, w, k if n == last + 1 else q, ALU.mult))

        def score(n):
            w = work[n % 3]
            p.wait(pe, multiplied[n], self.bank[0:4])
            for s in range(4 * NT):
                t = slice(s * P, (s + 1) * P)
                mm = pe.matmul(self.psum[:, s * P:(s + 1) * P], w[:, t], w[:, t] if n else self.cst(C_ONE), start=True, stop=True)
            scored[n] = PE(mm)

        def keep(n):
            p.wait(dve, scored[n], copied.get(n - 1))
            mask = self.cst(C_LEVEL + (n - 1) * P if n else C_ID).bitcast(U32).unsqueeze(1).broadcast_to([P, 4 * NT, P])
            ps3 = self.psum[:, 0:4 * T].rearrange("p (s t) -> p s t", t=P)
            copied[n] = V(dve.copy_predicated(S.rearrange("p (s t) -> p s t", t=P), mask, ps3))
            self.bank[0:4] = [copied[n]] * 4

        ends = []
        conv = self.convolve()
        exponents(1)
        for n in range(last + 1):
            self.leave_psum(0)
            if n:
                keep(n - 1)
            exponents(n + 2)
            multiply(n + 1)
            if n > 3:
                next(conv)
            self.fill(2 if 0 < n else 1)
            score(n)
            if n == 3:
                p.wait(act, self.filled[15])
                gate_done = A(act.activation(gate, gate, ACT.Silu))
        keep(last)
        multiply(last + 2)
        kw, qe = work[(last + 1) % 3], work[(last + 2) % 3]
        e_done, qe_done = ends[0], multiplied[last + 2]
        kt, v = self.B(9), self.B(8)
        p.wait(act, scored[last])
        kt_done = self.turn_tiles(kw, 4 * NT, 0, kt, [multiplied[last + 1], scored[last]])
        self.fill(1)
        p.wait(act, multiplied[last + 1])
        v_done = self.turn_tiles(v_in, 4 * NT, 0, v, self.filled[11])
        self.fill(1)
        state = lambda c, h: self.big[:, ((c - 1) * H + h) * P:((c - 1) * H + h + 1) * P]
        p.wait(pe, kt_done, v_done)
        made = []
        for c in range(NC - 1):
            b = c % 4
            rows = slice((c % 2) * CH, (c % 2 + 1) * CH)
            p.wait(pe, self.bank[b])
            for h in range(H):
                t = slice((h * NT + c // 2) * P, (h * NT + c // 2 + 1) * P)
                mm = pe.matmul(self.ps[b][:, h * P:(h + 1) * P], kt[rows, t], v[rows, t], start=True, stop=True)
            d = PE(mm)
            if c == 2:
                self.leave_psum(0)
            p.wait(dve, d)
            if c == 0:
                p.wait(dve, qe_done)
                d = V(dve.tensor_copy(self.big[:, 0:T], self.ps[b]))
            else:
                p.wait(dve, made[-1], e_done)
                for h in range(H):
                    d = V(dve.scalar_tensor_tensor(out=state(c + 1, h), in0=state(c, h), scalar=e_end[:, h * NC + c:h * NC + c + 1],
                                                   in1=self.ps[b][:, h * P:(h + 1) * P], op0=ALU.mult, op1=ALU.add))
            made.append(d)
            self.bank[b] = d
        self.fill(1)
        assert self.n_fill == len(self.to_fill)
        p.wait(pe, copied[last], qe_done)
        out = self.B(2)
        self.sq = (self.sc[0], self.sc[6])
        self.settle(act)
        stats, squares = [], []
        for h in range(H):
            b = (5, 7)[h % 2]
            p.wait(pe, self.bank[b])
            for i in range(NT):
                t = slice((h * NT + i) * P, (h * NT + i + 1) * P)
                mm = pe.matmul(self.ps[b][:, i * P:(i + 1) * P], v[:, t], S[:, t], start=True, stop=False)
                for c in (2 * i, 2 * i + 1):
                    if c:
                        p.wait(pe, made[c - 1])
                        mm = pe.matmul(self.ps[b][:, c * CH:(c + 1) * CH], state(c, h),
                                       qe[:, h * T + c * CH:h * T + (c + 1) * CH], start=False, stop=c % 2 == 1)
            d = PE(mm)
            p.wait(dve, d, v_done)
            t = slice(h * T, (h + 1) * T)
            o_done = V(dve.tensor_copy(out[:, t], self.ps[b]))
            self.bank[b] = o_done
            if h == 0:
                self.leave_psum(0)
                o_done = [o_done, self.filled[27]]
            squares.append(self.head_squares(out[:, t], h, o_done, stats[h - 2] if h > 1 else self.qk_done))
            if h:
                stats.append(self.head_sums(h - 1, squares[h - 1]))
            if h == 0:
                next(conv)
                rows_done = self.gate_sequences()
            next(rows_done, None)
        stats.append(self.head_sums(HEADS - 1, squares[-1]))
        for _ in rows_done:
            pass
        self.head_factors(stats[-1])
        self.hgrn_apply = lambda h, bank: self.head_apply(h, bank, out, "hgrn_norm", gate, self.B(0), gate_done)

    def head_squares(self, src, h, ready, sq_free):
        p, act = self.p, self.nc.scalar
        p.wait(act, ready, sq_free)
        return p.ACT.mark(act.activation(self.sq[h % 2][:, :], src, ACT.Square))

    def head_sums(self, h, squared):
        return self.token_sums(self.sq[h % 2], [squared], lambda i: self.ps[6][:, h * NT + i:h * NT + i + 1],
                               first_wait=self.bank[6])

    def head_factors(self, ready, scale=None):
        p, dve = self.p, self.nc.vector
        n = HEADS * NT
        r = self.misc[:, 32:32 + n]
        if scale is None:
            d = self.rsqrt(self.ps[6][:, 0:n], r, ready, P)
        else:
            p.wait(dve, ready)
            d = p.DVE.mark(dve.tensor_tensor(r, self.ps[6][:, 0:n], scale, ALU.mult))
            p.wait(dve, d)
            d = p.DVE.mark(dve.tensor_tensor(r, r, scale, ALU.mult))
            d = self.rsqrt(r, r, d, P)
            p.wait(dve, d)
            d = p.DVE.mark(dve.tensor_tensor(r, r, scale, ALU.mult))
        self.bank[6] = self.factors_done = d

    def head_spread(self, h, bank):
        r = self.misc[:, 32 + h * NT:32 + (h + 1) * NT]
        self.spread_used[h % 2] = self.spread(r, self.factors_done, self.sc[2 + h % 2], self.spread_used[h % 2], bank)

    def head_apply(self, h, bank, o, gain, gate, dst, gate_done):
        p, dve = self.p, self.nc.vector
        t = slice(h * T, (h + 1) * T)
        p.wait(dve, self.spread_used[h % 2], gate_done)
        e = p.DVE.mark(dve.scalar_tensor_tensor(out=dst[:, t], in0=o[:, t], scalar=self.par(gain, h), in1=self.ps[bank],
                                                op0=ALU.mult, op1=ALU.mult))
        self.bank[bank] = e
        p.wait(dve, e)
        e = p.DVE.mark(dve.tensor_tensor(dst[:, t], dst[:, t], gate[:, t], ALU.mult))
        self.mixed.append([self.round(dst[:, t], self.tile(self.uhi, len(self.mixed)), e), e])

    def round(self, src, hi, ready):
        self.p.wait(self.nc.scalar, ready)
        return self.p.ACT.mark(self.nc.scalar.copy(hi, src))

    def rest(self, src, k, h):
        p, dve = self.p, self.nc.vector
        p.wait(dve, self.mixed[k])
        self.mixed[k].append(p.DVE.mark(dve.tensor_tensor(self.tile(self.ulo, k), src[:, h * T:(h + 1) * T],
                                                          self.tile(self.uhi, k).bitcast(F32), ALU.subtract)))

    def convolve(self):
        p, nc = self.p, self.nc
        act, dve = nc.scalar, nc.vector
        x = self.qk = self.B(4)
        yt = self.sc[6][:, :]
        self.qk_done = []
        for n in range(4):
            xt = self.tile(x, n)
            cw = lambda tap: self.par("conv_w", tap * 4 + n)
            p.wait(dve, self.filled[16 + n], self.qk_done)
            d = p.DVE.mark(dve.tensor_scalar(yt, xt, cw(CONV - 1), self.par("conv_b", n), ALU.mult, ALU.add))
            for lag in range(1, CONV):
                p.wait(dve, d)
                d = p.DVE.mark(dve.scalar_tensor_tensor(out=yt[:, lag:T], in0=xt[:, 0:T - lag], scalar=cw(CONV - 1 - lag),
                                                        in1=yt[:, lag:T], op0=ALU.mult, op1=ALU.add))
            p.wait(act, d)
            self.qk_done.append(p.ACT.mark(act.activation(xt, yt, ACT.Silu)))
            yield

    def gate_sequences(self):
        p, nc = self.p, self.nc
        act, dve = nc.scalar, nc.vector
        A, V = p.ACT.mark, p.DVE.mark
        H, gate_bias = HEADS, self.gate_bias
        li, z, lf, B, w, M, ones = (self.tile(self.uf, n)[0:H, :] for n in (4, 5, 6, 7, KD + 4, KD + 5, KD + 6))
        self.rows = w, z, M
        p.wait(dve, self.filled[27])
        V(dve.tensor_scalar(li, self.gate_rows[0:H, :], gate_bias[:, 0:1], None, ALU.add))
        z_done = V(dve.tensor_scalar(z, self.gate_rows[32:32 + H, :], gate_bias[:, 1:2], None, ALU.add))
        one = V(dve.memset(ones, 1.0))
        p.wait(act, z_done)
        d = A(act.activation(lf, z, ACT.Abs)); p.wait(act, d)
        d = A(act.activation(lf, lf, ACT.Exp, scale=-1.0)); p.wait(act, d)
        d = A(act.activation(lf, lf, ACT.Ln, bias=1.0))
        self.mo_done = A(act.activation(self.B(6), self.B(6), ACT.Sigmoid))
        yield
        p.wait(dve, d, one)
        d = V(dve.scalar_tensor_tensor(out=lf, in0=z, scalar=0.0, in1=lf, op0=ALU.min, op1=ALU.subtract)); p.wait(dve, d)
        d = V(dve.tensor_tensor_scan(B, ones, lf, 0.0, ALU.mult, ALU.add))
        yield
        p.wait(dve, d)
        d = V(dve.tensor_tensor(w, li, B, ALU.subtract)); p.wait(dve, d)
        self.M_done = V(dve.tensor_tensor_scan(M, ones, w, 0.0, ALU.mult, ALU.max))
        yield
        p.wait(dve, self.M_done)
        d = V(dve.tensor_tensor(z, B, M, ALU.add)); p.wait(act, d)
        self.em_done = A(act.activation(z, z, ACT.Exp, scale=-1.0))

    def mlstm(self):
        p, nc = self.p, self.nc
        pe, act, dve = nc.tensor, nc.scalar, nc.vector
        A, V, PE = p.ACT.mark, p.DVE.mark, p.PE.mark
        H, m = HEADS, self.misc
        v_in, gate = self.B(5), self.B(6)
        v, qk = self.B(9), self.qk
        w, z, M = self.rows
        v_done = self.turn_tiles(v_in, 4 * NT, 0, v, self.filled[23])
        p.wait(pe, self.em_done, self.bank[6])
        for n, row in ((0, w), (1, z)):
            for i in range(NT):
                mm = pe.transpose(self.ps[6][:, 32 + (n * NT + i) * H:32 + (n * NT + i + 1) * H], row[:, i * P:(i + 1) * P],
                                  self.const[0:H, C_ID:C_ID + H])
        d = PE(mm)
        cols = m[:, 64:64 + 2 * NT * H]
        p.wait(act, d)
        cols_done = A(act.copy(cols, self.ps[6][:, 32:32 + 2 * NT * H]))
        self.bank[6] = cols_done
        w_col = lambda i, h: cols[:, i * H + h:i * H + h + 1]
        out = self.B(7)
        sum_w = self.ps[6][:, 128:128 + H * NT]
        stats = []
        p.wait(pe, self.qk_done, self.M_done, v_done)
        self.settle(act, dve)
        pair = (self.B(1), self.B(8))
        pv = [None, None]
        decayed, products, weighted, squares = {}, {}, {}, []

        def decays(h):
            E = pair[h % 2]
            rows = slice((h % 2) * ML_QK, (h % 2 + 1) * ML_QK)
            qh, kh = self.tile(qk, h // 2)[rows, :], self.tile(qk, 2 + h // 2)[rows, :]
            p.wait(pe, self.bank[7])
            rb = PE(pe.matmul(self.ps[7], self.const[0:H, C_SEL + h * P:C_SEL + (h + 1) * P], M, start=True, stop=True))
            p.wait(dve, rb, cols_done, pv[h % 2])
            for (i, t0, n, c) in CAUSAL:
                d = V(dve.tensor_scalar(E[:, c:c + n], self.ps[7][:, t0:t0 + n], w_col(i, h), 0.0, ALU.subtract, ALU.max))
            self.bank[7] = d
            p.wait(act, d)
            decayed[h] = A(act.activation(E[:, 0:N_CAUSAL], E[:, 0:N_CAUSAL], ACT.Exp, scale=-1.0))
            b0 = 3 * (h % 2)
            products[h] = self.causal_product(b0, lambda i: kh[:, i * P:(i + 1) * P], lambda t0, n: qh[:, t0:t0 + n], None)

        def weigh(h):
            E, b0 = pair[h % 2], 3 * (h % 2)
            p.wait(dve, decayed[h], products[h])
            d = V(dve.scalar_tensor_tensor(out=E[:, 0:N_CAUSAL], in0=self.psum[:, b0 * T:b0 * T + N_CAUSAL], scalar=ML_QK ** -0.5,
                                           in1=E[:, 0:N_CAUSAL], op0=ALU.mult, op1=ALU.mult))
            self.bank[b0:b0 + 3] = [d] * 3
            p.wait(dve, d)
            weighted[h] = self.mask_diagonals(E, C_LE)

        decays(0)
        weigh(0)
        decays(1)
        for h in range(H):
            E, b0 = pair[h % 2], 3 * (h % 2)
            p.wait(pe, weighted[h], self.bank[b0], self.bank[6])
            nd = PE(self.causal_values(self.ps[b0], lambda i: v[:, (h * NT + i) * P:(h * NT + i + 1) * P], E))
            for j in range(NT):
                for i in range(j + 1):
                    c = causal_column(i, j)
                    mm = pe.matmul(sum_w[:, h * NT + j:h * NT + j + 1], E[:, c:c + P], self.cst(C_ONE, 1), start=i == 0, stop=i == j)
            pv[h % 2] = PE(mm)
            self.head_spread(h, b0 + 1)
            if h + 1 < H:
                weigh(h + 1)
            p.wait(dve, nd)
            t = slice(h * T, (h + 1) * T)
            o_done = V(dve.tensor_copy(out[:, t], self.ps[b0]))
            self.bank[b0] = o_done
            if h == 0:
                self.settle(act)
            squares.append(self.head_squares(out[:, t], h, o_done, stats[h - 2] if h > 1 else None))
            if h:
                stats.append(self.head_sums(h - 1, squares[h - 1]))
            self.hgrn_apply(h, b0 + 1)
            if h:
                self.rest(self.B(0), h - 1, h - 1)
            if h + 2 < H:
                decays(h + 2)
        self.rest(self.B(0), H - 1, H - 1)
        stats.append(self.head_sums(H - 1, squares[-1]))
        scale = m[:, 96:96 + H * NT]
        neg = m[:, 112:112 + H * NT]
        self.settle(dve)
        d = V(dve.tensor_scalar(neg, sum_w, -1.0, None, ALU.mult)); p.wait(dve, d)
        d = V(dve.tensor_tensor(scale, sum_w, neg, ALU.max)); p.wait(dve, d)
        em = cols[:, NT * H:2 * NT * H].rearrange("p (i h) -> p h i", h=H)
        s3 = scale.rearrange("p (h i) -> p h i", h=H)
        d = V(dve.tensor_tensor(s3, s3, em, ALU.max)); p.wait(dve, d)
        d = V(dve.reciprocal(scale, scale)); p.wait(dve, d)
        self.head_factors([d, stats[-1]], scale)
        self.head_spread(0, 7)
        for h in range(H):
            if h + 1 < H:
                self.head_spread(h + 1, 3 if h % 2 == 0 else 7)
            self.head_apply(h, 7 if h % 2 == 0 else 3, out, "mlstm_norm", gate, self.B(2), self.mo_done)
            if h:
                self.rest(self.B(2), H + h - 1, h - 1)
        self.rest(self.B(2), 2 * H - 1, H - 1)


    def attention_mixer(self):
        p, nc, a = self.p, self.nc, self.a
        pe, act, dve = nc.tensor, nc.scalar, nc.vector
        A, V, PE = p.ACT.mark, p.DVE.mark, p.PE.mark
        pair = (lambda k: self.tile(self.uhi, k), lambda k: self.tile(self.ulo, k))
        self.fresh = True
        self.project(a["proj_in"], 0, 2, self.big, then=self.rope_tables)
        self.latent_ready = []
        self.latent_hi = lambda k: self.tile(self.hlo, LATENT_AT + k)
        self.latent_lo = lambda k: self.tile(self.hlo, LATENT_AT + KCQ + KCKV + k)
        self.project(a["proj_in"], 8, 2, self.big[:, 8 * T:], between=self.latent_norm("q_latent", 0, KCQ, 5))
        for j in range(2):
            d = self.one_chunk(a["proj_in"][16 + j], j, pair, KD)
            p.wait(dve, d)
            self.bank[j] = V(dve.tensor_tensor(self.tile(self.big, 16 + j), self.ps[j], self.rb, ALU.mult))
        self.project(a["proj_in"], 18, 4, self.big[:, GATE_AT * T:], ACT.Sigmoid,
                     between=self.latent_norm("kv_latent", KCQ, KCKV, 7))
        self.settle(pe, act, dve)
        self.make_heads()
        self.attend()
        self.merge()

    def rope_tables(self):
        p, nc = self.p, self.nc
        act, dve = nc.scalar, nc.vector
        A, V = p.ACT.mark, p.DVE.mark
        rows = slice(NOPE, QK)
        pos, ang, n, t = (self.sc[i][rows, :] for i in (4, 1, 2, 3))
        cos, sin = self.cos, self.sin = self.sc[5][rows, :], self.sc[6][rows, :]
        self.settle(act, dve)
        landed = nc.alloc_semaphore("positions_loaded")
        act.dma_start(pos.bitcast(I32), self.a["positions"].broadcast_to([ROPE, T])).then_inc(landed, 16)
        dve.wait_ge(landed, 16)
        d = V(dve.tensor_copy(ang, pos.bitcast(I32))); p.wait(dve, d)
        d = V(dve.tensor_scalar(ang, ang, self.const[rows, C_FREQ:C_FREQ + 1], None, ALU.mult)); p.wait(dve, d)
        magic = 1.5 * 2.0 ** 23
        d = V(dve.tensor_scalar(n, ang, 1.0 / (2 * np.pi), magic, ALU.mult, ALU.add)); p.wait(dve, d)
        d = V(dve.tensor_scalar(n, n, -magic, None, ALU.add)); p.wait(dve, d)
        c1 = 6.28125
        c2 = float(np.floor((2 * np.pi - c1) * 2 ** 22) / 2 ** 22)
        c3 = 2 * np.pi - c1 - c2
        for c in (c1, c2, c3):
            d = V(dve.scalar_tensor_tensor(out=ang, in0=n, scalar=-c, in1=ang, op0=ALU.mult, op1=ALU.add)); p.wait(dve, d)
        edge = 3.1415925
        d = V(dve.tensor_scalar(t, ang, float(np.pi / 2), None, ALU.add)); p.wait(dve, d)
        d = V(dve.tensor_scalar(n, t, float(np.pi), -2 * float(np.pi), ALU.is_gt, ALU.mult)); p.wait(dve, d)
        d = V(dve.tensor_tensor(t, t, n, ALU.add)); p.wait(dve, d)
        V(dve.tensor_scalar(t, t, edge, -edge, ALU.min, ALU.max))
        d = V(dve.tensor_scalar(ang, ang, edge, -edge, ALU.min, ALU.max)); p.wait(act, d)
        A(act.activation(cos, t, ACT.Sin))
        self.tables_done = A(act.activation(sin, ang, ACT.Sin))

    def latent_norm(self, name, first, count, bank):
        p, nc = self.p, self.nc
        pe, act, dve = nc.tensor, nc.scalar, nc.vector
        r = self.sc[3]
        used = [None, None]
        latents = Done(p.DVE, p.DVE.count, False)
        for k in range(count):
            sq = self.sc[1 + k % 2]
            p.wait(act, latents, used[k % 2])
            squared = p.ACT.mark(act.activation(sq[:, :], self.tile(self.big, first + k), ACT.Square))
            p.wait(pe, squared, self.bank[bank])
            done = used[k % 2] = p.PE.mark(pe.matmul(self.ps[bank], self.cst(C_ONE), sq[:, :], start=k == 0, stop=k == count - 1))
        yield
        p.wait(act, latents)
        self.bank[bank] = ready = self.rsqrt(self.ps[bank], r[:, :], done, count * P)
        for k in range(first, first + count):
            if k == first + 1:
                yield
            t = self.tile(self.big, k)
            p.wait(dve, ready)
            d = p.DVE.mark(dve.scalar_tensor_tensor(out=t, in0=t, scalar=self.par(name, k - first), in1=r[:, :], op0=ALU.mult, op1=ALU.mult))
            self.latent_ready += self.split_pair(t, self.latent_hi(k), self.latent_lo(k), d)

    def rotate(self, x, ready, bank, tmp):
        p, nc = self.p, self.nc
        rows = slice(NOPE, QK)
        p.wait(nc.tensor, ready, self.bank[bank])
        rot = self.ps[bank][rows, :]
        turned = p.PE.mark(nc.tensor.matmul(rot, self.const[rows, C_ROT:C_ROT + ROPE], x, start=True, stop=True))
        p.wait(nc.vector, turned, self.tables_done)
        p.DVE.mark(nc.vector.tensor_tensor(x, x, self.cos, ALU.mult))
        d = p.DVE.mark(nc.vector.tensor_tensor(tmp[rows, :], rot, self.sin, ALU.mult))
        self.bank[bank] = d
        p.wait(nc.vector, d)
        return p.DVE.mark(nc.vector.tensor_tensor(x, x, tmp[rows, :], ALU.add))

    def make_heads(self):
        p, nc, a = self.p, self.nc, self.a
        pe, act, dve = nc.tensor, nc.scalar, nc.vector
        A, V, PE = p.ACT.mark, p.DVE.mark, p.PE.mark
        q_gain, k_gain = self.misc[0:QK, 128:129], self.misc[0:QK, 129:130]
        landed = nc.alloc_semaphore("head_gains_loaded")
        act.dma_start(self.misc[0:QK, 128:130], a["head_gains"]).then_inc(landed, 16)
        dve.wait_ge(landed, 16)
        self.Q = Q = [self.tile(self.uf, h) for h in range(AH)]
        self.K = K = [self.tile(self.uf, KD + h) for h in range(AH)]
        v = self.B(0)
        rope_rows = slice(NOPE, QK)
        self.settle(pe, act, dve)
        kr = self.tile(self.big, KCQ + KCKV)[rope_rows, :]
        krot = self.sc[4]
        sq = self.sc[0:2]
        for n in range(2):
            kr_sq = A(act.activation(self.sc[2 + n][rope_rows, :], kr, ACT.Square))
        krot_scaled = V(dve.tensor_scalar(krot[rope_rows, :], kr, k_gain[rope_rows, :], None, ALU.mult))
        at = lambda first: (lambda k: self.latent_hi(first + k), lambda k: self.latent_lo(first + k))

        def products(name, heads_cols, tiles, first):
            xhi, xlo = at(first)
            chunk = None
            for h in range(AH):
                if h % 4 == 0:
                    hi, lo, ready = self.w.chunk(a[name][h // 4])
                    p.wait(pe, ready, self.latent_ready)
                b = h % 2
                p.wait(pe, self.bank[b])
                for k in range(tiles):
                    c = (h % 4 * tiles + k) * heads_cols
                    m = self.mm3(self.ps[b][0:heads_cols, :], hi, lo, slice(c, c + heads_cols), xhi(k), xlo(k), k == 0, k == tiles - 1)
                yield h, b, (self.w.used.mark(m) if h % 4 == 3 else PE(m))

        sums, q_done = [None, None], []

        def after_q(h, b, d):
            p.wait(act, d, sums[h % 2], krot_done)
            s = A(act.activation(sq[h % 2][0:QK, :], self.ps[b][0:QK, :], ACT.Square))
            p.wait(dve, s)
            g_done = self.bank[b] = V(dve.tensor_scalar(Q[h][0:QK, :], self.ps[b][0:QK, :], q_gain, None, ALU.mult))
            return h, s, g_done

        def finish_q(h, s, g_done):
            sums[h % 2] = self.token_sums(sq[h % 2], s, lambda i: self.ps[6][:, h * NT + i:h * NT + i + 1], rows=QK,
                                          first_wait=self.bank[6])
            p.wait(dve, q_done[-2] if h > 1 else krot_done)
            q_done.append(self.rotate(Q[h][rope_rows, :], g_done, 2 + h % 2, self.vt[h % 2]))

        before = krot_done = None
        for x in products("q_up", QK, KCQ, 0):
            if krot_done is None:
                krot_done = self.rotate(krot[rope_rows, :], krot_scaled, 3, self.sc[0])
            x = after_q(*x)
            if before:
                finish_q(*before)
            before = x
        finish_q(*before)
        self.settle(act, dve)
        sv = self.big[:, 14 * T:18 * T]
        self.turn_tiles(sv, 4 * NT, 0, sv, None)
        V(dve.tensor_scalar(self.big[:, 6 * T:10 * T], self.big[:, 6 * T:10 * T], HV ** -0.5, None, ALU.mult))
        masks = self.sc[5][:, :].bitcast(BF16)
        self.id16, self.ngt16, self.nge16 = (masks[:, n * P:(n + 1) * P] for n in range(3))
        for to, c in ((self.id16, C_ID), (self.ngt16, C_NGT), (self.nge16, C_NGE)):
            V(dve.tensor_copy(to, self.cst(c)))
        self.nsuf, self.none = self.sums_lhs[:, 0:P], self.sums_lhs[:, P:2 * P]
        for to, c in ((self.nsuf, C_NSUF), (self.none, C_NONE)):
            V(dve.tensor_copy(to, self.cst(c)))
        ksum, vt_used, self.k_done = [None, None], [None, None], []

        def after_k(h, b, d):
            ks, vt = self.sc[2 + h % 2], self.vt[h % 2]
            p.wait(act, d, ksum[h % 2], vt_used[h % 2], kr_sq)
            A(act.activation(ks[0:NOPE, :], self.ps[b][0:NOPE, :], ACT.Square))
            s = A(act.copy(vt[NOPE:P, :], self.ps[b][NOPE:P, :]))
            p.wait(dve, s)
            self.bank[b] = V(dve.tensor_scalar(K[h][0:NOPE, :], self.ps[b][0:NOPE, :], k_gain[0:NOPE, :], None, ALU.mult))
            self.k_done.append([self.bank[b], A(act.copy(K[h][rope_rows, :], krot[rope_rows, :]))])
            return h, s

        def finish_k(h, s):
            ks, vt = self.sc[2 + h % 2], self.vt[h % 2]
            ksum[h % 2] = self.token_sums(ks, s, lambda i: self.ps[6][:, (AH + h) * NT + i:(AH + h) * NT + i + 1], rows=QK)
            b = 7 - 2 * (h % 2)
            p.wait(pe, self.bank[b])
            for i in range(NT):
                m = pe.transpose(self.ps[b][:, i * HV:(i + 1) * HV], vt[NOPE:P, i * P:(i + 1) * P], self.const[NOPE:P, C_ID + NOPE:C_ID + P])
            vt_used[h % 2] = PE(m)
            p.wait(dve, vt_used[h % 2])
            self.bank[b] = V(dve.tensor_copy(v[:, h * NT * HV:(h + 1) * NT * HV], self.ps[b][:, 0:NT * HV]))

        before = None
        for x in products("kv_up", P, KCKV, KCQ):
            x = after_k(*x)
            if before:
                finish_k(*before)
            before = x
        finish_k(*before)
        self.settle(dve)
        r = self.misc[:, 32:32 + 2 * AH * NT]
        d = self.rsqrt(self.ps[6][:, 0:2 * AH * NT], r, ksum, QK)
        self.bank[6] = d
        self.rq, self.rk = r[:, 0:AH * NT], r[:, AH * NT:2 * AH * NT]
        p.wait(dve, d)
        self.rk_done = V(dve.tensor_scalar(self.rq, self.rq, QK ** -0.5, None, ALU.mult))

    def attend(self):
        p, nc, a = self.p, self.nc, self.a
        pe, act, dve = nc.tensor, nc.scalar, nc.vector
        A, V, PE = p.ACT.mark, p.DVE.mark, p.PE.mark
        Q, K, rq, v = self.Q, self.K, self.rq, self.B(0)
        sq, sk = (lambda n, f=f: self.tile(self.big, f + n) for f in (6, 10))
        sv = self.big[:, 14 * T:18 * T]
        row = lambda t, n: t[:, n * N_CAUSAL:(n + 1) * N_CAUSAL]
        probs, turned, *z = (row(self.big[:, (KF + LATENT_AT) * T:], n) for n in range(4))
        soft = [row(self.scf, n) for n in range(2)]
        free_pair = self.w.n % PAIR
        soft_hi, soft_lo = self.w.hi[1 - free_pair][:, 0:N_CAUSAL], self.w.lo[1 - free_pair][:, 0:N_CAUSAL]
        mx, nb, rs = (self.misc[:, c:c + AH * NT] for c in (96, 130, 162))
        self.o_mla, self.o_sb = [sk(n) for n in range(AH // 2)], [sq(n) for n in range(AH // 2)]
        self.pairs = []
        scaled_keys = [None] * AH
        diag = [self.tile(self.big, KF + LATENT_AT + n) for n in (3, 4)]
        self.settle(pe, act, dve)
        A0, B0 = 0, 3 * T
        none = [None] * AH
        scaled, exps, divided, turned_done, turned_used, probs_used = (list(none) for _ in range(6))
        z_done, ln_done, soft_used, softs, weights_done, weights_used = (list(none) for _ in range(6))
        half = lambda h: slice(h % 2 * HV, (h % 2 + 1) * HV)
        prior = lambda x, h, n: x[h - n] if h >= n else None

        def logits(h):
            p.wait(pe, self.bank[0:3], scaled_keys[h])
            for i, c in ROWS:
                n = (i + 1) * P
                pe.matmul(self.psum[:, c:c + n], Q[h][0:QK, i * P:(i + 1) * P], K[h][0:QK, 0:n], start=True, stop=True)
                m = pe.matmul(self.psum[:, c + n - P:c + n], self.id16, self.ngt16, start=False, stop=True, skip_group_check=True)
            p.wait(dve, PE(m))
            for i, c in ROWS:
                d = V(dve.tensor_reduce(mx[:, h * NT + i:h * NT + i + 1], self.psum[:, c:c + (i + 1) * P], AX.X, ALU.max))
            p.wait(dve, d)
            hs = slice(h * NT, (h + 1) * NT)
            d = V(dve.scalar_tensor_tensor(out=nb[:, hs], in0=mx[:, hs], scalar=-1.0, in1=rq[:, hs], op0=ALU.mult, op1=ALU.mult))
            scaled[h] = d
            self.bank[0:3] = [d] * 3

        def exponents(h):
            p.wait(act, scaled[h], prior(probs_used, h, 1))
            for i, c in ROWS:
                x = h * NT + i
                exps[h] = A(act.activation(probs[:, c:c + (i + 1) * P], self.psum[:, c:c + (i + 1) * P], ACT.Exp,
                                           bias=nb[:, x:x + 1], scale=rq[:, x:x + 1], accum_out=rs[:, x:x + 1]))
            self.bank[0:3] = [exps[h]] * 3

        def divide(h):
            hs = slice(h * NT, (h + 1) * NT)
            p.wait(dve, exps[h])
            d = V(dve.reciprocal(rs[:, hs], rs[:, hs]))
            p.wait(dve, d)
            for i, c in ROWS:
                w = probs[:, c:c + (i + 1) * P]
                d = V(dve.tensor_scalar(w, w, rs[:, h * NT + i:h * NT + i + 1], None, ALU.mult))
            divided[h] = d

        def transpose(h):
            p.wait(pe, divided[h], self.bank[3:6])
            for i, c in ROWS:
                for j in range(i + 1):
                    to = B0 + causal_column(j, i)
                    m = pe.transpose(self.psum[:, to:to + P], probs[:, c + j * P:c + (j + 1) * P], self.cst(C_ID))
            probs_used[h] = PE(m)
            p.wait(dve, probs_used[h], prior(turned_used, h, 1))
            turned_done[h] = V(dve.tensor_copy(turned, self.psum[:, B0:B0 + N_CAUSAL]))
            self.bank[3:6] = [turned_done[h]] * 3

        def mla_values(h):
            p.wait(pe, turned_done[h], self.bank[6])
            v_at = lambda i: v[:, (h * NT + i) * HV:(h * NT + i + 1) * HV]
            turned_used[h] = PE(self.causal_values(self.ps[6][half(h), :], v_at, turned))
            p.wait(dve, turned_used[h])
            self.bank[6] = V(dve.tensor_copy(self.o_mla[h // 2][half(h), :], self.ps[6][half(h), :]))

        def stick_logits(h):
            p.wait(pe, self.bank[0:3])
            for i, t0, n, c in CAUSAL:
                m = pe.matmul(self.psum[:, A0 + c:A0 + c + n], sk(h // 2)[half(h), i * P:(i + 1) * P], sq(h // 2)[half(h), t0:t0 + n],
                              start=True, stop=True)
            s, zh = soft[h % 2], z[h % 2]
            p.wait(act, PE(m), prior(weights_used, h, 2))
            z_done[h] = A(act.copy(zh, self.psum[:, A0:A0 + N_CAUSAL]))
            self.bank[0:3] = [z_done[h]] * 3
            p.wait(act, z_done[h], prior(softs, h, 2))
            d = A(act.activation(s, zh, ACT.Abs)); p.wait(act, d)
            ln_done[h] = A(act.activation(s, s, ACT.Exp, scale=-1.0))

        def logarithm(h):
            s = soft[h % 2]
            p.wait(act, ln_done[h])
            ln_done[h] = A(act.activation(s, s, ACT.Ln, bias=1.0))

        def softplus(h):
            s, zh = soft[h % 2], z[h % 2]
            p.wait(dve, ln_done[h], z_done[h])
            d = V(dve.scalar_tensor_tensor(out=s, in0=zh, scalar=0.0, in1=s, op0=ALU.max, op1=ALU.add))
            p.wait(dve, d)
            softs[h] = self.mask_diagonals(s, C_LT)

        def split(h):
            s, d = soft[h % 2], softs[h]
            p.wait(act, d, prior(soft_used, h, 1))
            d = A(act.copy(soft_hi, s))
            p.wait(dve, d, prior(soft_used, h, 1))
            softs[h] = [d, V(dve.tensor_tensor(soft_lo, s, soft_hi.bitcast(F32), ALU.subtract))]

        def stick_sums(h):
            p.wait(pe, self.bank[3:6])
            first = {}

            def add(c, n, lhs, rhs):
                b = c // T
                m = pe.matmul(self.psum[:, B0 + c:B0 + c + n], lhs, rhs, start=b not in first, stop=True, skip_group_check=b in first)
                first[b] = True
                return m
            for part, ready in zip((soft_hi, soft_lo), softs[h]):
                p.wait(pe, ready)
                for c in range(0, N_CAUSAL, T):
                    n = min(T, N_CAUSAL - c)
                    add(c, n, self.nsuf, part[:, c:c + n])
                for c, first_from, step, blocks in SUMMED:
                    if step == 0:
                        rhs = part[:, first_from:first_from + P].unsqueeze(1).broadcast_to([P, blocks, P])
                    elif step == P:
                        rhs = part[:, first_from:first_from + blocks * P]
                    else:
                        rhs = part.rearrange("p (b t) -> p b t", t=step)[:, :, first_from:first_from + P]
                    add(c, blocks * P, self.none, rhs)
            m = add(0, T, self.id16, self.nge16.unsqueeze(1).broadcast_to([P, NT, P]))
            soft_used[h] = PE(m)
            zh = z[h % 2]
            p.wait(dve, soft_used[h])
            d = V(dve.tensor_tensor(zh, zh, self.psum[:, B0:B0 + N_CAUSAL], ALU.add))
            self.bank[3:6] = [d] * 3
            p.wait(act, d)
            weights_done[h] = A(act.activation(zh, zh, ACT.Exp))

        def stick_values(h):
            p.wait(pe, weights_done[h], self.bank[7])
            v_at = lambda i: sv[:, ((h // 2) * NT + i) * P + h % 2 * HV:((h // 2) * NT + i) * P + (h % 2 + 1) * HV]
            weights_used[h] = PE(self.causal_values(self.ps[7][half(h), :], v_at, z[h % 2]))
            p.wait(dve, weights_used[h])
            self.bank[7] = V(dve.tensor_copy(self.o_sb[h // 2][half(h), :], self.ps[7][half(h), :]))

        def pair(n):
            src = (self.o_mla + self.o_sb)[n]
            self.pairs += self.split_pair(src, self.tile(self.uhi, n), self.tile(self.ulo, n), [self.bank[6:8], exps[n]])

        def spread_key(h):
            self.spread_used[h % 2] = self.spread(self.rk[:, h * NT:(h + 1) * NT], self.rk_done, diag[h % 2],
                                                  self.spread_used[h % 2], 4 + h % 2)

        def scale_keys(first, last):
            for h in range(first, last):
                if h + 1 < AH:
                    spread_key(h + 1)
                b = 4 + h % 2
                p.wait(dve, self.bank[b], self.k_done[h])
                self.bank[b] = scaled_keys[h] = V(dve.tensor_tensor(K[h][0:QK, :], K[h][0:QK, :], self.ps[b][0:QK, :], ALU.mult))

        complete = {1: [0], 3: [1], 4: [4], 5: [2, 5], 6: [6], 7: [3, 7]}

        def following(h):
            stick_logits(h)
            if h:
                stick_sums(h - 1)
            else:
                spread_key(0)
                scale_keys(0, 1)
            logits(h)
            logarithm(h)
            if h:
                transpose(h - 1)
                stick_values(h - 1)
            softplus(h)
            if h:
                mla_values(h - 1)
            else:
                scale_keys(1, AH)
            exponents(h)
            split(h)
            divide(h)
            for n in complete.get(h - 1, ()):
                pair(n)

        for h in range(AH):
            following(h)
        stick_sums(AH - 1)
        transpose(AH - 1)
        stick_values(AH - 1)
        mla_values(AH - 1)
        for n in complete[AH - 1]:
            pair(n)
        p.wait(nc.gpsimd, soft_used[AH - 1], softs[AH - 1])

    def merge(self):
        p, nc, a = self.p, self.nc, self.a
        pe, act, dve = nc.tensor, nc.scalar, nc.vector
        A, V, PE = p.ACT.mark, p.DVE.mark, p.PE.mark
        W, ps = self.w, self.ps
        self.settle(pe, act, dve)
        t1, t2 = self.sc[0:2], self.sc[2:4]
        W.begin()
        with p.loop(2, act=4, dve=16, split=8, used=4) as i:
            for j in range(4):
                lo_done = p.DVE.ahead(4 * j + 4)
                before = lambda eng: (p.wait(eng, p.DVE.ahead(4 * j + 4 - 8)) if j > 1 else p.wait(eng, p.DVE.ahead(4 * j + 4 + 8), back=1))
                hi, lo, split = W.chunk(a["branch"][i * 4 + j])
                p.wait(pe, split)
                before(pe)
                b = 2 * (j % 2)
                for half in range(2):
                    for k in range(4):
                        m = self.mm3(ps[b + half], hi, lo, slice((4 * half + k) * P, (4 * half + k + 1) * P),
                                     self.tile(self.uhi, 4 * half + k), self.tile(self.ulo, 4 * half + k), k == 0, k == 3)
                product = W.used.mark(m)
                p.wait(dve, product)
                before(dve)
                x, y = t1[j % 2][:, :], t2[j % 2][:, :]
                g = lambda n: self.big[:, ds((i * 4 + (GATE_AT + n * KD + j)) * T, T)]
                V(dve.tensor_tensor(x, ps[b], g(0), ALU.mult))
                d = V(dve.tensor_tensor(y, ps[b + 1], g(1), ALU.mult))
                p.wait(dve, d)
                d = V(dve.tensor_tensor(x, x, y, ALU.add))
                mhi, mlo = self.hhi[:, ds((i * 4 + j) * T, T)], self.hlo[:, ds((i * 4 + (LO_AT + j)) * T, T)]
                p.wait(act, d)
                d = A(act.copy(mhi, x))
                p.wait(dve, d)
                V(dve.tensor_tensor(mlo, x, mhi.bitcast(F32), ALU.subtract))
        W.finish(2)
        self.bank[0:4] = [[Done(p.ACT, p.ACT.count, False), Done(p.DVE, p.DVE.count, False)]] * 4
        merged = [Done(p.ACT, p.ACT.count, False), Done(p.DVE, p.DVE.count, False)]
        inputs = ([Done(p.DVE, p.DVE.count - 4, False), self.bank[4:]], merged, KD - 1)
        self.into_stream(a["proj_out"], 2, 4, 1, KD, self.hhi, self.hlo[:, LO_AT * T:], 1.0, None, ("ffn2_norm", 0), inputs)

    def load_p(self):
        self.settle(self.nc.scalar)
        self.p_landed = self.nc.alloc_semaphore("p_loaded")
        self.nc.scalar.dma_start(self.scf[:, 3 * T:5 * T], self.a["p"]).then_inc(self.p_landed, 16)

    def embed(self):
        p, nc, a = self.p, self.nc, self.a
        pe, act, dve = nc.tensor, nc.scalar, nc.vector
        A, V = p.ACT.mark, p.DVE.mark
        W, ps = self.w, self.ps
        self.settle(act)
        self.stored = nc.alloc_semaphore("stored")
        at = self.scf[:, 3 * T:5 * T]
        act.wait_ge(self.p_landed, 16)
        dve.wait_ge(self.p_landed, 16)
        pairs = []
        for k in range(2):
            pairs += self.split_pair(at[:, k * T:(k + 1) * T], self.tile(self.hhi, k), self.tile(self.hlo, k), None)
        g, t = self.sc[1:3], self.sc[3:5]
        p.wait(pe, self.bank[0:4])

        def turn(i):
            for j in range(4):
                before = (p.DVE.ahead(3 * (j - 1)), 0) if j > 1 else (p.DVE.ahead(3 * (j + 3)), 1)
                hi, lo, split = W.chunk(a["embed"][i * 4 + j])
                p.wait(pe, split)
                b = 2 * (j % 2)
                if p.once and j == 0:
                    product = self.first_chunk(ps[b], hi, lo, last=False)
                    self.factor()
                    for line in (p.ACT, p.DVE):
                        line.start = line.count
                else:
                    p.wait(pe, before[0], back=before[1])
                    for k in range(KD):
                        self.mm3(ps[b], hi, lo, slice(k * P, (k + 1) * P), self.tile(self.uhi, k), self.tile(self.ulo, k), k == 0, k == KD - 1)
                if p.once and j == 0:
                    p.wait(pe, pairs)
                for k in range(2):
                    m = self.mm3(ps[b + 1], hi, lo, slice((KD + k) * P, (KD + k + 1) * P), self.tile(self.hhi, k), self.tile(self.hlo, k),
                                 k == 0, k == 1)
                product = W.used.mark(m)
                gt, tt = g[j % 2][:, :], t[j % 2][:, :]
                p.wait(dve, product)
                p.wait(dve, before[0], back=before[1])
                d = V(dve.tensor_tensor(gt, ps[b], self.rb, ALU.mult))
                p.wait(act, d)
                d = A(act.activation(gt, gt, ACT.Sigmoid))
                p.wait(dve, d)
                d = V(dve.tensor_tensor(tt, gt, ps[b + 1], ALU.mult))
                p.wait(dve, d)
                at = ds((i * 4 + j) * T, T)
                x = self.x[:, at]
                d = V(dve.tensor_tensor(x, x, tt, ALU.add))
                p.wait(act, d)
                act.dma_start(self.out[:, at], x).then_inc(self.stored, 16)

        p.turns(2, turn, act=4, dve=12, split=8, used=4)


    def causal_product(self, b0, lhs, rhs, ready):
        p, pe = self.p, self.nc.tensor
        p.wait(pe, ready, self.bank[b0:b0 + 3])
        for (i, t0, n, c) in CAUSAL:
            m = pe.matmul(self.psum[:, b0 * T + c:b0 * T + c + n], lhs(i), rhs(t0, n), start=True, stop=True)
        d = p.PE.mark(m)
        self.bank[b0:b0 + 3] = [d] * 3
        return d

    def mask_diagonals(self, x, mask):
        x3 = x[:, 0:T].rearrange("p (i t) -> p i t", t=P)
        m3 = self.cst(mask).unsqueeze(1).broadcast_to([P, NT, P])
        return self.p.DVE.mark(self.nc.vector.tensor_tensor(x3, x3, m3, ALU.mult))

    def causal_values(self, out, v, w):
        blocks = sorted(CAUSAL, key=lambda x: (x[0], x[1]))
        for n, (i, t0, width, c) in enumerate(blocks):
            m = self.nc.tensor.matmul(out[:, t0:t0 + width], v(i), w[:, c:c + width], start=n == 0, stop=n == len(blocks) - 1,
                                      skip_group_check=True)
        return m

    def col(self, i):
        return self.ps[4][:, i:i + 1]


def block_program(nc, a, out):
    b = Build(nc, a, out)
    b.load()
    par = lambda name, first=0: (lambda k: b.par(name, first + k))
    b.from_stream(par("norm_pre"))
    b.ffn(a["ffn1_in"], a["ffn1_out"], par("norm_post", 0), ("norm_pre", KD))
    b.gated_mixer()
    b.y_tiles = b.y
    b.ffn(a["ffn2_in"], a["ffn2_out"], par("norm_post", 2 * KD), ("ffn1_norm", 0))
    b.ffn(a["ffn3_in"], a["ffn3_out"], None, ("mix_norm", 0))
    b.attention_mixer()
    b.ffn(a["ffn4_in"], a["ffn4_out"], None, ("ple_norm", 0), b.load_p)
    b.embed()
    b.store()


def lhs_tiles(w, cols=None):
    k, n = w.shape
    cols = cols or P
    return np.ascontiguousarray(w.reshape(k // P, P, n // cols, cols).transpose(2, 1, 0, 3)).reshape(n // cols, P, -1)


def columns(v):
    return np.ascontiguousarray(v.reshape(-1, P).T)


def ffn_in(w):
    t = lhs_tiles(w)
    return np.ascontiguousarray(t.reshape(2, KF, P, -1).transpose(1, 0, 2, 3)).reshape(2 * KF, P, -1)


def ffn_out(w):
    t = lhs_tiles(w)
    return np.ascontiguousarray(t.reshape(KD, P, 2, SLOT).transpose(0, 2, 1, 3)).reshape(2 * KD, P, SLOT)


def mix_in(w):
    n = w.shape[1] - 2 * HEADS
    gates = np.concatenate([w[:, n:n + HEADS], w[:, 0:32 - HEADS], w[:, n + HEADS:], w[:, 0:P - 32 - HEADS]], axis=1)
    return lhs_tiles(np.concatenate([w[:, :n], gates], axis=1))


def proj_in(w):
    n = KCQ * P + KCKV * P
    rope = np.concatenate([w[:, 0:NOPE], w[:, n:n + ROPE], w[:, 0:P - QK]], axis=1)
    return lhs_tiles(np.concatenate([w[:, :n], rope, w[:, n + ROPE:]], axis=1))


def head_tiles(w, cols):
    t = lhs_tiles(w, cols)
    return np.ascontiguousarray(t.reshape(2, 4, P, -1).transpose(0, 2, 1, 3)).reshape(2, P, -1)


def constants():
    c = np.zeros((P, N_CONST), np.float32)
    s, t = np.arange(P)[:, None], np.arange(P)[None, :]
    c[:, C_ID:C_ID + P] = s == t
    c[:, C_ONE:C_ONE + P] = 1
    c[:, C_LE:C_LE + P] = s <= t
    c[:, C_LT:C_LT + P] = s < t
    c[:, C_NSUF:C_NSUF + P] = -1.0 * (s >= t)
    c[:, C_NONE:C_NONE + P] = -1
    c[:, C_NGT:C_NGT + P] = NEVER * (t > s)
    c[:, C_NGE:C_NGE + P] = NEVER * (s >= t)
    for n, h in enumerate(LEVELS):
        c[:, C_LEVEL + n * P:C_LEVEL + (n + 1) * P] = (s // (2 * h) == t // (2 * h)) & (s % (2 * h) < h) & (t % (2 * h) >= h)
    c[:, C_RESET:C_RESET + T] = np.arange(T) % CH != 0
    for h in range(HEADS):
        c[h, C_SEL + h * P:C_SEL + (h + 1) * P] = 1
    r = np.arange(ROPE // 2)
    c[NOPE + ROPE // 2 + r, C_ROT + r] = -1
    c[NOPE + r, C_ROT + ROPE // 2 + r] = 1
    freq = (10000.0 ** (-(2.0 * r) / ROPE)).astype(np.float32)
    c[NOPE:QK, C_FREQ] = np.concatenate([freq, freq])
    return c


def layout(i):
    f = {k: np.asarray(v) for k, v in i.items()}
    pieces = {
        "norm_pre": columns(f["norm_pre"]), "norm_post": columns(f["norm_post"]),
        "conv_w": columns(f["conv_w"]), "conv_b": columns(f["conv_b"]), "lb": columns(f["hgrn_lb_logits"]),
        "hgrn_norm": columns(f["hgrn_norm"]), "mlstm_norm": columns(f["mlstm_norm"]),
        "ffn1_norm": columns(f["ffn1_norm_2"]), "mix_norm": columns(f["mix_norm_2"]),
        "q_latent": columns(f["q_latent_norm_2"]), "kv_latent": columns(f["kv_latent_norm_2"]),
        "ffn2_norm": columns(f["ffn2_norm_2"]), "ple_norm": columns(f["ple_norm_2"]),
    }
    return {
        "const": constants(),
        "param": np.concatenate([pieces[n] for n in PARAMS], axis=1),
        "x": np.ascontiguousarray(f["x"][0].T.reshape(KD, P, T).transpose(1, 0, 2)).reshape(P, KD * T),
        "ffn1_in": ffn_in(f["ffn1_w_in"][0]), "ffn1_out": ffn_out(f["ffn1_w_out"][0]),
        "mix_in": mix_in(f["w_mix_in"][0]), "mix_out": lhs_tiles(f["w_mix_out"][0]),
        "gate_bias": np.ascontiguousarray(f["mlstm_gate_bias"].reshape(2, HEADS).T),
        "ffn2_in": ffn_in(f["ffn2_w_in"][0]), "ffn2_out": ffn_out(f["ffn2_w_out"][0]),
        "ffn3_in": ffn_in(f["ffn1_w_in_2"][0]), "ffn3_out": ffn_out(f["ffn1_w_out_2"][0]),
        "proj_in": proj_in(f["w_in_2"][0]),
        "q_up": head_tiles(f["w_q_up_2"][0], QK), "kv_up": head_tiles(f["w_kv_up_2"][0], NOPE + HV),
        "head_gains": np.concatenate([f["q_head_norm_2"], f["k_head_norm_2"]]).T.copy(),
        "positions": f["positions_2"],
        "branch": np.concatenate([lhs_tiles(f["w_branch_mla_2"][0]), lhs_tiles(f["w_branch_sb_2"][0])], axis=2),
        "proj_out": lhs_tiles(f["w_out_2"][0]),
        "ffn4_in": ffn_in(f["ffn2_w_in_2"][0]), "ffn4_out": ffn_out(f["ffn2_w_out_2"][0]),
        "embed": np.concatenate([lhs_tiles(f["w_ple_gate_2"][0]), lhs_tiles(f["w_ple_proj_2"][0])], axis=2),
        "p": np.ascontiguousarray(f["p_2"][0, 0].T.reshape(2, P, T).transpose(1, 0, 2)).reshape(P, 2 * T),
    }


def kernel(**inputs):
    import concourse.bacc as bacc
    from concourse.bass_utils import run_bass_kernel_spmd

    nc = bacc.Bacc("TRN2", target_bir_lowering=False, num_devices=1)
    arrays = layout(inputs)
    aps = {n: nc.dram_tensor(f"in_{n}", v.shape, mybir.dt.from_np(v.dtype), kind="ExternalInput").ap() for n, v in arrays.items()}
    out = nc.dram_tensor("out", (P, KD * T), F32, kind="ExternalOutput").ap()
    block_program(nc, aps, out)
    r = run_bass_kernel_spmd(nc, [{f"in_{n}": v for n, v in arrays.items()}], core_ids=[0])
    y = r.results[0]["out"]
    return np.ascontiguousarray(y.reshape(P, KD, T).transpose(2, 1, 0)).reshape(1, T, D)
```
